# Optimizing a Trainium2 kernel written in Bass

```python
import math
import jax, jax.numpy as jnp
from jax import lax
import numpy as np

D_MODEL = 1024
BATCH = 1
SEQ = 512
DEPTH = 1

HEAD_DIM = 64
SB_HEADS = 8
SB_WIDTH = SB_HEADS * HEAD_DIM
RW_HEADS = 8
RW_WIDTH = RW_HEADS * HEAD_DIM
DECAY_LORA = 64
ICLR_LORA = 64
GATE_LORA = 160
N_BRANCHES = 2
SHIFT_WIDTH = 3 * RW_WIDTH + DECAY_LORA + ICLR_LORA + GATE_LORA
IN_COLS = 3 * SB_WIDTH + SHIFT_WIDTH + N_BRANCHES * D_MODEL
N_GROUPS = 4
EXPERTS_PER_GROUP = 8
N_EXPERTS = N_GROUPS * EXPERTS_PER_GROUP
TOP_K_IN_GROUP = 2
D_EXPERT = 512
Q_BLOCK = 128
NORM_EPS = 1e-6
GN_EPS = 64e-5
L2_EPS = 1e-12

kernel_name = 'hybrid_stickbreak_rwkv7_hmoe_block'

def rmsnorm(x, g):
    xf = x.astype(jnp.float32)
    inv = lax.rsqrt(jnp.mean(xf * xf, axis=-1, keepdims=True) + NORM_EPS)
    return (xf * inv).astype(x.dtype) * g

def stick_breaking_attention(q, k, v):
    seq_len = q.shape[2]
    scale = 1.0 / math.sqrt(q.shape[-1])
    outs = []
    for i in range(seq_len // Q_BLOCK):
        q0 = i * Q_BLOCK
        n_keys = q0 + Q_BLOCK
        qb = q[:, :, q0:n_keys].astype(jnp.float32)
        kb = k[:, :, :n_keys].astype(jnp.float32)
        vb = v[:, :, :n_keys].astype(jnp.float32)
        z = jnp.einsum('bhqd,bhkd->bhqk', qb, kb) * scale
        t_idx = q0 + jnp.arange(Q_BLOCK)[:, None]
        s_idx = jnp.arange(n_keys)[None, :]
        strict = s_idx < t_idx
        log_keep = jnp.where(strict, jax.nn.log_sigmoid(-z), 0.0)
        later = lax.cumsum(log_keep, axis=3, reverse=True) - log_keep
        att = jnp.where(strict, jnp.exp(jax.nn.log_sigmoid(z) + later), 0.0)
        outs.append(jnp.einsum('bhqk,bhkd->bhqd', att, vb).astype(v.dtype))
    return jnp.concatenate(outs, axis=2)

def token_shift(p, mu):
    prev = jnp.pad(p[:, :-1], ((0, 0), (1, 0), (0, 0)))
    return p + mu * (prev - p)

def rwkv7_time_mix(cols, shift_mu, w0, w_decay_up, a0, w_iclr_up, w_gate_up, k_k, k_a, r_k, lnx_w, lnx_b):
    b, s, _ = cols.shape
    xs = token_shift(cols, shift_mu)
    r, k, v, wd, ad, gd = jnp.split(
        xs, [RW_WIDTH, 2 * RW_WIDTH, 3 * RW_WIDTH, 3 * RW_WIDTH + DECAY_LORA,
             3 * RW_WIDTH + DECAY_LORA + ICLR_LORA], axis=-1)
    w = -jax.nn.softplus(-(w0 + jnp.tanh(wd) @ w_decay_up)) - 0.5
    decay = jnp.exp(-jnp.exp(w.astype(jnp.float32)))
    a = jax.nn.sigmoid(a0 + ad @ w_iclr_up)
    g = jax.nn.sigmoid(gd) @ w_gate_up
    kk = k * k_k
    k = k * (1.0 + (a - 1.0) * k_a)

    def heads(t):
        return t.astype(jnp.float32).reshape(b, s, RW_HEADS, HEAD_DIM)

    r_h, k_h, v_h, a_h, kk_h, dec_h = heads(r), heads(k), heads(v), heads(a), heads(kk), heads(decay)
    kk_h = kk_h / jnp.maximum(jnp.sqrt(jnp.sum(kk_h * kk_h, axis=-1, keepdims=True)), L2_EPS)
    vec_a = -kk_h
    vec_b = kk_h * a_h

    def step(state, inp):
        r_t, dec_t, k_t, v_t, a_t, b_t = inp
        sa = jnp.einsum('bhvk,bhk->bhv', state, a_t)
        state = (state * dec_t[:, :, None, :] + sa[..., None] * b_t[:, :, None, :]
                 + v_t[..., None] * k_t[:, :, None, :])
        return state, jnp.einsum('bhvk,bhk->bhv', state, r_t)

    tm = lambda t: jnp.moveaxis(t, 1, 0)
    state0 = jnp.zeros((b, RW_HEADS, HEAD_DIM, HEAD_DIM), jnp.float32)
    _, y = lax.scan(step, state0, (tm(r_h), tm(dec_h), tm(k_h), tm(v_h), tm(vec_a), tm(vec_b)))
    y = jnp.moveaxis(y, 0, 1)
    mean = jnp.mean(y, axis=-1, keepdims=True)
    var = jnp.mean(jnp.square(y - mean), axis=-1, keepdims=True)
    yn = ((y - mean) * lax.rsqrt(var + GN_EPS)).reshape(b, s, RW_WIDTH)
    yn = yn * lnx_w.astype(jnp.float32) + lnx_b.astype(jnp.float32)
    bonus = jnp.sum(r_h * k_h * r_k.astype(jnp.float32), axis=-1, keepdims=True) * v_h
    out = (yn + bonus.reshape(b, s, RW_WIDTH)) * g.astype(jnp.float32)
    return out.astype(cols.dtype)

def hybrid_mixer(h, w_in, gate_bias, shift_mu, w0, w_decay_up, a0, w_iclr_up, w_gate_up,
                 k_k, k_a, r_k, lnx_w, lnx_b, w_o_sb, w_o_rw, w_out):
    b, s, _ = h.shape
    p = h @ w_in
    q, k, v, rw_cols, gate_logits = jnp.split(
        p, [SB_WIDTH, 2 * SB_WIDTH, 3 * SB_WIDTH, 3 * SB_WIDTH + SHIFT_WIDTH], axis=-1)
    to_bhsd = lambda t: t.reshape(b, s, SB_HEADS, HEAD_DIM).transpose(0, 2, 1, 3)
    y_sb = stick_breaking_attention(to_bhsd(q), to_bhsd(k), to_bhsd(v))
    y_sb = y_sb.transpose(0, 2, 1, 3).reshape(b, s, SB_WIDTH)
    y_rw = rwkv7_time_mix(rw_cols, shift_mu, w0, w_decay_up, a0, w_iclr_up, w_gate_up,
                          k_k, k_a, r_k, lnx_w, lnx_b)
    gates = jax.nn.sigmoid(gate_logits + gate_bias)
    g_sb, g_rw = jnp.split(gates, 2, axis=-1)
    merged = g_sb * (y_sb @ w_o_sb) + g_rw * (y_rw @ w_o_rw)
    return merged @ w_out

def hierarchical_moe(h, w_group, w_router, w_up1, w_up3, w_down):
    b, s, d = h.shape
    t = h.reshape(b * s, d)
    n = t.shape[0]
    group_logits = (t @ w_group).astype(jnp.float32)
    group_prob = jax.nn.softmax(group_logits, axis=-1)
    group_sel = jnp.argmax(group_logits, axis=-1)
    group_w = jnp.max(group_prob, axis=-1, keepdims=True)
    expert_logits = (t @ w_router).astype(jnp.float32).reshape(n, N_GROUPS, EXPERTS_PER_GROUP)
    in_group = jnp.einsum('nge,ng->ne', expert_logits, jax.nn.one_hot(group_sel, N_GROUPS, dtype=jnp.float32))
    top_p, top_i = lax.top_k(jax.nn.softmax(in_group, axis=-1), TOP_K_IN_GROUP)
    top_p = top_p / jnp.sum(top_p, axis=-1, keepdims=True)
    expert_ids = group_sel[:, None] * EXPERTS_PER_GROUP + top_i
    combine = jnp.sum(jax.nn.one_hot(expert_ids, N_EXPERTS, dtype=jnp.float32)
                      * (group_w * top_p)[..., None], axis=1).astype(t.dtype)
    y = jnp.zeros_like(t)
    for e in range(N_EXPERTS):
        hid = jax.nn.silu(t @ w_up1[e]) * (t @ w_up3[e])
        y = y + combine[:, e:e + 1] * (hid @ w_down[e])
    return y.reshape(b, s, d)

def setup_inputs(seed: int = 0) -> dict:
    key = jax.random.key(seed)
    ks = jax.random.split(key, 32)
    f32 = jnp.float32
    L = DEPTH

    def nrm(k, shape, scale):
        return jax.random.normal(k, shape, f32) * scale

    return {
        'x': nrm(ks[0], (BATCH, SEQ, D_MODEL), 1.0),
        'c': nrm(ks[1], (BATCH, D_MODEL), 1.0),
        'w_mod': nrm(ks[2], (L, D_MODEL, 6 * D_MODEL), 0.5 * D_MODEL ** -0.5),
        'b_mod': nrm(ks[3], (L, 6 * D_MODEL), 0.01),
        'norm_gains': 1.0 + nrm(ks[4], (L, 4, D_MODEL), 0.02),
        'w_in': nrm(ks[5], (L, D_MODEL, IN_COLS), D_MODEL ** -0.5),
        'gate_bias': nrm(ks[6], (L, N_BRANCHES * D_MODEL), 0.01),
        'shift_mu': jax.random.uniform(ks[7], (L, SHIFT_WIDTH), f32),
        'w0': nrm(ks[8], (L, RW_WIDTH), 0.5),
        'w_decay_up': nrm(ks[9], (L, DECAY_LORA, RW_WIDTH), 0.5 * DECAY_LORA ** -0.5),
        'a0': nrm(ks[10], (L, RW_WIDTH), 0.1),
        'w_iclr_up': nrm(ks[11], (L, ICLR_LORA, RW_WIDTH), ICLR_LORA ** -0.5),
        'w_gate_up': nrm(ks[12], (L, GATE_LORA, RW_WIDTH), GATE_LORA ** -0.5),
        'k_k': 0.85 + nrm(ks[13], (L, RW_WIDTH), 0.05),
        'k_a': 1.0 + nrm(ks[14], (L, RW_WIDTH), 0.05),
        'r_k': nrm(ks[15], (L, RW_HEADS, HEAD_DIM), 0.1),
        'lnx_w': 1.0 + nrm(ks[16], (L, RW_WIDTH), 0.02),
        'lnx_b': nrm(ks[17], (L, RW_WIDTH), 0.01),
        'w_o_sb': nrm(ks[18], (L, SB_WIDTH, D_MODEL), SB_WIDTH ** -0.5),
        'w_o_rw': nrm(ks[19], (L, RW_WIDTH, D_MODEL), RW_WIDTH ** -0.5),
        'w_out': nrm(ks[20], (L, D_MODEL, D_MODEL), D_MODEL ** -0.5),
        'w_group': nrm(ks[21], (L, D_MODEL, N_GROUPS), D_MODEL ** -0.5),
        'w_router': nrm(ks[22], (L, D_MODEL, N_EXPERTS), D_MODEL ** -0.5),
        'w_up1': nrm(ks[23], (L, N_EXPERTS, D_MODEL, D_EXPERT), D_MODEL ** -0.5),
        'w_up3': nrm(ks[24], (L, N_EXPERTS, D_MODEL, D_EXPERT), D_MODEL ** -0.5),
        'w_down': nrm(ks[25], (L, N_EXPERTS, D_EXPERT, D_MODEL), D_EXPERT ** -0.5),
    }

def reference(x, c, w_mod, b_mod, norm_gains, w_in, gate_bias, shift_mu, w0, w_decay_up, a0,
              w_iclr_up, w_gate_up, k_k, k_a, r_k, lnx_w, lnx_b, w_o_sb, w_o_rw, w_out,
              w_group, w_router, w_up1, w_up3, w_down):
    for l in range(DEPTH):
        mod = jax.nn.silu(c) @ w_mod[l] + b_mod[l]
        sh1, sc1, gt1, sh2, sc2, gt2 = [m[:, None, :] for m in jnp.split(mod, 6, axis=-1)]
        h = rmsnorm(x, norm_gains[l, 0]) * (1.0 + sc1) + sh1
        y = hybrid_mixer(h, w_in[l], gate_bias[l], shift_mu[l], w0[l], w_decay_up[l], a0[l],
                         w_iclr_up[l], w_gate_up[l], k_k[l], k_a[l], r_k[l], lnx_w[l], lnx_b[l],
                         w_o_sb[l], w_o_rw[l], w_out[l])
        x = x + gt1 * rmsnorm(y, norm_gains[l, 1])
        h = rmsnorm(x, norm_gains[l, 2]) * (1.0 + sc2) + sh2
        y = hierarchical_moe(h, w_group[l], w_router[l], w_up1[l], w_up3[l], w_down[l])
        x = x + gt2 * rmsnorm(y, norm_gains[l, 3])
    return x


_drawn_inputs = setup_inputs


def setup_inputs(seed=0):
    import zlib

    import numpy as np

    out = dict(_drawn_inputs(seed))
    spreads = {}
    factors = {'gate_bias': 7.372, 'k_k': 4.407, 'lnx_w': 3.122, 'lnx_b': 8.0}
    for name, (base, spread) in spreads.items():
        noise = np.random.default_rng([zlib.crc32(name.encode()), seed]).standard_normal(out[name].shape)
        drawn = base * np.exp(spread * noise) if base else spread * noise
        out[name] = __import__('jax').numpy.asarray(drawn.astype(out[name].dtype))
    for name, factor in factors.items():
        out[name] = (out[name] * factor).astype(out[name].dtype)
    return out
```

```python
from contextlib import ExitStack

import numpy as np

import concourse.bass as bass
from concourse import mybir

F32 = mybir.dt.float32
I32 = mybir.dt.int32
ALU = mybir.AluOpType
ACT = mybir.ActivationFunctionType
AX = mybir.AxisListType.X

P = 128
T = 512
D = 1024
KD = D // P
NT = T // P
W = 512
FT = W // P
HD = 64
NH = 8
C = 64
NCH = T // C
E = 32
EG = 8
NG = 4
DE = 512
CAP = 64
MAXB = 48
DECAY = float(np.exp(-0.5))
BIG = 1e30

COL_Q, COL_K, COL_V = 0, W, 2 * W
COL_RW = 3 * W
COL_LORA = COL_RW + 3 * W
N_LORA = 288
COL_GATE = COL_LORA + N_LORA

OFF = [0, 512, 1024, 896]
WID = [T - P * j for j in range(NT)]
ZW = 1280

_widths = [("ident", 128), ("ntri", 128), ("nones", 128), ("ones", 128), ("blk", 128), ("before", 128),
           ("strictU", 64), ("inclU", 64), ("eye", 64), ("lvlL", 6 * 64), ("lvlU", 6 * 64),
           ("iota64", 64), ("m64", 8), ("blk16", 16), ("tok", 4), ("eps", 4)]
CONST = {}
_at = 0
for _n, _w in _widths:
    CONST[_n] = (_at, _w)
    _at += _w
NCONST = _at

_rows = [("mu", 15), ("w0", 4), ("a0", 4), ("kk", 4), ("ka", 4), ("rk", 4), ("lnw", 4), ("lnb", 4), ("gb", 16)]
NROW = sum(w for _, w in _rows)
_pw = _rows + [("c", 8), ("bmod", 16), ("g0", 8), ("silc", 8), ("omka", 4), ("A1", 8), ("SH1", 8), ("ss", 16), ("rs", 16)]
PAR = {}
_at = 0
for _n, _w in _pw:
    PAR[_n] = (_at, _w)
    _at += _w
NPAR = _at


def constants():
    m = np.zeros((P, NCONST), np.float32)

    def put(name, v):
        a, w = CONST[name]
        m[:, a:a + w] = np.asarray(v, np.float32).reshape(P, w)

    p = np.arange(P)[:, None]
    q = np.arange(P)[None, :]
    put("ident", p == q)
    put("ntri", -(p >= q).astype(np.float32))
    put("nones", -np.ones((P, P)))
    put("ones", np.ones((P, P)))
    put("blk", (p // 64) == (q // 64))
    put("before", p < q)
    r = p % 64
    c = np.arange(64)[None, :]
    put("strictU", r < c)
    put("inclU", r <= c)
    put("eye", r == c)

    def level(k, t, s):
        return ((t >> (k + 1)) == (s >> (k + 1))) & (((t >> k) & 1) == 1) & (((s >> k) & 1) == 0)

    put("lvlL", np.concatenate([level(k, r, c) for k in range(6)], 1))
    put("lvlU", np.concatenate([level(k, c, r) for k in range(6)], 1))
    put("iota64", np.broadcast_to(c, (P, 64)))
    put("m64", np.broadcast_to(CAP * np.arange(8)[None, :], (P, 8)))
    put("blk16", np.broadcast_to(E + np.arange(16)[None, :], (P, 16)))
    put("tok", p + P * np.arange(4)[None, :])
    put("eps", np.broadcast_to(np.array([[1e-6, 64e-5, 1.0, 0.0]]), (P, 4)))
    return m


def build(nc, x, c, w_mod, b_mod, gains, w_in, gate_bias, shift_mu, w0, w_decay_up, a0, w_iclr_up, w_gate_up,
          k_k, k_a, r_k, lnx_w, lnx_b, w_o_sb, w_o_rw, w_out, w_group, w_router, w_up1, w_up3, w_down,
          consts, out):
    ctx = ExitStack()
    with ctx:
        def sb(name, shape, dt=F32):
            return ctx.enter_context(nc.sbuf_tensor(name, shape, dt))

        def sem(name):
            return ctx.enter_context(nc.semaphore(name))

        h2_dram = nc.dram_tensor("h2_rows", [T, D], F32, kind="Internal").ap()
        ye_dram = nc.dram_tensor("expert_rows", [MAXB * CAP, D], F32, kind="Internal").ap()

        cst = sb("cst", [P, NCONST])
        par = sb("par", [P, NPAR])
        wr = sb("wr", [P, KD, NG + E])
        hT = sb("hT", [P, KD, T])
        ring = sb("ring", [P, 3, 4096])
        arena = sb("arena", [P, 15, 2048])
        prow = sb("prow", [NROW, P])
        raw = sb("raw", [P, 2, T + 1])
        PC = sb("PC", [P, FT * NCH])
        ST = sb("ST", [P, 2, FT * HD])
        SD = sb("SD", [P, FT * HD])
        Zs = sb("Zs", [P, FT * HD])
        SAs = sb("SAs", [P, 2, FT * HD])
        rt = sb("rt", [P, 2048 // 4])
        routf = sb("routf", [P, 16])
        slots_i = sb("slots_i", [P, 8], I32)
        idx_i = sb("idx_i", [CAP, MAXB], I32)
        idx_now = sb("idx_now", [CAP, 2], I32)
        nblk_i = sb("nblk_i", [1, 20], I32)
        ps = ctx.enter_context(nc.psum_tensor("ps", [P, 8, 512], F32))
        psf = ps[:, :, :].rearrange("p b n -> p (b n)")

        def K(name):
            a, w = CONST[name]
            return cst[:, a:a + w]

        def V(name, i=None, n=1):
            a, w = PAR[name]
            return par[:, a:a + w] if i is None else par[:, a + i:a + i + n]

        def S(i, n=1):
            return arena[:, i:i + n, :].rearrange("p a b -> p (a b)")

        def S4(i):
            return arena[:, i, :].rearrange("p (f t) -> p f t", f=FT)

        eps_rms, eps_gn, one = K("eps")[:, 0:1], K("eps")[:, 1:2], K("eps")[:, 2:3]

        s_r, s_k, s_v = 0, 1, 10
        s_sig, s_cum, s_a, s_P, s_Pi = 3, 4, 5, 6, 7
        s_AR, s_lora, s_g = 8, 8, 13
        s_kk, s_kk2, s_Bh, s_Kh = 11, 12, 11, 12
        s_Vt, s_Bt, s_Kt = 0, 1, 4
        s_q, s_ka, s_va, s_scr = 2, 14, 6, 10
        s_B, s_Kd, s_bonus = 3, 7, 5
        s_MT, s_X, s_XT, s_Mak, s_Mrb, s_Mrk, s_W = 10, 11, 12, 14, 3, 7, 6
        s_H, s_y, s_y2 = 6, 10, 14
        s_rows, s_x1, s_merged = 0, 3, 8

        wlo = S(s_ka)[:, 0:3 * W].rearrange("p (a n) -> p a n", a=3)
        AR = S(s_AR, 2).rearrange("p (f c a t) -> p f c a t", f=FT, c=NCH, a=2)
        lora = S(s_lora, 1).rearrange("p (a t) -> p a t", a=4)
        tok = {i: arena[:, i, :].rearrange("p (c f d) -> p c f d", c=NCH, f=FT) for i in (s_Vt, s_Bt, s_Kt, s_H)}
        chk = {i: arena[:, i, :].rearrange("p (f c t) -> p f c t", f=FT, c=NCH)
               for i in (s_MT, s_X, s_XT, s_Mak, s_Mrb, s_Mrk, s_W, s_B, s_Kd)}
        eb = S(s_scr, 3)
        e_buf = [eb[:, 0:ZW], eb[:, ZW:2 * ZW]]
        sp_buf = [eb[:, 2 * ZW:3 * ZW], eb[:, 3 * ZW:4 * ZW]]
        merged = S(s_merged, 2).rearrange("p (k t) -> p k t", k=KD)
        rows = S(s_rows, 2).rearrange("p (m n) -> p m n", m=4)
        x1 = S(s_x1, 2).rearrange("p (t n) -> p t n", t=NT)
        xin, xn = x1, S(s_rows, 2).rearrange("p (t n) -> p t n", t=NT)
        mring = [S(11, 2), S(6, 2)]
        acc_e = S(5, 1).rearrange("p (b n) -> p b n", b=2)
        acc_l = S(14, 1).rearrange("p (b n) -> p b n", b=2)
        rowp = S(13, 1).rearrange("p (b n) -> p b n", b=2)
        ytok = S(2, 1).rearrange("p (b n) -> p b n", b=2)
        h2tok = S(10, 1).rearrange("p (b n) -> p b n", b=2)
        gate_t = S(5, 1).rearrange("p (b n) -> p b n", b=4)
        eset = [ring[:, :, :], S(5, 6).rearrange("p (m n) -> p m n", m=3)]
        hrow = S(11, 1).rearrange("p (b n) -> p b n", b=2)
        hgT = S(12, 1)[:, 0:1024].rearrange("p (b k s) -> p b k s", b=2, k=KD)
        yo = S(12, 1)[:, 1024:2048].rearrange("p (b n) -> p b n", b=2)
        sil = S(13, 1)[:, 0:512].rearrange("p (b n) -> p b n", b=2)
        hid = S(13, 1)[:, 512:1024].rearrange("p (b n) -> p b n", b=2)
        hidT = S(13, 1)[:, 1024:1536].rearrange("p (b n) -> p b n", b=2)
        rsc = S(12, 1)
        selb = S(13, 1)[:, 0:2 * NT * MAXB].rearrange("p (c t b) -> p c t b", c=2, t=NT)
        ovb = S(13, 1)[:, 512:1024].rearrange("p (m e) -> p m e", e=E)

        def rview(a, n, t):
            return rsc[:, a:a + n].rearrange("p (t n) -> p t n", t=t)

        fin = [S(5, 2).rearrange("p (a n) -> p a n", a=4), S(7, 2).rearrange("p (a n) -> p a n", a=4)]

        prow_zero, rows_in, rows_turned = sem("prow_zero"), sem("rows_in"), sem("rows_turned")
        consts_in, params_in, lora_in, x_in = sem("consts_in"), sem("params_in"), sem("lora_in"), sem("x_in")
        ring_in = [sem(f"ring_in{i}") for i in range(3)]
        dve_chunk = sem("dve_chunk")
        act_link, dve_link, pool_link = sem("act_link"), sem("dve_link"), sem("pool_link")
        acc_ready, modcol_done, modcol_ready = sem("acc_ready"), sem("modcol_done"), sem("modcol_ready")
        rstd0, xn_ready, xT_done, xT_evac = sem("rstd0"), sem("xn_ready"), sem("xT_done"), sem("xT_evac")
        pa_done, pa_evac, shifted = sem("pa_done"), sem("pa_evac"), sem("shifted")
        lora_act = sem("lora_act")
        cum_ready, exps_ready = sem("cum_ready"), sem("exps_ready")
        kk2_ready, pd_done, kk_max, rn_ready, bonus_in, bonus_ready = (sem(n) for n in (
            "kk2_ready", "pd_done", "kk_max", "rn_ready", "bonus_in", "bonus_ready"))
        tok_src, tr_done, tr_act, tr_dve = sem("tok_src"), sem("tr_done"), sem("tr_act"), sem("tr_dve")
        z_done, log_ready, sp_ready, sp_masked, cum_done, att_ready, att_masked, av_all, ysb_ready = (
            sem(n) for n in ("z_done", "log_ready", "sp_ready", "sp_masked", "cum_done", "att_ready",
                             "att_masked", "av_all", "ysb_ready"))
        gram_done, gram_evac, invw_done, invw_evac, invu_done, invu_evac = (sem(n) for n in (
            "gram_done", "gram_evac", "invw_done", "invw_evac", "invu_done", "invu_evac"))
        hp_done, hp_evac, zc_done, zc_evac, sa_done, sa_evac, st_done, st_evac, yc_done, yc_evac = (sem(n) for n in (
            "hp_done", "hp_evac", "zc_done", "zc_evac", "sa_done", "sa_evac", "st_done", "st_evac", "yc_done", "yc_evac"))
        gn_in, gn_sum, gn_sq, gn_sqsum, gn_rstd, yrw_ready, yrw_mean = (sem(n) for n in (
            "gn_in", "gn_sum", "gn_sq", "gn_sqsum", "gn_rstd", "yrw_ready", "yrw_mean"))
        mix_done, osb_evac, gate_evac, merged_ready = sem("mix_done"), sem("osb_evac"), sem("gate_evac"), sem("merged_ready")
        mring_in = [sem("mring_in0"), sem("mring_in1")]
        mring_free, lacc_ready, lrow_done, lrow_ready = sem("mring_free"), sem("lacc_ready"), sem("lrow_done"), sem("lrow_ready")
        pe_pass, pool_pass = sem("pe_pass"), sem("pool_pass")
        rowp_in, zero_tile, zero_stored = sem("rowp_in"), sem("zero_tile"), sem("zero_stored")
        x_again = sem("x_again")
        y_done, y_evac, rstd1, x1_ready, rstd2, h2_ready, h2T_done, h2T_evac = (sem(n) for n in (
            "y_done", "y_evac", "rstd1", "x1_ready", "rstd2", "h2_ready", "h2T_done", "h2T_evac"))
        h2_stored = [sem("h2_stored0"), sem("h2_stored1")]
        logit_done, gsum_in, gsum_ready, oh_ready, rank_done, sel_ready, idx_done, route_ready = (sem(n) for n in (
            "logit_done", "gsum_in", "gsum_ready", "oh_ready", "rank_done", "sel_ready", "idx_done", "route_ready"))
        w_in_sem = [[sem(f"expert_w{m}_in{u}") for m in range(3)] for u in range(2)]
        hrow_in = [sem("hrow_in0"), sem("hrow_in1")]
        hg_done = [sem("hg_done0"), sem("hg_done1")]
        hg_ready = [sem("hg_ready0"), sem("hg_ready1")]
        up_done = [sem("up_done0"), sem("up_done1")]
        sil_ready = [sem("sil_ready0"), sem("sil_ready1")]
        hid_ready = [sem("hid_ready0"), sem("hid_ready1")]
        ht_done = [sem("ht_done0"), sem("ht_done1")]
        ht_ready = [sem("ht_ready0"), sem("ht_ready1")]
        down_done = [sem("down_done0"), sem("down_done1")]
        yo_ready = [sem("yo_ready0"), sem("yo_ready1")]
        yo_stored = [sem("yo_stored0"), sem("yo_stored1")]
        pick_in = [sem("pick_in0"), sem("pick_in1")]
        pick_used, fin_ss, fin_rstd, fin_ready = (sem(n) for n in (
            "pick_used", "fin_ss", "fin_rstd", "fin_ready"))
        out_stored = [sem("out_stored0"), sem("out_stored1")]

        N_SMALL = 4
        wv = w_in.rearrange("o (p k) n -> p (o k) n", k=KD)
        mv = w_mod.rearrange("o (p k) n -> p (o k) n", k=KD)

        def win(a, n):
            return wv[:, :, a:a + n], KD * n

        chunks = [("d", mv[:, :, 512 * j:512 * j + 512], 4096) for j in range(4)]
        for a, n in ((COL_LORA, N_LORA), (COL_RW + W, W), (COL_RW, W), (COL_RW + 2 * W, W),
                     (COL_Q, W), (COL_K, W), (COL_V, W)):
            chunks.append(("p", *win(a, n)))
        chunks.append(("p", w_o_sb.rearrange("o (k p) n -> p (o k) n", p=P), 4096))
        chunks += [("p", *win(COL_GATE, 512)), ("p", *win(COL_GATE + 512, 512))]
        chunks.append(("p", w_o_rw.rearrange("o (k p) n -> p (o k) n", p=P), 4096))
        chunks += [("p", *win(COL_GATE + D, 512)), ("p", *win(COL_GATE + D + 512, 512))]
        wo = w_out.rearrange("o (k p) n -> p (o k) n", p=P)
        chunks += [("p", wo[:, :, 0:512], 4096), ("p", wo[:, :, 512:1024], 4096)]
        LORA, CK, CR, CV, AQ, AK, AV_, OSB, GS0, GS1, ORW, GR0, GR1, WO0, WO1 = range(4, 19)

        def used_by(n):
            if n < LORA:
                return dve_chunk, n + 1
            return {LORA: (pa_done, 3), CK: (pa_done, 7), CR: (pa_done, 11), CV: (pa_done, 15), AQ: (pa_done, 31),
                    AK: (pa_done, 35), AV_: (pa_done, 39), OSB: (mix_done, 8), GS0: (mix_done, 12), GS1: (mix_done, 16),
                    ORW: (mix_done, 32), GR0: (mix_done, 23), GR1: (mix_done, 31), WO0: (y_done, NT), WO1: (y_done, NT)}[n]

        def arrived(eng, n):
            eng.wait_ge(ring_in[n % 3], 16 * (n // 3 + 1))

        def chunk(n, k, width=512):
            return ring[:, n % 3, 0:k * width].rearrange("p (k n) -> p k n", k=k)

        up1 = w_up1.rearrange("o e (p k) n -> p (o e) (k n)", k=KD)
        up3 = w_up3.rearrange("o e (p k) n -> p (o e) (k n)", k=KD)
        dn = w_down.rearrange("o e (k p) n -> p (o e) k n", p=P)
        esrc = [up1, up3, dn]

        def load_expert(eng, u, m, e):
            dst = eset[u][:, m, :]
            if m < 2:
                src = esrc[m][:, bass.ds(e, 1), :].rearrange("p a n -> p (a n)")
            else:
                src = dn[:, bass.ds(e, 1), :, :].rearrange("p a k n -> p (a k) n")
                dst = dst.rearrange("p (k n) -> p k n", k=4)
            eng.dma_start(dst, src).then_inc(w_in_sem[u][m], 16)

        block = ctx.enter_context(nc.Block())

        @block.sync
        def _(sp):
            for n, (kind, src, width) in enumerate(chunks):
                if n >= 3:
                    s, v = used_by(n - 3)
                    sp.wait_ge(s, v)
                dst = ring[:, n % 3, 0:width].rearrange("p (k n) -> p k n", k=src.shape[1])
                sp.dma_start(dst, src).then_inc(ring_in[n % 3], 16)
            for s_, v_ in (used_by(len(chunks) - 1),):
                sp.wait_ge(s_, v_)
            for m in range(3):
                load_expert(sp, 0, m, 0)
            sp.wait_ge(h2T_done, NT)
            sp.wait_ge(h2_ready, NT)
            sp.wait_ge(h2_stored[0], 32)
            sp.wait_ge(h2_stored[1], 32)
            for m in range(3):
                load_expert(sp, 1, m, 1)
            with sp.Fori(1, E // 2) as it:
                for u in range(2):
                    sp.wait_ge(up_done[u], it)
                    load_expert(sp, u, 0, 2 * it + u)
                    load_expert(sp, u, 1, 2 * it + u)
                    sp.wait_ge(down_done[u], it)
                    load_expert(sp, u, 2, 2 * it + u)
            sp.wait_ge(route_ready, 1)
            n_over = sp.value_load(nblk_i[0:1, 1:2], min_val=0, max_val=8)
            with sp.If(n_over > 0):
                with sp.Fori(0, n_over) as it:
                    for u in range(2):
                        e = sp.value_load(nblk_i[0:1, bass.ds(2 * it + 2 + u, 1)], min_val=0, max_val=E - 1)
                        sp.wait_ge(up_done[u], it + E // 2)
                        load_expert(sp, u, 0, e)
                        load_expert(sp, u, 1, e)
                        sp.wait_ge(down_done[u], it + E // 2)
                        load_expert(sp, u, 2, e)
            with sp.Else():
                sp.nop()
            sp.nop()
            for t in range(NT):
                sp.wait_ge(fin_ready, t + 1)
                sp.dma_start(out[0, P * t:P * t + P, :], fin[t % 2][:, 2, :]).then_inc(out_stored[t % 2], 16)
            sp.wait_ge(out_stored[0], 32)
            sp.wait_ge(out_stored[1], 32)

        @block.gpsimd
        def _(pool):
            nc.gpsimd.memset(S(10), 0.0).then_inc(zero_tile, 1)
            pool.wait_ge(zero_tile, 1)
            over = ye_dram[E * CAP:MAXB * CAP, :].rearrange("(p r) n -> p (r n)", p=P)
            for q in range(4):
                pool.dma_start(over[:, 2048 * q:2048 * q + 2048], S(10)).then_inc(zero_stored, 16)

            def diag(buf, ready):
                for j in range(NT):
                    v = buf[:, OFF[j]:OFF[j] + P]
                    last = nc.gpsimd.affine_select(out=v, in_=v, compare_op=ALU.is_gt, fill=0.0, base=0,
                                                   pattern=[[1, P]], channel_multiplier=-1)
                last.then_inc(ready, 1)

            for h in range(NH + 1):
                if h < NH:
                    pool.wait_ge(sp_ready, h + 1)
                    diag(sp_buf[h % 2], sp_masked)
                if h >= 1:
                    pool.wait_ge(att_ready, h)
                    diag(e_buf[(h - 1) % 2], att_masked)
            pool.wait_ge(yc_done, NCH)
            pool.wait_ge(zc_evac, NCH)
            for m in range(4):
                for j in (2 * m, 2 * m + 1):
                    if j >= 2:
                        pool.wait_ge(mring_free, j - 1)
                    dst = mring[j % 2].rearrange("p (k n) -> p k n", k=KD)
                    pool.dma_start(dst, mv[:, :, 2048 + 512 * j:2560 + 512 * j]).then_inc(mring_in[j % 2], 16)
                if m == 0:
                    pool.wait_ge(yrw_ready, 1)
                else:
                    pool.wait_ge(lrow_ready, m)
                pool.dma_start(rowp[:, 0, :], b_mod[0:1, D * (m + 2):D * (m + 3)].partition_broadcast(P)).then_inc(rowp_in, 16)
                gi = (1, None, 2, 3)[m]
                if gi is not None:
                    pool.dma_start(rowp[:, 1, :], gains[0, gi:gi + 1, :].partition_broadcast(P)).then_inc(rowp_in, 16)
            pool.wait_ge(route_ready, 1)
            pool.wait_ge(h2_stored[0], 32)
            pool.wait_ge(h2_stored[1], 32)
            steps = pool.value_load(nblk_i[0:1, 0:1], min_val=E // 2, max_val=MAXB // 2)
            with pool.Fori(0, steps) as it:
                for u in range(2):
                    pool.wait_ge(hg_done[u], it + 1)
                    nc.gpsimd.tensor_copy(idx_now[:, u:u + 1], idx_i[:, bass.ds(2 * it + u, 1)]).then_inc(pool_link, 1)
                    pool.wait_ge(pool_link, 2 * it + u + 1)
                    pool.sem_inc(pool_pass, 1)
                    nc.gpsimd.indirect_dma_start(
                        out=hrow[0:CAP, u, :], out_offset=None, in_=h2_dram,
                        in_offset=bass.IndirectOffsetOnAxis(ap=idx_now[:, u:u + 1], axis=0)).then_inc(hrow_in[u], 16)
            for u in range(2):
                pool.wait_ge(yo_stored[u], steps * 32 + 32)
                pool.sem_inc(pool_pass, 1)
            for t in range(NT):
                if t >= 2:
                    pool.wait_ge(pick_used, t - 1)
                for ch in range(2):
                    nc.gpsimd.indirect_dma_start(
                        out=fin[t % 2][:, ch, :], out_offset=None, in_=ye_dram,
                        in_offset=bass.IndirectOffsetOnAxis(ap=slots_i[:, 2 * t + ch:2 * t + ch + 1], axis=0)
                    ).then_inc(pick_in[t % 2], 16)

        @block.scalar
        def _(act):
            links = [0]

            def link(ins):
                links[0] += 1
                ins.then_inc(act_link, 1)
                act.wait_ge(act_link, links[0])

            A = nc.scalar.activation
            act.dma_start(xin[:, :, :], x.rearrange("o (t p) n -> p (o t) n", p=P)).then_inc(x_in, 16)
            act.dma_start(cst[:, :], consts).then_inc(consts_in, 16)
            act.dma_start(V("c"), c.rearrange("o (p k) -> p (o k)", k=KD)).then_inc(params_in, 16)
            for m in range(2):
                act.dma_start(V("bmod", 8 * m, 8), b_mod[0:1, D * m:D * m + D].rearrange("o (p k) -> p (o k)", k=KD)).then_inc(params_in, 16)
            act.dma_start(V("g0"), gains[0, 0:1, :].rearrange("o (p k) -> p (o k)", k=KD)).then_inc(params_in, 16)
            act.wait_ge(prow_zero, 1)
            act.dma_start(prow[0:14, :], shift_mu[0:1, 0:1792].rearrange("o (f p) -> (o f) p", p=P)).then_inc(rows_in, 16)
            act.dma_start(prow[14:15, 0:32], shift_mu[0:1, 1792:1824]).then_inc(rows_in, 16)
            for name, src in (("w0", w0), ("a0", a0), ("kk", k_k), ("ka", k_a), ("lnw", lnx_w), ("lnb", lnx_b),
                              ("gb", gate_bias)):
                a, w = PAR[name]
                act.dma_start(prow[a:a + w, :], src.rearrange("o (f p) -> (o f) p", p=P)).then_inc(rows_in, 16)
            a, w = PAR["rk"]
            act.dma_start(prow[a:a + w, :], r_k.rearrange("o (f a) d -> (o f) (a d)", a=2)).then_inc(rows_in, 16)
            act.dma_start(wlo[0:64, 0, :], w_decay_up[0]).then_inc(lora_in, 16)
            act.dma_start(wlo[64:128, 0, :], w_iclr_up[0]).then_inc(lora_in, 16)
            act.dma_start(wlo[:, 1, :], w_gate_up[0, 0:128, :]).then_inc(lora_in, 16)
            act.dma_start(wlo[0:32, 2, :], w_gate_up[0, 128:160, :]).then_inc(lora_in, 16)
            act.dma_start(wr[:, :, 0:NG], w_group.rearrange("o (p k) n -> p (o k) n", k=KD)).then_inc(lora_in, 16)
            act.dma_start(wr[:, :, NG:], w_router.rearrange("o (p k) n -> p (o k) n", k=KD)).then_inc(lora_in, 16)
            act.wait_ge(params_in, 16 * N_SMALL)
            act.wait_ge(consts_in, 16)
            link(A(V("silc"), V("c"), ACT.Sigmoid))
            act.wait_ge(x_in, 16)
            for t in range(NT):
                link(A(xn[:, t, :], xin[:, t, :], ACT.Square, accum_out=V("ss", t)))
            link(A(V("ss", 0, 4), V("ss", 0, 4), ACT.Ln, scale=1.0 / D, bias=eps_rms))
            A(V("rs", 8, 4), V("ss", 0, 4), ACT.Exp, scale=-0.5).then_inc(rstd0, 1)
            act.wait_ge(modcol_ready, 1)
            for k in range(KD):
                act.wait_ge(xT_done, k + 1)
                A(hT[:, k, :], ps[:, k % 4, :], ACT.Identity, scale=V("A1", k), bias=V("SH1", k)).then_inc(xT_evac, 1)

            g = 0

            def evac(dst, func, **kw):
                nonlocal g
                act.wait_ge(pa_done, g + 1)
                bank = ps[:, g % 6, 0:T]
                ins = A(dst, bank[0:dst.shape[0], :], func, **kw)
                ins.then_inc(pa_evac, 1)
                g += 1
                return ins

            for n in range(15):
                if n >= 2:
                    act.wait_ge(shifted, n - 1)
                rows_ = 32 if n == 2 else P
                evac(raw[0:rows_, n % 2, 1:T + 1], ACT.Copy)
                if n == 4:
                    act.wait_ge(shifted, 3)
                    A(lora[0:64, 0, :], lora[0:64, 0, :], ACT.Tanh)
                    A(lora[:, 1, :], lora[:, 1, :], ACT.Sigmoid)
                    A(lora[0:32, 2, :], lora[0:32, 2, :], ACT.Sigmoid).then_inc(lora_act, 1)
            for f in range(FT):
                evac(S4(s_sig)[:, f, :], ACT.Sigmoid, bias=V("w0", f))
            for f in range(FT):
                evac(S4(s_a)[:, f, :], ACT.Sigmoid, bias=V("a0", f))
            for f in range(FT):
                evac(S4(s_g)[:, f, :], ACT.Copy)
            for f in range(FT):
                evac(S4(s_q)[:, f, :], ACT.Copy, scale=HD ** -0.5)
            act.wait_ge(cum_ready, 1)
            A(S(s_P), S(s_cum), ACT.Exp, scale=-DECAY)
            A(S(s_Pi), S(s_cum), ACT.Exp, scale=DECAY)
            A(S(s_sig), S(s_sig), ACT.Exp, scale=-DECAY).then_inc(exps_ready, 1)
            act.wait_ge(kk_max, FT)
            link(A(S(s_kk2), S(s_kk2), ACT.Ln))
            A(S(s_kk2), S(s_kk2), ACT.Exp, scale=-0.5).then_inc(rn_ready, 1)
            for f in range(FT):
                evac(S4(s_ka)[:, f, :], ACT.Copy)
            act.wait_ge(tok_src, 1)
            for t in range(NT):
                evac(S4(s_va)[:, t, :], ACT.Copy)
            for n in range(0, 3 * NCH, 2):
                act.wait_ge(tr_done, n + 1)
                cc, dst = n % NCH, tok[(s_Vt, s_Bt, s_Kt)[n // NCH]]
                src = ps[0:64, n % 6, :].rearrange("p (f d) -> p f d", f=FT)
                A(dst[0:64, cc, :, :], src[:, :, 0:64], ACT.Copy)
                A(dst[64:128, cc, :, :], src[:, :, 64:128], ACT.Copy).then_inc(tr_act, 1)

            nc.scalar.preload_act_table_set("natural_log_exp_and_others")
            for h in range(NH + 1):
                if h < NH:
                    act.wait_ge(z_done, h + 1)
                    if h >= 2:
                        act.wait_ge(av_all, h - 1)
                    link(A(e_buf[h % 2], psf[:, 1536 * (h % 2):1536 * (h % 2) + ZW], ACT.Abs))
                    link(A(e_buf[h % 2], e_buf[h % 2], ACT.Exp, scale=-1.0))
                    A(e_buf[h % 2], e_buf[h % 2], ACT.Ln, bias=one).then_inc(log_ready, 1)
                if h >= 1:
                    g_ = h - 1
                    act.wait_ge(cum_done, g_ + 1)
                    A(e_buf[g_ % 2], psf[:, 1536 * (g_ % 2):1536 * (g_ % 2) + ZW], ACT.Exp).then_inc(att_ready, 1)
                    if g_ % 2 == 1:
                        f = g_ // 2
                        act.wait_ge(av_all, 2 * f + 2)
                        A(S4(s_q)[:, f, :], ps[:, 6 + f % 2, :], ACT.Copy).then_inc(ysb_ready, 1)

            for n in range(5 * FT):
                act.wait_ge(invw_done, n + 1)
                f = n % FT
                A(S4(s_W)[:, f, :], ps[:, f, :], ACT.Copy).then_inc(invw_evac, 1)
            for b in range(4):
                act.wait_ge(hp_done, b + 1)
                A(S(s_H)[:, 512 * b:512 * b + 512], ps[:, b, :], ACT.Copy).then_inc(hp_evac, 1)
            for cc in range(NCH):
                act.wait_ge(sa_done, cc + 1)
                if cc >= 2:
                    act.wait_ge(yc_done, cc - 1)
                A(SAs[:, cc % 2, :], ps[:, 5, 0:256], ACT.Copy).then_inc(sa_evac, 1)
                act.wait_ge(yc_done, cc + 1)
                A(S4(s_y)[:, :, C * cc:C * cc + C], ps[:, 7 if cc % 2 else 3, 0:256].rearrange("p (f t) -> p f t", f=FT),
                  ACT.Copy).then_inc(yc_evac, 1)
            act.dma_start(x1[:, :, :], x.rearrange("o (t p) n -> p (o t) n", p=P)).then_inc(x_again, 16)
            for f in range(FT):
                act.wait_ge(gn_sqsum, f + 1)
                link(A(S4(s_y2)[:, f, :], ps[:, 4 + f, :], ACT.Ln, scale=1.0 / HD, bias=eps_gn))
                A(S4(s_y2)[:, f, :], S4(s_y2)[:, f, :], ACT.Exp, scale=-0.5).then_inc(gn_rstd, 1)
            for n in range(8):
                act.wait_ge(mix_done, n + 1)
                A(merged[:, n, :], ps[:, n % 4, :], ACT.Copy).then_inc(osb_evac, 1)
            act.wait_ge(yrw_ready, 1)
            for n in range(16):
                grp = 8 + n if n < 8 else 16 + 2 * (n - 8)
                act.wait_ge(mix_done, grp + 1)
                if n >= 2:
                    act.wait_ge(merged_ready, n - 1)
                A(gate_t[:, n % 2, :], ps[:, grp % 4, :], ACT.Sigmoid, bias=V("gb", n)).then_inc(gate_evac, 1)
            for t in range(NT):
                act.wait_ge(y_done, t + 1)
                if t >= 2:
                    act.wait_ge(x1_ready, t - 1)
                bk = 2 * (t % 2)
                link(A(ytok[:, t % 2, :], psf[:, 512 * bk:512 * bk + D], ACT.Copy))
                link(A(psf[:, 512 * bk:512 * bk + D], ytok[:, t % 2, :], ACT.Square, accum_out=V("ss", 4 + t)))
                link(A(V("ss", 4 + t), V("ss", 4 + t), ACT.Ln, scale=1.0 / D, bias=eps_rms))
                A(V("rs", 4 + t), V("ss", 4 + t), ACT.Exp, scale=-0.5).then_inc(rstd1, 1)
                act.wait_ge(x1_ready, t + 1)
                link(A(ytok[:, t % 2, :], x1[:, t, :], ACT.Square, accum_out=V("ss", 8 + t)))
                link(A(V("ss", 8 + t), V("ss", 8 + t), ACT.Ln, scale=1.0 / D, bias=eps_rms))
                A(V("rs", 8 + t), V("ss", 8 + t), ACT.Exp, scale=-0.5).then_inc(rstd2, 1)
                act.wait_ge(h2_ready, t + 1)
                act.dma_start(h2_dram[P * t:P * t + P, :], h2tok[:, t % 2, :]).then_inc(h2_stored[t % 2], 16)
                act.wait_ge(h2T_done, t + 1)
                A(hT[:, :, P * t:P * t + P], psf[:, 2048:2048 + D].rearrange("p (k t) -> p k t", k=KD),
                  ACT.Copy).then_inc(h2T_evac, 1)
            act.wait_ge(gsum_in, 1)
            A(rt[:, 16:32], rt[:, 0:16], ACT.Exp)
            A(rt[:, 36:40], rt[:, 32:36], ACT.Exp).then_inc(gsum_ready, 1)
            act.wait_ge(route_ready, 1)
            nc.scalar.preload_act_table_set("silu_and_others")
            steps = act.value_load(nblk_i[0:1, 0:1], min_val=E // 2, max_val=MAXB // 2)
            for u in range(2):
                act.sem_inc(yo_stored[u], 32)
            with act.Fori(0, steps) as it:
                for u in range(2):
                    act.wait_ge(up_done[u], it + 1)
                    A(sil[:, u, :], ps[:, 2 + u, 0:256], ACT.Silu).then_inc(sil_ready[u], 1)
                    act.wait_ge(down_done[u], it + 1)
                    act.wait_ge(yo_stored[u], it * 32 + 32)
                    A(yo[:, u, :], ps[:, 4 + u, :], ACT.Copy).then_inc(yo_ready[u], 1)
                    act.wait_ge(yo_ready[u], it + 2)
                    for hf in range(2):
                        act.dma_start(ye_dram[bass.ds(it * (2 * CAP) + CAP * u, CAP), 512 * hf:512 * hf + 512],
                                      yo[64 * hf:64 * hf + 64, u, :]).then_inc(yo_stored[u], 16)
            for t in range(NT):
                act.wait_ge(fin_ss, t + 1)
                link(A(fin[t % 2][:, 3, :], fin[t % 2][:, 2, :], ACT.Square, accum_out=V("ss", 12 + t)))
                link(A(V("ss", 12 + t), V("ss", 12 + t), ACT.Ln, scale=1.0 / D, bias=eps_rms))
                A(V("rs", 12 + t), V("ss", 12 + t), ACT.Exp, scale=-0.5).then_inc(fin_rstd, 1)

        @block.vector
        def _(dve):
            links = [0]

            def link(ins):
                links[0] += 1
                ins.then_inc(dve_link, 1)
                dve.wait_ge(dve_link, links[0])

            TT, TS, STT, CP = (nc.vector.tensor_tensor, nc.vector.tensor_scalar, nc.vector.scalar_tensor_tensor,
                               nc.vector.tensor_copy)
            nc.vector.memset(prow[:, :], 0.0).then_inc(prow_zero, 1)
            dve.wait_ge(rows_turned, 1)
            link(CP(par[:, 0:NROW], ps[:, 6, 0:NROW]))
            dve.wait_ge(act_link, 1)
            link(TT(V("silc"), V("silc"), V("c"), ALU.mult))
            link(TS(V("omka"), V("ka"), -1.0, 1.0, ALU.mult, ALU.add))
            nc.vector.memset(raw[:, :, 0:1], 0.0)

            def modulation(acc, src_of, arrive, free, ready):
                arrive()
                for k in range(KD):
                    w = src_of[:, k, :]
                    if k == 0:
                        ins = TS(acc, w, V("silc", 0), None, ALU.mult)
                    else:
                        ins = STT(acc, w, V("silc", k), acc, ALU.mult, ALU.add)
                    if k < KD - 1:
                        link(ins)
                ins.then_inc(dve_link, 1)
                links[0] += 1
                dve.wait_ge(dve_link, links[0])
                nc.vector.engine_nop().then_inc(free, 1)
                if ready is not None:
                    nc.vector.engine_nop().then_inc(ready, 1)

            modulation(acc_e[:, 0, 0:512], chunk(0, KD), lambda: arrived(dve, 0), dve_chunk, None)
            modulation(acc_e[:, 0, 512:1024], chunk(1, KD), lambda: arrived(dve, 1), dve_chunk, acc_ready)
            dve.wait_ge(rstd0, 1)
            for t in range(NT):
                TS(xn[:, t, :], xin[:, t, :], V("rs", 8 + t), None, ALU.mult).then_inc(xn_ready, 1)
            modulation(acc_e[:, 1, 0:512], chunk(2, KD), lambda: arrived(dve, 2), dve_chunk, None)
            modulation(acc_e[:, 1, 512:1024], chunk(3, KD), lambda: arrived(dve, 3), dve_chunk, acc_ready)
            dve.wait_ge(modcol_done, 1)
            TT(V("SH1"), ps[:, 7, 0:8], V("bmod", 0, 8), ALU.add)
            link(TT(V("A1"), ps[:, 7, 8:16], V("bmod", 8, 8), ALU.add))
            STT(V("A1"), V("A1"), 1.0, V("g0"), ALU.add, ALU.mult).then_inc(modcol_ready, 1)

            order = [(12, lora[:, 0, :], P), (13, lora[:, 1, :], P), (14, lora[0:32, 2, :], 32)]
            order += [(4 + f, S4(s_k)[:, f, :], P) for f in range(FT)]
            order += [(f, S4(s_r)[:, f, :], P) for f in range(FT)]
            order += [(8 + f, S4(s_v)[:, f, :], P) for f in range(FT)]
            for n, (m, dst, r_) in enumerate(order):
                dve.wait_ge(pa_evac, n + 1)
                if n == 3:
                    dve.wait_ge(xT_done, KD)
                    dve.wait_ge(zero_stored, 64)
                b = raw[0:r_, n % 2, :]
                link(TT(dst, b[:, 0:T], b[:, 1:T + 1], ALU.subtract))
                STT(dst, dst, V("mu", m)[0:r_, :], b[:, 1:T + 1], ALU.mult, ALU.add).then_inc(shifted, 1)
            dve.wait_ge(shifted, 15)
            for f in range(FT):
                ins = TS(S4(s_kk)[:, f, :], S4(s_k)[:, f, :], V("kk", f), None, ALU.mult)
            link(ins)
            TT(S(s_kk2), S(s_kk), S(s_kk), ALU.mult).then_inc(kk2_ready, 1)
            for f in range(FT):
                dve.wait_ge(pa_evac, 15 + f + 1)
                for cc in range(NCH):
                    sl = slice(C * cc, C * cc + C)
                    ins = nc.vector.tensor_tensor_scan(S4(s_cum)[:, f, sl], K("ones")[:, 0:C], S4(s_sig)[:, f, sl], 0.0,
                                                       ALU.mult, ALU.add)
            link(ins)
            TT(S(s_sig), S(s_cum), S(s_sig), ALU.subtract).then_inc(cum_ready, 1)
            for f in range(FT):
                dve.wait_ge(pd_done, f + 1)
                TS(S4(s_kk2)[:, f, :], ps[:, 6 + f % 2, :], 1e-24, None, ALU.max).then_inc(kk_max, 1)
            dve.wait_ge(rn_ready, 1)
            dve.wait_ge(exps_ready, 1)
            dve.wait_ge(pa_evac, 15 + 2 * FT)
            link(TT(S(s_kk), S(s_kk), S(s_kk2), ALU.mult))
            link(TT(S(s_kk2), S(s_kk), S(s_a), ALU.mult))
            dve.wait_ge(pa_done, 15 + 3 * FT)
            ARv = S(s_AR, 2).rearrange("p (g a t) -> p g a t", a=2, t=C)
            P3 = lambda i: S(i).rearrange("p (g t) -> p g t", t=C)
            link(STT(ARv[:, :, 0, :], P3(s_kk), -1.0, P3(s_sig), ALU.mult, ALU.mult))
            link(TT(S(s_B), S(s_kk2), S(s_Pi), ALU.mult))
            for f in range(FT):
                ins = TS(S4(s_a)[:, f, :], S4(s_a)[:, f, :], V("ka", f), V("omka", f), ALU.mult, ALU.add)
            link(ins)
            link(TT(S(s_k), S(s_k), S(s_a), ALU.mult))
            for f in range(FT):
                ins = STT(S4(s_a)[:, f, :], S4(s_r)[:, f, :], V("rk", f), S4(s_k)[:, f, :], ALU.mult, ALU.mult)
            ins.then_inc(bonus_in, 1)
            TT(ARv[:, :, 1, :], P3(s_r), P3(s_P), ALU.mult)
            link(CP(PC[:, :], P3(s_P)[:, :, C - 1]))
            link(TT(S(s_Kd), S(s_k), S(s_Pi), ALU.mult))
            pcb = PC[:, :].rearrange("p (g o) -> p g o", o=1).broadcast_to((P, FT * NCH, C))
            TT(P3(s_Bh), P3(s_B), pcb, ALU.mult)
            TT(P3(s_Kh), P3(s_Kd), pcb, ALU.mult).then_inc(tok_src, 1)
            dve.wait_ge(bonus_in, 1)
            for f in range(FT):
                dve.wait_ge(pd_done, FT + f + 1)
                TT(S4(s_bonus)[:, f, :], ps[:, 6 + f % 2, :], S4(s_v)[:, f, :], ALU.mult).then_inc(bonus_ready, 1)
            for n in range(1, 3 * NCH, 2):
                dve.wait_ge(tr_done, n + 1)
                cc, dst = n % NCH, tok[(s_Vt, s_Bt, s_Kt)[n // NCH]]
                src = ps[0:64, n % 6, :].rearrange("p (f d) -> p f d", f=FT)
                CP(dst[0:64, cc, :, :], src[:, :, 0:64])
                CP(dst[64:128, cc, :, :], src[:, :, 64:128]).then_inc(tr_dve, 1)

            dve.wait_ge(tr_done, 3 * NCH)
            for h in range(NH):
                z = psf[:, 1536 * (h % 2):1536 * (h % 2) + ZW]
                dve.wait_ge(log_ready, h + 1)
                STT(sp_buf[h % 2], z, 0.0, e_buf[h % 2], ALU.max, ALU.add).then_inc(sp_ready, 1)

            dve.wait_ge(av_all, NH)
            eyeb = K("eye").rearrange("p (o t) -> p o t", o=1).broadcast_to((P, FT * NCH, C))
            CP(P3(s_X), eyeb)
            link(CP(P3(s_XT), eyeb))

            def mk(name, k=0):
                return K(name)[:, 64 * k:64 * k + 64].rearrange("p (o t) -> p o t", o=1).broadcast_to((P, NCH, C))

            for f in range(FT):
                BA = psf[:, 0:1024].rearrange("p (c a t) -> p c a t", c=NCH, a=2)
                KA = psf[:, 1024:2048].rearrange("p (c a t) -> p c a t", c=NCH, a=2)
                MM = ps[:, 4 + f % 2, :].rearrange("p (c t) -> p c t", c=NCH)
                dve.wait_ge(gram_done, 3 * f + 1)
                TT(chk[s_MT][:, f], BA[:, :, 0, :], mk("strictU"), ALU.mult)
                nc.vector.copy_predicated(chk[s_XT][:, f], mk("lvlU").bitcast(I32), BA[:, :, 0, :])
                dve.wait_ge(gram_done, 3 * f + 3)
                TT(chk[s_Mrb][:, f], BA[:, :, 1, :], mk("inclU"), ALU.mult).then_inc(gram_evac, 1)
                TT(chk[s_Mak][:, f], KA[:, :, 0, :], mk("strictU"), ALU.mult)
                TT(chk[s_Mrk][:, f], KA[:, :, 1, :], mk("inclU"), ALU.mult).then_inc(gram_evac, 1)
                nc.vector.copy_predicated(chk[s_X][:, f], mk("lvlL").bitcast(I32), MM).then_inc(gram_evac, 1)
            for k in range(1, 6):
                for f in range(FT):
                    n = FT * (k - 1) + f
                    dve.wait_ge(invu_done, n + 1)
                    if k < 5:
                        nc.vector.copy_predicated(chk[s_X][:, f], mk("lvlL", k).bitcast(I32),
                                                  ps[:, 4 + 2 * (f % 2), :].rearrange("p (c t) -> p c t", c=NCH))
                    nc.vector.copy_predicated(chk[s_XT][:, f], mk("lvlU", k).bitcast(I32),
                                              ps[:, 5 + 2 * (f % 2), :].rearrange("p (c t) -> p c t", c=NCH)
                                              ).then_inc(invu_evac, 1)
            PCv = PC[:, :].rearrange("p (f c) -> p f c", c=NCH)
            f4 = lambda a: a.rearrange("p (f v) -> p f v", f=FT)
            for cc in range(NCH):
                if cc == 0:
                    dve.wait_ge(hp_evac, 4)
                    CP(Zs[:, :], tok[s_H][:, 0, :, :].rearrange("p f v -> p (f v)")).then_inc(zc_evac, 1)
                else:
                    dve.wait_ge(zc_done, cc)
                    dve.wait_ge(sa_done, cc)
                    TT(Zs[:, :], ps[:, 4, 0:256], tok[s_H][:, cc, :, :].rearrange("p f v -> p (f v)"), ALU.add).then_inc(zc_evac, 1)
                if cc < NCH - 1:
                    if cc == 0:
                        dve.wait_ge(st_done, 1)
                        CP(ST[:, 1, :], ps[:, 6, 0:256]).then_inc(st_evac, 1)
                    else:
                        dve.wait_ge(st_evac, cc)
                        pc1 = PCv[:, :, cc:cc + 1].broadcast_to((P, FT, HD))
                        link(TT(f4(SD[:, :]), f4(ST[:, cc % 2, :]), pc1, ALU.mult))
                        dve.wait_ge(st_done, cc + 1)
                        dve.wait_ge(yc_done, cc)
                        TT(ST[:, (cc + 1) % 2, :], SD[:, :], ps[:, 6, 0:256], ALU.add).then_inc(st_evac, 1)
            for f in range(FT):
                dve.wait_ge(gn_sum, f + 1)
                STT(S4(s_y)[:, f, :], ps[:, f, :], -1.0 / HD, S4(s_y)[:, f, :], ALU.mult, ALU.add).then_inc(yrw_mean, 1)
                dve.wait_ge(yrw_mean, f + 1)
                TT(S4(s_y2)[:, f, :], S4(s_y)[:, f, :], S4(s_y)[:, f, :], ALU.mult).then_inc(gn_sq, 1)
            for f in range(FT):
                dve.wait_ge(gn_rstd, f + 1)
                y = S4(s_y)[:, f, :]
                link(TT(y, y, S4(s_y2)[:, f, :], ALU.mult))
                link(TS(y, y, V("lnw", f), V("lnb", f), ALU.mult, ALU.add))
                link(TT(y, y, S4(s_bonus)[:, f, :], ALU.add))
                ins = TT(y, y, S4(s_g)[:, f, :], ALU.mult)
            ins.then_inc(yrw_ready, 1)
            dve.wait_ge(yrw_ready, 1)
            def late_half(j):
                modulation(acc_l[:, j % 2, 0:512], mring[j % 2].rearrange("p (k n) -> p k n", k=KD),
                           lambda: dve.wait_ge(mring_in[j % 2], 16 * (j // 2 + 1)), mring_free, lacc_ready)

            def late_rows(m):
                dve.wait_ge(rowp_in, (32, 48, 80, 112)[m])
                dve.wait_ge(lrow_done, 2 * m + 2)
                for hf in range(2):
                    dst = rows[:, m, 512 * hf:512 * hf + 512]
                    b_, g_ = rowp[:, 0, 512 * hf:512 * hf + 512], rowp[:, 1, 512 * hf:512 * hf + 512]
                    ins = TT(dst, ps[:, 6 + hf, :], b_, ALU.add)
                    if m != 1:
                        link(ins)
                        ins = STT(dst, dst, 1.0 if m == 2 else 0.0, g_, ALU.add, ALU.mult)
                    if not hf:
                        link(ins)
                ins.then_inc(lrow_ready, 1)

            for n in range(8):
                dve.wait_ge(gate_evac, n + 1)
                TT(merged[:, n, :], merged[:, n, :], gate_t[:, n % 2, :], ALU.mult).then_inc(merged_ready, 1)
                if n in (1, 3, 6, 7):
                    late_half((0, 1, 2, 3)[(1, 3, 6, 7).index(n)])
                if n == 5:
                    late_rows(0)
            for n in range(8):
                dve.wait_ge(gate_evac, 8 + n + 1)
                dve.wait_ge(mix_done, 16 + 2 * n + 2)
                link(TT(gate_t[:, 2 + n % 2, :], gate_t[:, n % 2, :], ps[:, (17 + 2 * n) % 4, :], ALU.mult))
                TT(merged[:, n, :], merged[:, n, :], gate_t[:, 2 + n % 2, :], ALU.add).then_inc(merged_ready, 1)
                if n in (1, 4):
                    late_rows(1 + n // 4)
                elif n in (2, 3, 5, 6):
                    late_half(4 + (2, 3, 5, 6).index(n))
            late_rows(3)
            dve.wait_ge(lrow_ready, 4)
            dve.wait_ge(x_again, 16)
            for t in range(NT):
                dve.wait_ge(rstd1, t + 1)
                y = ytok[:, t % 2, :]
                link(STT(y, y, V("rs", 4 + t), rows[:, 0, :], ALU.mult, ALU.mult))
                TT(x1[:, t, :], x1[:, t, :], y, ALU.add).then_inc(x1_ready, 1)
                dve.wait_ge(rstd2, t + 1)
                if t >= 2:
                    dve.wait_ge(h2_stored[t % 2], 16)
                    dve.wait_ge(h2T_done, t - 1)
                hh = h2tok[:, t % 2, :]
                link(STT(hh, x1[:, t, :], V("rs", 8 + t), rows[:, 2, :], ALU.mult, ALU.mult))
                TT(hh, hh, rows[:, 1, :], ALU.add).then_inc(h2_ready, 1)
            R = rview
            gl, el = R(0, 16, 4), R(16, 128, 4)
            dve.wait_ge(logit_done, 1)
            lg = psf[:, 0:4 * 64].rearrange("p (t n) -> p t n", t=NT)
            CP(gl, lg[:, :, 0:NG])
            link(CP(el, lg[:, :, NG:NG + E]))
            gmax = rt[:, 40:44].rearrange("p (t o) -> p t o", o=1)
            bc = lambda a, n: a.broadcast_to((P, NT, n))
            io = K("iota64").rearrange("p (o n) -> p o n", o=1)
            o1 = lambda a: a.rearrange("p (t o) -> p t o", o=1)
            link(nc.vector.tensor_reduce(gmax, gl, AX, ALU.max))
            link(TT(rt[:, 0:16].rearrange("p (t n) -> p t n", t=NT), gl, bc(gmax, NG), ALU.subtract))

            def first_max(vals, n, mx, oh, tmp, idx):
                link(nc.vector.tensor_reduce(mx, vals, AX, ALU.max))
                link(TT(tmp, vals, bc(mx, n), ALU.is_lt))
                link(STT(tmp, tmp, 64.0, io[:, :, 0:n].broadcast_to((P, NT, n)), ALU.mult, ALU.add))
                link(nc.vector.tensor_reduce(idx, tmp, AX, ALU.min))
                link(TT(oh, io[:, :, 0:n].broadcast_to((P, NT, n)), bc(idx, n), ALU.is_equal))

            ohg, tmg = R(144, 16, 4), R(160, 16, 4)
            i_g, m1, m2, i1, i2 = (o1(rt[:, a:a + 4]) for a in (44, 48, 52, 56, 60))
            first_max(gl, NG, gmax, ohg, tmg, i_g)
            ml, tme, oh1, oh2, oh = (R(a, 128, 4) for a in (176, 304, 432, 560, 688))
            g8 = lambda a: a.rearrange("p t (g e) -> p (t g) e", e=EG)
            og = R(144, 16, 16)
            link(TT(g8(ml), g8(el), og.broadcast_to((P, 16, EG)), ALU.mult))
            link(TS(R(144, 16, 4), ohg, 1.0, BIG, ALU.subtract, ALU.mult))
            link(TT(g8(ml), g8(ml), og.broadcast_to((P, 16, EG)), ALU.add))
            first_max(ml, E, m1, oh1, tme, i1)
            link(STT(tme, oh1, -2 * BIG, ml, ALU.mult, ALU.add))
            link(CP(ml, tme))
            first_max(ml, E, m2, oh2, tme, i2)
            link(TT(o1(rt[:, 32:36]), m2, m1, ALU.subtract))
            TT(oh, oh1, oh2, ALU.add).then_inc(gsum_in, 1)
            dve.wait_ge(gsum_in, 1)
            nc.vector.engine_nop().then_inc(oh_ready, 1)
            dve.wait_ge(gsum_ready, 1)
            gs = o1(rt[:, 64:68])
            link(nc.vector.tensor_reduce(gs, rt[:, 16:32].rearrange("p (t n) -> p t n", t=NT), AX, ALU.add))
            link(STT(rt[:, 68:72], rt[:, 36:40], 1.0, rt[:, 64:68], ALU.add, ALU.mult))
            link(nc.vector.reciprocal(routf[:, 0:4], rt[:, 68:72]))
            link(TT(routf[:, 4:8], routf[:, 0:4], rt[:, 36:40], ALU.mult))
            dve.wait_ge(rank_done, 1)
            rk_all = R(816, 128, 4)
            link(CP(rk_all, ps[:, 1, 0:128].rearrange("p (t e) -> p t e", t=NT)))
            cnt, nov, ends, base = rt[:, 72:104], rt[:, 104:136], rt[:, 136:168], rt[:, 168:200]
            link(CP(cnt, ps[:, 2, 0:E]))
            cmp7 = R(944, 7 * E, 7)
            link(TT(cmp7, cnt.rearrange("p (o e) -> p o e", o=1).broadcast_to((P, 7, E)),
                    K("m64")[:, 1:8].rearrange("p (m o) -> p m o", o=1).broadcast_to((P, 7, E)), ALU.is_gt))
            link(nc.vector.tensor_reduce(nov.rearrange("p (e o) -> p e o", o=1), cmp7.rearrange("p m e -> p e m"), AX, ALU.add))
            link(nc.vector.tensor_tensor_scan(ends, K("ones")[:, 0:E], nov, float(E), ALU.mult, ALU.add))
            link(TT(base, ends, nov, ALU.subtract))
            for ch, (ohc, ic) in enumerate(((oh1, i1), (oh2, i2))):
                rk_, bs_, q_, blk_, t1, rr = (rt[:, 200 + 24 * ch + 4 * a:204 + 24 * ch + 4 * a] for a in range(6))
                link(TT(tme, rk_all, ohc, ALU.mult))
                link(nc.vector.tensor_reduce(o1(rk_), tme, AX, ALU.add))
                link(TT(tme, ohc, base.rearrange("p (o e) -> p o e", o=1).broadcast_to((P, NT, E)), ALU.mult))
                link(nc.vector.tensor_reduce(o1(bs_), tme, AX, ALU.add))
                c7 = R(944, 28, 4)
                link(TT(c7, o1(rk_).broadcast_to((P, NT, 7)),
                        K("m64")[:, 1:8].rearrange("p (o m) -> p o m", o=1).broadcast_to((P, NT, 7)), ALU.is_ge))
                link(nc.vector.tensor_reduce(o1(q_), c7, AX, ALU.add))
                link(STT(blk_, bs_, -1.0, q_, ALU.add, ALU.add))
                link(TT(blk_, blk_, ic.rearrange("p t o -> p (t o)"), ALU.subtract))
                link(TS(t1, q_, 0.0, None, ALU.is_gt))
                link(TT(blk_, blk_, t1, ALU.mult))
                link(TT(blk_, blk_, ic.rearrange("p t o -> p (t o)"), ALU.add))
                link(STT(rr, q_, -float(CAP), rk_, ALU.mult, ALU.add))
                link(STT(routf[:, 8:16].rearrange("p (t c) -> p c t", c=2)[:, ch, :], blk_, float(CAP), rr, ALU.mult, ALU.add))
                ohr = R(1168 + 256 * ch, 256, 4)
                link(TT(ohr, io[:, :, 0:CAP].broadcast_to((P, NT, CAP)), o1(rr).broadcast_to((P, NT, CAP)), ALU.is_equal))
                ohb = selb[:, ch]
                link(TT(ohb, io[:, :, 0:MAXB].broadcast_to((P, NT, MAXB)), o1(blk_).broadcast_to((P, NT, MAXB)), ALU.is_equal))
                link(TT(ohb, ohb, o1(K("tok")).broadcast_to((P, NT, MAXB)), ALU.mult))
            link(CP(slots_i[:, :], routf[:, 8:16]))
            nc.vector.engine_nop().then_inc(sel_ready, 1)
            ov = ovb
            b16 = K("blk16")[0:1, :].rearrange("p (m o) -> p m o", o=1).broadcast_to((1, 16, E))
            link(TT(ov[0:1], ends[0:1].rearrange("p (o e) -> p o e", o=1).broadcast_to((1, 16, E)), b16, ALU.is_le))
            link(nc.vector.tensor_reduce(rt[0:1, 260:276].rearrange("p (m o) -> p m o", o=1), ov[0:1], AX, ALU.add))
            link(TS(rt[0:1, 260:276], rt[0:1, 260:276], float(E - 1), None, ALU.min))
            link(CP(nblk_i[0:1, 2:18], rt[0:1, 260:276]))
            lt8 = rt[0:1, 276:284]
            link(TT(lt8, K("blk16")[0:1, 0:16:2], ends[0:1, E - 1:E].broadcast_to((1, 8)), ALU.is_lt))
            link(nc.vector.tensor_reduce(rt[0:1, 284:285], lt8, AX, ALU.add))
            link(CP(nblk_i[0:1, 1:2], rt[0:1, 284:285]))
            link(TS(nblk_i[0:1, 0:1], rt[0:1, 284:285], float(E // 2), None, ALU.add))
            dve.wait_ge(idx_done, 1)
            link(CP(idx_i[:, :], ps[0:CAP, 3, 0:MAXB]))
            nc.vector.engine_nop().then_inc(route_ready, 1)
            dve.wait_ge(route_ready, 1)
            steps = dve.value_load(nblk_i[0:1, 0:1], min_val=E // 2, max_val=MAXB // 2)
            with dve.Fori(0, steps) as it:
                for u in range(2):
                    dve.wait_ge(hg_done[u], it + 2)
                    CP(hgT[:, u, :, :].rearrange("p k s -> p (k s)"), ps[:, 0, :]).then_inc(hg_ready[u], 1)
                    dve.wait_ge(sil_ready[u], it + 1)
                    TT(hid[:, u, :], sil[:, u, :], ps[:, 2 + u, 256:512], ALU.mult).then_inc(hid_ready[u], 1)
                    dve.wait_ge(ht_done[u], it + 1)
                    CP(hidT[:, u, :], ps[:, 1, 0:256]).then_inc(ht_ready[u], 1)
            for t in range(NT):
                dve.wait_ge(pick_in[t % 2], 32 * (t // 2 + 1))
                if t >= 2:
                    dve.wait_ge(out_stored[t % 2], 16)
                b = fin[t % 2]
                link(TS(b[:, 2, :], b[:, 0, :], routf[:, t:t + 1], None, ALU.mult))
                STT(b[:, 2, :], b[:, 1, :], routf[:, 4 + t:5 + t], b[:, 2, :], ALU.mult, ALU.add).then_inc(fin_ss, 1)
                dve.wait_ge(fin_rstd, t + 1)
                link(STT(b[:, 2, :], b[:, 2, :], V("rs", 12 + t), rows[:, 3, :], ALU.mult, ALU.mult))
                nc.vector.tensor_tensor(b[:, 2, :], b[:, 2, :], x1[:, t, :], ALU.add).then_inc(fin_ready, 1)
                if t < NT - 1:
                    nc.vector.engine_nop().then_inc(pick_used, 1)

        @block.tensor
        def _(pe):
            mm, tr = nc.tensor.matmul, nc.tensor.transpose
            ident = K("ident")
            pe.wait_ge(consts_in, 16)
            pe.wait_ge(rows_in, 16 * 10)
            tr(ps[:, 6, 0:NROW], prow[:, :], ident[0:NROW, 0:NROW]).then_inc(rows_turned, 1)
            for m in range(2):
                pe.wait_ge(acc_ready, m + 1)
                a = acc_e[:, m, :].rearrange("p (q k) -> p k q", k=KD)
                for k in range(KD):
                    last = mm(ps[:, 7, 8 * m + k:8 * m + k + 1], a[:, k, :], K("ones")[:, 0:1], start=True, stop=True)
            last.then_inc(modcol_done, 1)
            pe.wait_ge(xn_ready, NT)
            for k in range(KD):
                if k >= 4:
                    pe.wait_ge(xT_evac, k - 3)
                for t in range(NT):
                    src = xn[:, t, :].rearrange("p (q k) -> p k q", k=KD)[:, k, :]
                    last = tr(ps[:, k % 4, P * t:P * t + P], src, ident)
                last.then_inc(xT_done, 1)
            pe.wait_ge(xT_evac, KD)

            g = 0

            def group():
                nonlocal g
                if g >= 6:
                    pe.wait_ge(pa_evac, g - 5)
                g += 1
                return (g - 1) % 6

            def project(n, tiles, width=512, cols=P):
                w = chunk(n, KD, width)
                arrived(pe, n)
                for i, (a, m_) in enumerate(tiles):
                    b = group()
                    for k in range(KD):
                        last = mm(ps[0:m_, b, :], w[:, k, a:a + m_], hT[:, k, :], start=(k == 0), stop=(k == KD - 1))
                    last.then_inc(pa_done, 1)

            full = [(P * f, P) for f in range(FT)]
            project(LORA, [(0, P), (128, P), (256, 32)], N_LORA)
            project(CK, full)
            project(CR, full)
            project(CV, full)
            pe.wait_ge(lora_in, 16 * 6)
            pe.wait_ge(lora_act, 1)
            pe.wait_ge(shifted, 3)
            for f in range(FT):
                mm(ps[:, group(), :], wlo[0:64, 0, P * f:P * f + P], lora[0:64, 0, :], start=True, stop=True).then_inc(pa_done, 1)
            for f in range(FT):
                mm(ps[:, group(), :], wlo[64:128, 0, P * f:P * f + P], lora[64:128, 0, :], start=True, stop=True).then_inc(pa_done, 1)
            for f in range(FT):
                b = group()
                mm(ps[:, b, :], wlo[:, 1, P * f:P * f + P], lora[:, 1, :], start=True, stop=False)
                mm(ps[:, b, :], wlo[0:32, 2, P * f:P * f + P], lora[0:32, 2, :], start=False, stop=True).then_inc(pa_done, 1)
            project(AQ, full)
            pe.wait_ge(kk2_ready, 1)
            for f in range(FT):
                if f >= 2:
                    pe.wait_ge(kk_max, f - 1)
                mm(ps[:, 6 + f % 2, :], K("blk"), S4(s_kk2)[:, f, :], start=True, stop=True).then_inc(pd_done, 1)
            project(AK, full)
            pe.wait_ge(bonus_in, 1)
            for f in range(FT):
                if f >= 2:
                    pe.wait_ge(bonus_ready, f - 1)
                mm(ps[:, 6 + f % 2, :], K("blk"), S4(s_bonus)[:, f, :], start=True, stop=True).then_inc(pd_done, 1)
            arrived(pe, AV_)
            w = chunk(AV_, KD)
            for t in range(NT):
                b = group()
                for k in range(KD):
                    last = mm(ps[:, b, :], hT[:, k, P * t:P * t + P], w[:, k, :], start=(k == 0), stop=(k == KD - 1))
                last.then_inc(pa_done, 1)
            pe.wait_ge(pa_evac, g)
            pe.wait_ge(tok_src, 1)
            pe.wait_ge(bonus_ready, FT)
            for n in range(3 * NCH):
                if n >= 6:
                    s = tr_act if n % 2 == 0 else tr_dve
                    pe.wait_ge(s, (n - 6) // 2 + 1)
                src = (s_v, s_Bh, s_Kh)[n // NCH]
                cc = n % NCH
                for f in range(FT):
                    last = tr(ps[0:64, n % 6, P * f:P * f + P], S4(src)[:, f, C * cc:C * cc + C], ident)
                last.then_inc(tr_done, 1)
            pe.wait_ge(tr_act, 12)
            pe.wait_ge(tr_dve, 12)

            def scores(h):
                f, a = h // 2, HD * (h % 2)
                if h >= 2:
                    pe.wait_ge(att_ready, h - 1)
                for j in (0, 1, 3, 2):
                    o = 1536 * (h % 2) + OFF[j]
                    last = mm(psf[:, o:o + WID[j]], S4(s_ka)[a:a + HD, f, P * j:P * j + P],
                              S4(s_q)[a:a + HD, f, P * j:T], start=(j != 3), stop=True, skip_group_check=True)
                last.then_inc(z_done, 1)

            def sums(h):
                pe.wait_ge(sp_masked, h + 1)
                sp = sp_buf[h % 2]
                for j in range(NT):
                    for jj in range(j, NT):
                        o = 1536 * (h % 2) + OFF[j] + P * (jj - j)
                        last = mm(psf[:, o:o + WID[jj]], K("ntri") if jj == j else K("nones"),
                                  sp[:, OFF[jj]:OFF[jj] + WID[jj]], start=False, stop=True, skip_group_check=True)
                last.then_inc(cum_done, 1)

            def values(h):
                f, a = h // 2, HD * (h % 2)
                if h % 2 == 0 and f >= 2:
                    pe.wait_ge(ysb_ready, f - 1)
                pe.wait_ge(att_masked, h + 1)
                for j in range(NT):
                    last = mm(ps[a:a + HD, 6 + f % 2, P * j:T], S4(s_va)[:, j, HD * h:HD * h + HD],
                              e_buf[h % 2][:, OFF[j]:OFF[j] + WID[j]], start=(j == 0), stop=(j == NT - 1),
                              skip_group_check=True)
                last.then_inc(av_all, 1)

            scores(0)
            for h in range(NH):
                if h + 1 < NH:
                    scores(h + 1)
                sums(h)
                values(h)
            pe.wait_ge(ysb_ready, FT)

            for f in range(FT):
                if f >= 1:
                    pe.wait_ge(gram_evac, 3 * f)
                for (src, o) in ((s_B, 0), (s_Kd, 1024)):
                    for cc in range(NCH):
                        for a in (0, HD):
                            last = mm(psf[a:a + HD, o + P * cc:o + P * cc + P], chk[src][a:a + HD, f, cc, :],
                                      AR[a:a + HD, f, cc, :, :].rearrange("p a t -> p (a t)"), start=True, stop=True,
                                      skip_group_check=True)
                    last.then_inc(gram_done, 1)
                for cc in range(NCH):
                    for a in (0, HD):
                        last = mm(ps[a:a + HD, 4 + f % 2, C * cc:C * cc + C], AR[a:a + HD, f, cc, 0, :],
                                  chk[s_B][a:a + HD, f, cc, :], start=True, stop=True, skip_group_check=True)
                last.then_inc(gram_done, 1)
            pe.wait_ge(gram_evac, 3 * FT)

            def tiles64(bank, lhs, rhs, f, sig):
                for cc in range(NCH):
                    for a in (0, HD):
                        last = mm(ps[a:a + HD, bank, C * cc:C * cc + C], chk[lhs][a:a + HD, f, cc, :],
                                  chk[rhs][a:a + HD, f, cc, :], start=True, stop=True, skip_group_check=True)
                if sig is not None:
                    last.then_inc(sig, 1)

            for k in range(1, 6):
                for f in range(FT):
                    if k > 1:
                        pe.wait_ge(invu_evac, FT * (k - 2) + f + 1)
                    tiles64(f, s_MT, s_X, f, invw_done)
                for f in range(FT):
                    n = FT * (k - 1) + f
                    pe.wait_ge(invw_evac, n + 1)
                    if n >= 2:
                        pe.wait_ge(invu_evac, n - 1)
                    if k < 5:
                        tiles64(4 + 2 * (f % 2), s_XT, s_W, f, None)
                    tiles64(5 + 2 * (f % 2), s_W, s_XT, f, invu_done)
            pe.wait_ge(invu_evac, 5 * FT)
            for b in range(4):
                for cc in (2 * b, 2 * b + 1):
                    for f in range(FT):
                        for a in (0, HD):
                            o = 256 * (cc % 2) + HD * f
                            last = mm(ps[a:a + HD, b, o:o + HD], chk[s_Mak][a:a + HD, f, cc, :],
                                      tok[s_Vt][a:a + HD, cc, f, :], start=True, stop=True, skip_group_check=True)
                last.then_inc(hp_done, 1)
            fa = [(f, a) for f in range(FT) for a in (0, HD)]
            for cc in range(NCH):
                cur = ST[:, cc % 2, :]
                if cc:
                    pe.wait_ge(st_evac, cc)
                    for f, a in fa:
                        last = mm(ps[a:a + HD, 4, HD * f:HD * f + HD], AR[a:a + HD, f, cc, 0, :],
                                  cur[a:a + HD, HD * f:HD * f + HD], start=True, stop=True, skip_group_check=True)
                    last.then_inc(zc_done, 1)
                pe.wait_ge(zc_evac, cc + 1)
                for f, a in fa:
                    last = mm(ps[a:a + HD, 5, HD * f:HD * f + HD], chk[s_XT][a:a + HD, f, cc, :],
                              Zs[a:a + HD, HD * f:HD * f + HD], start=True, stop=True, skip_group_check=True)
                last.then_inc(sa_done, 1)
                pe.wait_ge(sa_evac, cc + 1)
                sa = SAs[:, cc % 2, :]
                if cc < NCH - 1:
                    for f, a in fa:
                        mm(ps[a:a + HD, 6, HD * f:HD * f + HD], tok[s_Bt][a:a + HD, cc, f, :],
                           sa[a:a + HD, HD * f:HD * f + HD], start=True, stop=False, skip_group_check=True)
                        last = mm(ps[a:a + HD, 6, HD * f:HD * f + HD], tok[s_Kt][a:a + HD, cc, f, :],
                                  tok[s_Vt][a:a + HD, cc, f, :], start=False, stop=True, skip_group_check=True)
                    last.then_inc(st_done, 1)
                yb = 7 if cc % 2 else 3
                if cc >= 2:
                    pe.wait_ge(yc_evac, cc - 1)
                elif cc == 1:
                    pass
                if cc == 0:
                    pe.wait_ge(hp_evac, 4)
                for f, a in fa:
                    o = ps[a:a + HD, yb, HD * f:HD * f + HD]
                    if cc:
                        mm(o, cur[a:a + HD, HD * f:HD * f + HD], AR[a:a + HD, f, cc, 1, :], start=True, stop=False, skip_group_check=True)
                    mm(o, sa[a:a + HD, HD * f:HD * f + HD], chk[s_Mrb][a:a + HD, f, cc, :], start=(cc == 0), stop=False, skip_group_check=True)
                    last = mm(o, tok[s_Vt][a:a + HD, cc, f, :], chk[s_Mrk][a:a + HD, f, cc, :], start=False, stop=True, skip_group_check=True)
                last.then_inc(yc_done, 1)
            pe.wait_ge(yc_evac, NCH)
            for f in range(FT):
                mm(ps[:, f, :], K("blk"), S4(s_y)[:, f, :], start=True, stop=True).then_inc(gn_sum, 1)
            pe.wait_ge(st_evac, NCH - 1)
            pe.wait_ge(zc_evac, NCH)
            for f in range(FT):
                pe.wait_ge(gn_sq, f + 1)
                mm(ps[:, 4 + f, :], K("blk"), S4(s_y2)[:, f, :], start=True, stop=True).then_inc(gn_sqsum, 1)

            def late_row(m):
                for hf in range(2):
                    j = 2 * m + hf
                    pe.wait_ge(lacc_ready, j + 1)
                    if m:
                        pe.wait_ge(lrow_ready, m)
                    mm(ps[:, 6 + hf, :], K("ones"), acc_l[:, hf, 0:512], start=True, stop=True).then_inc(lrow_done, 1)

            n = 0

            def mix(w, a, src, kt):
                nonlocal n
                for k in range(kt):
                    last = mm(ps[:, n % 4, :], w[:, k, a:a + P], src[:, k, :], start=(k == 0), stop=(k == kt - 1))
                last.then_inc(mix_done, 1)
                n += 1
                return last

            pe.wait_ge(yrw_mean, FT)
            arrived(pe, OSB)
            for f in range(KD):
                if f >= 4:
                    pe.wait_ge(osb_evac, f - 3)
                mix(chunk(OSB, 4, D), P * f, S4(s_q), FT)
            pe.wait_ge(osb_evac, 8)
            for f in range(KD):
                arrived(pe, GS0 + f // 4)
                if f >= 4:
                    pe.wait_ge(gate_evac, f - 3)
                mix(chunk(GS0 + f // 4, KD), P * (f % 4), hT, KD)
                if f == 5:
                    late_row(0)
            pe.wait_ge(yrw_ready, 1)
            arrived(pe, ORW)
            for f in range(KD):
                arrived(pe, GR0 + f // 4)
                if f < 2:
                    pe.wait_ge(gate_evac, 6 + 2 * f)
                    pe.wait_ge(gate_evac, 8)
                else:
                    pe.wait_ge(merged_ready, 8 + f - 1)
                mix(chunk(GR0 + f // 4, KD), P * (f % 4), hT, KD)
                mix(chunk(ORW, 4, D), P * f, S4(s_y), FT)
                if f in (1, 4):
                    late_row(1 + f // 4)
            late_row(3)
            def transposes_h2(t):
                pe.wait_ge(h2_ready, t + 1)
                if t:
                    pe.wait_ge(h2T_evac, t)
                for k in range(KD):
                    src = h2tok[:, t % 2, :].rearrange("p (q k) -> p k q", k=KD)[:, k, :]
                    last = tr(psf[:, 2048 + P * k:2048 + P * k + P], src, ident)
                last.then_inc(h2T_done, 1)

            pe.wait_ge(merged_ready, 16)
            arrived(pe, WO0)
            arrived(pe, WO1)
            for t in range(NT):
                bk = 2 * (t % 2)
                if t >= 2:
                    pe.wait_ge(rstd1, t - 1)
                for hf in range(2):
                    w = chunk(WO0 + hf, KD)
                    for k in range(KD):
                        last = mm(ps[:, bk + hf, :], merged[:, k, P * t:P * t + P], w[:, k, :], start=(k == 0), stop=(k == KD - 1))
                last.then_inc(y_done, 1)
                if t >= 1:
                    transposes_h2(t - 1)
            transposes_h2(NT - 1)
            pe.wait_ge(h2T_evac, NT)
            pe.wait_ge(rstd1, NT)
            for t in range(NT):
                for k in range(KD):
                    last = mm(ps[:, 0, 64 * t:64 * t + NG + E], hT[:, k, P * t:P * t + P], wr[:, k, :], start=(k == 0),
                              stop=(k == KD - 1), skip_group_check=True)
            last.then_inc(logit_done, 1)
            pe.wait_ge(oh_ready, 1)
            oh = rview(688, 128, 4)
            for t in range(NT):
                for q in range(t):
                    mm(ps[:, 1, E * t:E * t + E], K("ones"), oh[:, q, :], start=(q == 0), stop=False, skip_group_check=True)
                mm(ps[:, 1, E * t:E * t + E], K("before"), oh[:, t, :], start=(t == 0), stop=True, skip_group_check=True)
            for q in range(NT):
                last = mm(ps[:, 2, 0:E], K("ones"), oh[:, q, :], start=(q == 0), stop=(q == NT - 1))
            last.then_inc(rank_done, 1)
            pe.wait_ge(sel_ready, 1)
            for ch in range(2):
                ohr = rview(1168 + 256 * ch, 256, 4)
                for t in range(NT):
                    last = mm(ps[0:CAP, 3, 0:MAXB], ohr[:, t, :], selb[:, ch, t, :], start=(ch == 0 and t == 0),
                              stop=(ch == 1 and t == NT - 1))
            last.then_inc(idx_done, 1)
            pe.wait_ge(route_ready, 1)
            steps = pe.value_load(nblk_i[0:1, 0:1], min_val=E // 2, max_val=MAXB // 2)
            for u in range(2):
                pe.sem_inc(hg_done[u], 1)
                pe.sem_inc(yo_ready[u], 1)
            with pe.Fori(0, steps) as it:
                for u in range(2):
                    pe.wait_ge(hrow_in[u], it * 16 + 16)
                    pe.sem_inc(pe_pass, 1)
                    hv = hrow[0:CAP, u, :].rearrange("p (q k) -> p k q", k=KD)
                    for k in range(KD):
                        last = tr(ps[:, 0, CAP * k:CAP * k + CAP], hv[:, k, :], ident[0:CAP, 0:CAP])
                    last.then_inc(hg_done[u], 1)
                    pe.wait_ge(hg_ready[u], it + 1)
                    pe.wait_ge(w_in_sem[u][0], it * 16 + 16)
                    pe.wait_ge(w_in_sem[u][1], it * 16 + 16)
                    for k in range(KD):
                        for hf in range(2):
                            w2 = eset[u][:, 0:2, :].rearrange("p m (k n) -> p m k n", k=KD)
                            last = mm(ps[64 * hf:64 * hf + 64, 2 + u, :].rearrange("p (m n) -> p m n", m=2), hgT[:, u, k, :],
                                      w2[:, :, k, 256 * hf:256 * hf + 256], start=(k == 0), stop=(k == KD - 1))
                    last.then_inc(up_done[u], 1)
                    pe.wait_ge(hid_ready[u], it + 1)
                    for j in range(2):
                        last = tr(ps[:, 1, P * j:P * j + P], hid[:, u, P * j:P * j + P], ident)
                    last.then_inc(ht_done[u], 1)
                    pe.wait_ge(ht_ready[u], it + 1)
                    pe.wait_ge(w_in_sem[u][2], it * 16 + 16)
                    pe.wait_ge(yo_ready[u], it + 1)
                    wd = eset[u][:, 2, :].rearrange("p (k n) -> p k n", k=4)
                    hv2 = hidT[:, u, :].rearrange("p (j h s) -> p j h s", j=2, h=2)
                    for k in range(4):
                        for hf in range(2):
                            last = mm(ps[64 * hf:64 * hf + 64, 4 + u, :], hv2[:, k % 2, k // 2, :],
                                      wd[:, k, 512 * hf:512 * hf + 512], start=(k == 0), stop=(k == 3))
                    last.then_inc(down_done[u], 1)


_INS = ['x', 'c', 'w_mod', 'b_mod', 'norm_gains', 'w_in', 'gate_bias', 'shift_mu', 'w0', 'w_decay_up', 'a0',
        'w_iclr_up', 'w_gate_up', 'k_k', 'k_a', 'r_k', 'lnx_w', 'lnx_b', 'w_o_sb', 'w_o_rw', 'w_out',
        'w_group', 'w_router', 'w_up1', 'w_up3', 'w_down']


def kernel(**inputs):
    import concourse.bacc as bacc
    from concourse.bass_utils import run_bass_kernel_spmd

    nc = bacc.Bacc("TRN2", target_bir_lowering=False, num_devices=1)
    arrays, args = {}, []
    for name in _INS:
        a = np.ascontiguousarray(inputs[name])
        arrays[f"in_{name}"] = a
        args.append(nc.dram_tensor(f"in_{name}", a.shape, mybir.dt.from_np(a.dtype), kind="ExternalInput").ap())
    arrays["in_consts"] = constants()
    args.append(nc.dram_tensor("in_consts", (P, NCONST), F32, kind="ExternalInput").ap())
    args.append(nc.dram_tensor("out_0", (1, T, D), F32, kind="ExternalOutput").ap())
    build(nc, *args)
    r = run_bass_kernel_spmd(nc, [arrays], core_ids=[0])
    return r.results[0]["out_0"]
```

```python
from contextlib import ExitStack

import numpy as np

import concourse.bass as bass
from concourse import mybir

F32 = mybir.dt.float32
I32 = mybir.dt.int32
ALU = mybir.AluOpType
ACT = mybir.ActivationFunctionType
AX = mybir.AxisListType.X

P = 128
T = 512
D = 1024
KD = D // P
NT = T // P
W = 512
FT = W // P
HD = 64
NH = 8
C = 64
NCH = T // C
E = 32
EG = 8
NG = 4
DE = 512
CAP = 64
MAXB = 48
DECAY = float(np.exp(-0.5))
BIG = 1e30

COL_Q, COL_K, COL_V = 0, W, 2 * W
COL_RW = 3 * W
COL_LORA = COL_RW + 3 * W
N_LORA = 288
COL_GATE = COL_LORA + N_LORA

OFF = [0, 512, 1024, 896]
WID = [T - P * j for j in range(NT)]
ZW = 1280

_widths = [("ident", 128), ("ntri", 128), ("nones", 128), ("ones", 128), ("blk", 128), ("before", 128),
           ("strictU", 64), ("inclU", 64), ("eye", 64), ("lvlL", 6 * 64), ("lvlU", 6 * 64),
           ("iota64", 64), ("m64", 8), ("blk16", 16), ("tok", 4), ("eps", 4)]
CONST = {}
_at = 0
for _n, _w in _widths:
    CONST[_n] = (_at, _w)
    _at += _w
NCONST = _at

_rows = [("mu", 15), ("w0", 4), ("a0", 4), ("kk", 4), ("ka", 4), ("rk", 4), ("lnw", 4), ("lnb", 4), ("gb", 16),
         ("bl", 32), ("gl", 24)]
NROW = sum(w for _, w in _rows)
_pw = _rows + [("c", 8), ("bmod", 16), ("g0", 8), ("silc", 8), ("omka", 4), ("A1", 8), ("SH1", 8), ("ss", 16), ("rs", 16),
               ("modc", 32)]
PAR = {}
_at = 0
for _n, _w in _pw:
    PAR[_n] = (_at, _w)
    _at += _w
NPAR = _at


def constants():
    m = np.zeros((P, NCONST), np.float32)

    def put(name, v):
        a, w = CONST[name]
        m[:, a:a + w] = np.asarray(v, np.float32).reshape(P, w)

    p = np.arange(P)[:, None]
    q = np.arange(P)[None, :]
    put("ident", p == q)
    put("ntri", -(p >= q).astype(np.float32))
    put("nones", -np.ones((P, P)))
    put("ones", np.ones((P, P)))
    put("blk", (p // 64) == (q // 64))
    put("before", p < q)
    r = p % 64
    c = np.arange(64)[None, :]
    put("strictU", r < c)
    put("inclU", r <= c)
    put("eye", r == c)

    def level(k, t, s):
        return ((t >> (k + 1)) == (s >> (k + 1))) & (((t >> k) & 1) == 1) & (((s >> k) & 1) == 0)

    put("lvlL", np.concatenate([level(k, r, c) for k in range(6)], 1))
    put("lvlU", np.concatenate([level(k, c, r) for k in range(6)], 1))
    put("iota64", np.broadcast_to(c, (P, 64)))
    put("m64", np.broadcast_to(CAP * np.arange(8)[None, :], (P, 8)))
    put("blk16", np.broadcast_to(E + np.arange(16)[None, :], (P, 16)))
    put("tok", p + P * np.arange(4)[None, :])
    put("eps", np.broadcast_to(np.array([[1e-6, 64e-5, 1.0, 0.0]]), (P, 4)))
    return m


def build(nc, x, c, w_mod, b_mod, gains, w_in, gate_bias, shift_mu, w0, w_decay_up, a0, w_iclr_up, w_gate_up,
          k_k, k_a, r_k, lnx_w, lnx_b, w_o_sb, w_o_rw, w_out, w_group, w_router, w_up1, w_up3, w_down,
          consts, out):
    ctx = ExitStack()
    with ctx:
        def sb(name, shape, dt=F32):
            return ctx.enter_context(nc.sbuf_tensor(name, shape, dt))

        def sem(name):
            return ctx.enter_context(nc.semaphore(name))

        h2_dram = nc.dram_tensor("h2_rows", [T, D], F32, kind="Internal").ap()
        ye_dram = nc.dram_tensor("expert_rows", [MAXB * CAP, D], F32, kind="Internal").ap()

        cst = sb("cst", [P, NCONST])
        par = sb("par", [P, NPAR])
        wr = sb("wr", [P, KD, NG + E])
        hT = sb("hT", [P, KD, T])
        ring = sb("ring", [P, 3, 4096])
        arena = sb("arena", [P, 15, 2048])
        prow = sb("prow", [NROW, P])
        raw = sb("raw", [P, 2, T + 1])
        PC = sb("PC", [P, FT * NCH])
        ST = sb("ST", [P, 2, FT * HD])
        SDZ = sb("SDZ", [P, 2, FT * HD])
        SD, Zs = SDZ[:, 0, :], SDZ[:, 1, :]
        SAs = sb("SAs", [P, 2, FT * HD])
        rt = sb("rt", [P, 2048 // 4])
        routf = sb("routf", [P, 16])
        slots_i = sb("slots_i", [P, 8], I32)
        idx_i = sb("idx_i", [CAP, MAXB], I32)
        idx_now = sb("idx_now", [CAP, 2], I32)
        nblk_i = sb("nblk_i", [1, 20], I32)
        ps = ctx.enter_context(nc.psum_tensor("ps", [P, 8, 512], F32))
        psf = ps[:, :, :].rearrange("p b n -> p (b n)")

        def K(name):
            a, w = CONST[name]
            return cst[:, a:a + w]

        def V(name, i=None, n=1):
            a, w = PAR[name]
            return par[:, a:a + w] if i is None else par[:, a + i:a + i + n]

        def S(i, n=1):
            return arena[:, i:i + n, :].rearrange("p a b -> p (a b)")

        def S4(i):
            return arena[:, i, :].rearrange("p (f t) -> p f t", f=FT)

        eps_rms, eps_gn, one = K("eps")[:, 0:1], K("eps")[:, 1:2], K("eps")[:, 2:3]

        s_r, s_k, s_v = 0, 1, 10
        s_sig, s_cum, s_a, s_P, s_Pi = 3, 4, 5, 6, 7
        s_AR, s_lora, s_g = 8, 8, 13
        s_kk, s_kk2, s_Bh, s_Kh = 11, 12, 11, 12
        s_Vt, s_Bt, s_Kt = 0, 1, 4
        s_q, s_ka, s_va, s_scr = 2, 14, 6, 10
        s_B, s_Kd, s_bonus = 3, 7, 5
        s_MT, s_X, s_XT, s_Mak, s_Mrb, s_Mrk, s_W = 10, 11, 12, 14, 3, 7, 6
        s_H, s_y, s_y2 = 6, 10, 12
        s_orw = (11, 14)
        s_rows, s_x1 = 0, 3

        wlo = S(s_ka)[:, 0:3 * W].rearrange("p (a n) -> p a n", a=3)
        AR = S(s_AR, 2).rearrange("p (f c a t) -> p f c a t", f=FT, c=NCH, a=2)
        lora = S(s_lora, 1).rearrange("p (a t) -> p a t", a=4)
        tok = {i: arena[:, i, :].rearrange("p (c f d) -> p c f d", c=NCH, f=FT) for i in (s_Vt, s_Bt, s_Kt, s_H)}
        chk = {i: arena[:, i, :].rearrange("p (f c t) -> p f c t", f=FT, c=NCH)
               for i in (s_MT, s_X, s_XT, s_Mak, s_Mrb, s_Mrk, s_W, s_B, s_Kd)}
        eb = S(s_scr, 3)
        e_buf = [eb[:, 0:ZW], eb[:, ZW:2 * ZW]]
        sp_buf = [eb[:, 2 * ZW:3 * ZW], eb[:, 3 * ZW:4 * ZW]]
        merged = ring[:, 0, :].rearrange("p (k t) -> p k t", k=KD)
        rows = S(s_rows, 2).rearrange("p (m n) -> p m n", m=4)
        x1 = S(s_x1, 2).rearrange("p (t n) -> p t n", t=NT)
        xin, xn = x1, S(s_rows, 2).rearrange("p (t n) -> p t n", t=NT)
        acc_e = S(5, 1).rearrange("p (b n) -> p b n", b=2)
        acc_l = [raw[:, 0, 0:512], raw[:, 1, 0:512]] + [a[:, :, :].rearrange("p b n -> p (b n)") for a in (ST, SAs, SDZ)]
        acc_l += [rt[:, :], S(12, 1)[:, 1024:1536], S(12, 1)[:, 1536:2048]]
        DG = S(12, 1)[:, 0:1024].rearrange("p (b q n) -> p b q n", b=2, q=4)
        DG = [DG[:, 0], DG[:, 1]]
        ytok = S(2, 1).rearrange("p (b n) -> p b n", b=2)
        h2tok = S(10, 1).rearrange("p (b n) -> p b n", b=2)
        osb = raw[:, :, 1:T + 1]
        gates_rw = ring[:, 2, :].rearrange("p (k t) -> p k t", k=KD)
        gated = S(5, 1)[:, 0:1024].rearrange("p (b n) -> p b n", b=2)
        eset = [ring[:, :, :], S(5, 6).rearrange("p (m n) -> p m n", m=3)]
        hrow = S(11, 1).rearrange("p (b n) -> p b n", b=2)
        hgT = S(12, 1)[:, 0:1024].rearrange("p (b k s) -> p b k s", b=2, k=KD)
        yo = S(12, 1)[:, 1024:2048].rearrange("p (b n) -> p b n", b=2)
        sil = S(13, 1)[:, 0:512].rearrange("p (b n) -> p b n", b=2)
        hid = S(13, 1)[:, 512:1024].rearrange("p (b n) -> p b n", b=2)
        hidT = S(13, 1)[:, 1024:1536].rearrange("p (b n) -> p b n", b=2)
        rsc = S(12, 1)
        selb = S(13, 1)[:, 0:2 * NT * MAXB].rearrange("p (c t b) -> p c t b", c=2, t=NT)
        ovb = S(13, 1)[:, 512:1024].rearrange("p (m e) -> p m e", e=E)

        def rview(a, n, t):
            return rsc[:, a:a + n].rearrange("p (t n) -> p t n", t=t)

        fin = [S(5, 2).rearrange("p (a n) -> p a n", a=4), S(7, 2).rearrange("p (a n) -> p a n", a=4)]

        prow_zero, rows_in, rows_turned = sem("prow_zero"), sem("rows_in"), sem("rows_turned")
        consts_in, params_in, lora_in, x_in = sem("consts_in"), sem("params_in"), sem("lora_in"), sem("x_in")
        ring_in = [sem(f"ring_in{i}") for i in range(6)]
        dve_chunk = sem("dve_chunk")
        act_link, dve_link, pool_link = sem("act_link"), sem("dve_link"), sem("pool_link")
        acc_ready, modcol_done, modcol_ready = sem("acc_ready"), sem("modcol_done"), sem("modcol_ready")
        rstd0, xn_ready, xT_done, xT_evac = sem("rstd0"), sem("xn_ready"), sem("xT_done"), sem("xT_evac")
        pa_done, pa_evac, shifted = sem("pa_done"), sem("pa_evac"), sem("shifted")
        lora_act = sem("lora_act")
        cum_ready, exps_ready = sem("cum_ready"), sem("exps_ready")
        kk2_ready, pd_done, kk_max, rn_ready, bonus_in, bonus_ready = (sem(n) for n in (
            "kk2_ready", "pd_done", "kk_max", "rn_ready", "bonus_in", "bonus_ready"))
        tok_src, tr_done, tr_act, tr_dve = sem("tok_src"), sem("tr_done"), sem("tr_act"), sem("tr_dve")
        z_done, log_ready, sp_ready, sp_masked, cum_done, att_ready, att_masked, av_all, ysb_ready = (
            sem(n) for n in ("z_done", "log_ready", "sp_ready", "sp_masked", "cum_done", "att_ready",
                             "att_masked", "av_all", "ysb_ready"))
        gram_done, gram_evac, invw_done, invw_evac, invx_done, invx_evac, invt_done, invt_evac = (sem(n) for n in (
            "gram_done", "gram_evac", "invw_done", "invw_evac", "invx_done", "invx_evac", "invt_done", "invt_evac"))
        hp_done, hp_evac, zc_done, zc_evac, sa_done, sa_evac, st_done, st_evac, yc_done, yc_evac = (sem(n) for n in (
            "hp_done", "hp_evac", "zc_done", "zc_evac", "sa_done", "sa_evac", "st_done", "st_evac", "yc_done", "yc_evac"))
        gn_in, gn_sum, gn_sq, gn_sqsum, gn_rstd, yrw_ready, yrw_mean = (sem(n) for n in (
            "gn_in", "gn_sum", "gn_sq", "gn_sqsum", "gn_rstd", "yrw_ready", "yrw_mean"))
        orw_in, gs_evac, gs_ready, sb_gated = sem("orw_in"), sem("gs_evac"), sem("gs_ready"), sem("sb_gated")
        mix_done, osb_evac, gr_evac, merged_ready = sem("mix_done"), sem("osb_evac"), sem("gr_evac"), sem("merged_ready")
        lacc_ready, lcol_done, lcol_evac, diag_ready, lrow_done, lrow_ready = (sem(n) for n in (
            "lacc_ready", "lcol_done", "lcol_evac", "diag_ready", "lrow_done", "lrow_ready"))
        pe_pass, pool_pass = sem("pe_pass"), sem("pool_pass")
        zero_tile, zero_stored = sem("zero_tile"), sem("zero_stored")
        x_again = sem("x_again")
        y_done, y_evac, rstd1, x1_ready, rstd2, h2_ready, h2T_done, h2T_evac = (sem(n) for n in (
            "y_done", "y_evac", "rstd1", "x1_ready", "rstd2", "h2_ready", "h2T_done", "h2T_evac"))
        h2_stored = [sem("h2_stored0"), sem("h2_stored1")]
        logit_done, gsum_in, gsum_ready, oh_ready, rank_done, sel_ready, idx_done, route_ready = (sem(n) for n in (
            "logit_done", "gsum_in", "gsum_ready", "oh_ready", "rank_done", "sel_ready", "idx_done", "route_ready"))
        w_in_sem = [[sem(f"expert_w{m}_in{u}") for m in range(3)] for u in range(2)]
        hrow_in = [sem("hrow_in0"), sem("hrow_in1")]
        hg_done = [sem("hg_done0"), sem("hg_done1")]
        hg_ready = [sem("hg_ready0"), sem("hg_ready1")]
        up_done = [sem("up_done0"), sem("up_done1")]
        sil_ready = [sem("sil_ready0"), sem("sil_ready1")]
        hid_ready = [sem("hid_ready0"), sem("hid_ready1")]
        ht_done = [sem("ht_done0"), sem("ht_done1")]
        ht_ready = [sem("ht_ready0"), sem("ht_ready1")]
        down_done = [sem("down_done0"), sem("down_done1")]
        yo_ready = [sem("yo_ready0"), sem("yo_ready1")]
        yo_stored = [sem("yo_stored0"), sem("yo_stored1")]
        pick_in = [sem("pick_in0"), sem("pick_in1")]
        pick_used, fin_ss, fin_rstd, fin_ready = (sem(n) for n in (
            "pick_used", "fin_ss", "fin_rstd", "fin_ready"))
        out_stored = [sem("out_stored0"), sem("out_stored1")]

        N_SMALL = 4
        FILL_ATT = 4
        LATE_BANK = (2, 3, 4, 5, 2, 3, 2, 3)
        HP_BANK = (0, 1, 6, 7)
        wv = w_in.rearrange("o (p k) n -> p (o k) n", k=KD)
        mv = w_mod.rearrange("o (p k) n -> p (o k) n", k=KD)

        def win(a, n):
            return wv[:, :, a:a + n], KD * n

        mod = [(mv[:, :, 512 * j:512 * j + 512], 4096) for j in range(12)]
        wo = w_out.rearrange("o (k p) n -> p (o k) n", p=P)
        gate_q = [win(COL_GATE + 256 * j, 256) for j in range(8)]
        chunk_table = [(f"MOD{j}", *mod[j], j % 3) for j in range(4)]
        chunk_table += [("LORA", *win(COL_LORA, N_LORA), 1), ("CK", *win(COL_RW + W, W), 2), ("CR", *win(COL_RW, W), 0),
                        ("CV", *win(COL_RW + 2 * W, W), 1), ("AQ", *win(COL_Q, W), 2), ("AK", *win(COL_K, W), 0),
                        ("AV", *win(COL_V, W), 1),
                        ("MOD4", *mod[4], 2), ("GS0", *gate_q[0], 3), ("GS1", *gate_q[1], 4), ("MOD5", *mod[5], 2),
                        ("MOD6", *mod[6], 2), ("GS2", *gate_q[2], 3), ("MOD7", *mod[7], 2), ("MOD8", *mod[8], 2),
                        ("GS3", *gate_q[3], 4), ("MOD9", *mod[9], 2), ("MOD10", *mod[10], 2), ("MOD11", *mod[11], 2),
                        ("OSB", w_o_sb.rearrange("o (k p) n -> p (o k) n", p=P), 4096, 1),
                        ("GR0", *gate_q[4], 3), ("GR1", *gate_q[5], 4), ("GR2", *gate_q[6], 3), ("GR3", *gate_q[7], 4),
                        ("WO0", wo[:, :, 0:512], 4096, 1), ("WO1", wo[:, :, 512:1024], 4096, 5)]
        chunk_names = [c_[0] for c_ in chunk_table]
        slot_of = [c_[3] for c_ in chunk_table]
        before = {}
        for n, sl in enumerate(slot_of):
            shared = {1: (1, 3, 4), 3: (1, 3), 4: (1, 4)}.get(sl, (sl,))
            before[n] = max([i for i in range(n) if slot_of[i] in shared], default=None)
        orw = [S(i, 1).rearrange("p (k n) -> p k n", k=2) for i in s_orw]

        def used_by(n):
            name = chunk_names[n]
            if name.startswith("MOD"):
                return dve_chunk, int(name[3:]) + 1
            return {"LORA": (pa_done, 3), "CK": (pa_done, 7), "CR": (pa_done, 11), "CV": (pa_done, 15), "AQ": (pa_done, 31),
                    "AK": (pa_done, 35), "AV": (pa_done, 39), "GS0": (mix_done, 2), "GS1": (mix_done, 4),
                    "GS2": (mix_done, 6), "GS3": (mix_done, 8), "OSB": (mix_done, 16), "GR0": (mix_done, 18),
                    "GR1": (mix_done, 20), "GR2": (mix_done, 22), "GR3": (mix_done, 24)}[name]

        def arrived(eng, name):
            n = chunk_names.index(name)
            eng.wait_ge(ring_in[slot_of[n]], 16 * slot_of[:n + 1].count(slot_of[n]))

        def ring_place(n):
            if slot_of[n] == 5:
                return S(6, 2)
            at = {3: 4096, 4: 4096 + 2048}.get(slot_of[n], 4096 * slot_of[n])
            return ring[:, :, :].rearrange("p s n -> p (s n)")[:, at:at + chunk_table[n][2]]

        def chunk(name, k):
            return ring_place(chunk_names.index(name)).rearrange("p (k n) -> p k n", k=k)

        up1 = w_up1.rearrange("o e (p k) n -> p (o e) (k n)", k=KD)
        up3 = w_up3.rearrange("o e (p k) n -> p (o e) (k n)", k=KD)
        dn = w_down.rearrange("o e (k p) n -> p (o e) k n", p=P)
        esrc = [up1, up3, dn]

        def load_expert(eng, u, m, e):
            dst = eset[u][:, m, :]
            if m < 2:
                src = esrc[m][:, bass.ds(e, 1), :].rearrange("p a n -> p (a n)")
            else:
                src = dn[:, bass.ds(e, 1), :, :].rearrange("p a k n -> p (a k) n")
                dst = dst.rearrange("p (k n) -> p k n", k=4)
            eng.dma_start(dst, src).then_inc(w_in_sem[u][m], 16)

        def load_orw(eng):
            eng.wait_ge(hp_done, 4)
            wsrc = w_o_rw.rearrange("o (k p) n -> p (o k) n", p=P)
            for i in range(2):
                eng.dma_start(orw[i], wsrc[:, 2 * i:2 * i + 2, :]).then_inc(orw_in, 16)

        block = ctx.enter_context(nc.Block())

        @block.sync
        def _(sp):
            for n, (name, src, width, sl) in enumerate(chunk_table):
                if before[n] is not None:
                    s, v = used_by(before[n])
                    sp.wait_ge(s, v)
                if name == "GR2":
                    load_orw(sp)
                if name == "WO1":
                    sp.wait_ge(yc_done, NCH)
                    sp.wait_ge(zc_evac, NCH)
                sp.dma_start(ring_place(n).rearrange("p (k n) -> p k n", k=src.shape[1]), src).then_inc(ring_in[sl], 16)
            sp.wait_ge(y_done, NT)
            for m in range(3):
                load_expert(sp, 0, m, 0)
            sp.wait_ge(h2T_done, NT)
            sp.wait_ge(h2_ready, NT)
            sp.wait_ge(h2_stored[0], 32)
            sp.wait_ge(h2_stored[1], 32)
            for m in range(3):
                load_expert(sp, 1, m, 1)
            with sp.Fori(1, E // 2) as it:
                for u in range(2):
                    sp.wait_ge(up_done[u], it)
                    load_expert(sp, u, 0, 2 * it + u)
                    load_expert(sp, u, 1, 2 * it + u)
                    sp.wait_ge(down_done[u], it)
                    load_expert(sp, u, 2, 2 * it + u)
            sp.wait_ge(route_ready, 1)
            n_over = sp.value_load(nblk_i[0:1, 1:2], min_val=0, max_val=8)
            with sp.If(n_over > 0):
                with sp.Fori(0, n_over) as it:
                    for u in range(2):
                        e = sp.value_load(nblk_i[0:1, bass.ds(2 * it + 2 + u, 1)], min_val=0, max_val=E - 1)
                        sp.wait_ge(up_done[u], it + E // 2)
                        load_expert(sp, u, 0, e)
                        load_expert(sp, u, 1, e)
                        sp.wait_ge(down_done[u], it + E // 2)
                        load_expert(sp, u, 2, e)
            with sp.Else():
                sp.nop()
            sp.nop()
            for t in range(NT):
                sp.wait_ge(fin_ready, t + 1)
                sp.dma_start(out[0, P * t:P * t + P, :], fin[t % 2][:, 2, :]).then_inc(out_stored[t % 2], 16)
            sp.wait_ge(out_stored[0], 32)
            sp.wait_ge(out_stored[1], 32)

        @block.gpsimd
        def _(pool):
            nc.gpsimd.memset(S(10), 0.0).then_inc(zero_tile, 1)
            pool.wait_ge(zero_tile, 1)
            over = ye_dram[E * CAP:MAXB * CAP, :].rearrange("(p r) n -> p (r n)", p=P)
            for q in range(4):
                pool.dma_start(over[:, 2048 * q:2048 * q + 2048], S(10)).then_inc(zero_stored, 16)

            def diag(buf, ready):
                for j in range(NT):
                    v = buf[:, OFF[j]:OFF[j] + P]
                    last = nc.gpsimd.affine_select(out=v, in_=v, compare_op=ALU.is_gt, fill=0.0, base=0,
                                                   pattern=[[1, P]], channel_multiplier=-1)
                last.then_inc(ready, 1)

            for h in range(NH + 1):
                if h < NH:
                    pool.wait_ge(sp_ready, h + 1)
                    diag(sp_buf[h % 2], sp_masked)
                if h >= 1:
                    pool.wait_ge(att_ready, h)
                    diag(e_buf[(h - 1) % 2], att_masked)
            pool.wait_ge(gs_ready, 1)
            for n in range(KD):
                pool.wait_ge(osb_evac, n + 1)
                nc.gpsimd.tensor_tensor(merged[:, n, :], merged[:, n, :], osb[:, n % 2, :], ALU.mult).then_inc(sb_gated, 1)
            pool.wait_ge(route_ready, 1)
            pool.wait_ge(h2_stored[0], 32)
            pool.wait_ge(h2_stored[1], 32)
            steps = pool.value_load(nblk_i[0:1, 0:1], min_val=E // 2, max_val=MAXB // 2)
            with pool.Fori(0, steps) as it:
                for u in range(2):
                    pool.wait_ge(hg_done[u], it + 1)
                    nc.gpsimd.tensor_copy(idx_now[:, u:u + 1], idx_i[:, bass.ds(2 * it + u, 1)]).then_inc(pool_link, 1)
                    pool.wait_ge(pool_link, 2 * it + u + 1)
                    pool.sem_inc(pool_pass, 1)
                    nc.gpsimd.indirect_dma_start(
                        out=hrow[0:CAP, u, :], out_offset=None, in_=h2_dram,
                        in_offset=bass.IndirectOffsetOnAxis(ap=idx_now[:, u:u + 1], axis=0)).then_inc(hrow_in[u], 16)
            for u in range(2):
                pool.wait_ge(yo_stored[u], steps * 32 + 32)
                pool.sem_inc(pool_pass, 1)
            for t in range(NT):
                if t >= 2:
                    pool.wait_ge(pick_used, t - 1)
                for ch in range(2):
                    nc.gpsimd.indirect_dma_start(
                        out=fin[t % 2][:, ch, :], out_offset=None, in_=ye_dram,
                        in_offset=bass.IndirectOffsetOnAxis(ap=slots_i[:, 2 * t + ch:2 * t + ch + 1], axis=0)
                    ).then_inc(pick_in[t % 2], 16)

        @block.scalar
        def _(act):
            links = [0]

            def link(ins):
                links[0] += 1
                ins.then_inc(act_link, 1)
                act.wait_ge(act_link, links[0])

            A = nc.scalar.activation
            act.dma_start(xin[:, :, :], x.rearrange("o (t p) n -> p (o t) n", p=P)).then_inc(x_in, 16)
            act.dma_start(cst[:, :], consts).then_inc(consts_in, 16)
            act.dma_start(V("c"), c.rearrange("o (p k) -> p (o k)", k=KD)).then_inc(params_in, 16)
            for m in range(2):
                act.dma_start(V("bmod", 8 * m, 8), b_mod[0:1, D * m:D * m + D].rearrange("o (p k) -> p (o k)", k=KD)).then_inc(params_in, 16)
            act.dma_start(V("g0"), gains[0, 0:1, :].rearrange("o (p k) -> p (o k)", k=KD)).then_inc(params_in, 16)
            act.wait_ge(prow_zero, 1)
            act.dma_start(prow[0:14, :], shift_mu[0:1, 0:1792].rearrange("o (f p) -> (o f) p", p=P)).then_inc(rows_in, 16)
            act.dma_start(prow[14:15, 0:32], shift_mu[0:1, 1792:1824]).then_inc(rows_in, 16)
            for name, src in (("w0", w0), ("a0", a0), ("kk", k_k), ("ka", k_a), ("lnw", lnx_w), ("lnb", lnx_b),
                              ("gb", gate_bias)):
                a, w = PAR[name]
                act.dma_start(prow[a:a + w, :], src.rearrange("o (f p) -> (o f) p", p=P)).then_inc(rows_in, 16)
            a, w = PAR["bl"]
            act.dma_start(prow[a:a + w, :], b_mod[0:1, 2 * D:].rearrange("o (f p) -> (o f) p", p=P)).then_inc(rows_in, 16)
            a, w = PAR["gl"]
            act.dma_start(prow[a:a + w, :], gains[0, 1:4, :].rearrange("g (f p) -> (g f) p", p=P)).then_inc(rows_in, 16)
            a, w = PAR["rk"]
            act.dma_start(prow[a:a + w, :], r_k.rearrange("o (f a) d -> (o f) (a d)", a=2)).then_inc(rows_in, 16)
            act.dma_start(wlo[0:64, 0, :], w_decay_up[0]).then_inc(lora_in, 16)
            act.dma_start(wlo[64:128, 0, :], w_iclr_up[0]).then_inc(lora_in, 16)
            act.dma_start(wlo[:, 1, :], w_gate_up[0, 0:128, :]).then_inc(lora_in, 16)
            act.dma_start(wlo[0:32, 2, :], w_gate_up[0, 128:160, :]).then_inc(lora_in, 16)
            act.dma_start(wr[:, :, 0:NG], w_group.rearrange("o (p k) n -> p (o k) n", k=KD)).then_inc(lora_in, 16)
            act.dma_start(wr[:, :, NG:], w_router.rearrange("o (p k) n -> p (o k) n", k=KD)).then_inc(lora_in, 16)
            act.wait_ge(params_in, 16 * N_SMALL)
            act.wait_ge(consts_in, 16)
            link(A(V("silc"), V("c"), ACT.Sigmoid))
            act.wait_ge(x_in, 16)
            for t in range(NT):
                link(A(xn[:, t, :], xin[:, t, :], ACT.Square, accum_out=V("ss", t)))
            link(A(V("ss", 0, 4), V("ss", 0, 4), ACT.Ln, scale=1.0 / D, bias=eps_rms))
            A(V("rs", 8, 4), V("ss", 0, 4), ACT.Exp, scale=-0.5).then_inc(rstd0, 1)
            act.wait_ge(modcol_ready, 1)
            for k in range(KD):
                act.wait_ge(xT_done, k + 1)
                A(hT[:, k, :], ps[:, k % 4, :], ACT.Identity, scale=V("A1", k), bias=V("SH1", k)).then_inc(xT_evac, 1)

            g = 0

            def evac(dst, func, **kw):
                nonlocal g
                act.wait_ge(pa_done, g + 1)
                bank = ps[:, g % 6, 0:T]
                ins = A(dst, bank[0:dst.shape[0], :], func, **kw)
                ins.then_inc(pa_evac, 1)
                g += 1
                return ins

            for n in range(15):
                if n >= 2:
                    act.wait_ge(shifted, n - 1)
                rows_ = 32 if n == 2 else P
                evac(raw[0:rows_, n % 2, 1:T + 1], ACT.Copy)
                if n == 4:
                    act.wait_ge(shifted, 3)
                    A(lora[0:64, 0, :], lora[0:64, 0, :], ACT.Tanh)
                    A(lora[:, 1, :], lora[:, 1, :], ACT.Sigmoid)
                    A(lora[0:32, 2, :], lora[0:32, 2, :], ACT.Sigmoid).then_inc(lora_act, 1)
            for f in range(FT):
                evac(S4(s_sig)[:, f, :], ACT.Sigmoid, bias=V("w0", f))
            for f in range(FT):
                evac(S4(s_a)[:, f, :], ACT.Sigmoid, bias=V("a0", f))
            for f in range(FT):
                evac(S4(s_g)[:, f, :], ACT.Copy)
            for f in range(FT):
                evac(S4(s_q)[:, f, :], ACT.Copy, scale=HD ** -0.5)
            act.wait_ge(cum_ready, 1)
            A(S(s_P), S(s_cum), ACT.Exp, scale=-DECAY)
            A(S(s_Pi), S(s_cum), ACT.Exp, scale=DECAY)
            A(S(s_sig), S(s_sig), ACT.Exp, scale=-DECAY).then_inc(exps_ready, 1)
            act.wait_ge(kk_max, FT)
            link(A(S(s_kk2), S(s_kk2), ACT.Ln))
            A(S(s_kk2), S(s_kk2), ACT.Exp, scale=-0.5).then_inc(rn_ready, 1)
            for f in range(FT):
                evac(S4(s_ka)[:, f, :], ACT.Copy)
            act.wait_ge(tok_src, 1)
            for t in range(NT):
                evac(S4(s_va)[:, t, :], ACT.Copy)
            for n in range(0, 3 * NCH, 2):
                act.wait_ge(tr_done, n + 1)
                cc, dst = n % NCH, tok[(s_Vt, s_Bt, s_Kt)[n // NCH]]
                src = ps[0:64, n % 6, :].rearrange("p (f d) -> p f d", f=FT)
                A(dst[0:64, cc, :, :], src[:, :, 0:64], ACT.Copy)
                A(dst[64:128, cc, :, :], src[:, :, 64:128], ACT.Copy).then_inc(tr_act, 1)

            nc.scalar.preload_act_table_set("natural_log_exp_and_others")
            for h in range(NH + 1):
                if h < NH:
                    act.wait_ge(z_done, h + 1)
                    if h >= 2:
                        act.wait_ge(av_all, h - 1)
                    link(A(e_buf[h % 2], psf[:, 1536 * (h % 2):1536 * (h % 2) + ZW], ACT.Abs))
                    link(A(e_buf[h % 2], e_buf[h % 2], ACT.Exp, scale=-1.0))
                    A(e_buf[h % 2], e_buf[h % 2], ACT.Ln, bias=one).then_inc(log_ready, 1)
                if h >= 1:
                    g_ = h - 1
                    act.wait_ge(cum_done, g_ + 1)
                    A(e_buf[g_ % 2], psf[:, 1536 * (g_ % 2):1536 * (g_ % 2) + ZW], ACT.Exp).then_inc(att_ready, 1)
                    act.wait_ge(mix_done, g_ + 1)
                    A(merged[:, g_, :], ps[:, 7, :], ACT.Identity, bias=V("gb", g_)).then_inc(gs_evac, 1)
                    if g_ % 2 == 1:
                        f = g_ // 2
                        act.wait_ge(av_all, 2 * f + 2)
                        A(S4(s_q)[:, f, :], ps[:, 6, :], ACT.Copy).then_inc(ysb_ready, 1)

            act.wait_ge(gs_evac, KD)
            A(merged[:, :, :], merged[:, :, :], ACT.Sigmoid).then_inc(gs_ready, 1)

            def w_out_of_psum(k, f):
                act.wait_ge(invw_done, FT * (k - 1) + f + 1)
                A(S4(s_W)[:, f, :], ps[:, f % 2, :], ACT.Copy).then_inc(invw_evac, 1)

            def xt_out_of_psum(k, f):
                act.wait_ge(invt_done, FT * (k - 1) + f + 1)
                src = psf[0:64, 6 * 512:8 * 512].rearrange("p (c a t) -> p c a t", c=NCH, a=2)
                A(chk[s_XT][0:64, f], src[:, :, 0, :], ACT.Copy)
                A(chk[s_XT][64:128, f], src[:, :, 1, :], ACT.Copy).then_inc(invt_evac, 1)

            def output_evac(n):
                act.wait_ge(mix_done, KD + n + 1)
                if n >= 2:
                    act.wait_ge(sb_gated, n - 1)
                A(osb[:, n % 2, :], ps[:, 2 + n % 2, :], ACT.Copy).then_inc(osb_evac, 1)

            for n in range(3):
                output_evac(n)
            for k in range(1, 6):
                w_out_of_psum(k, 0)
                if k > 1:
                    xt_out_of_psum(k - 1, 3)
                w_out_of_psum(k, 1)
                w_out_of_psum(k, 2)
                if k < 5:
                    xt_out_of_psum(k, 0)
                w_out_of_psum(k, 3)
                if k < 5:
                    xt_out_of_psum(k, 1)
                    xt_out_of_psum(k, 2)
                output_evac(k + 2)
            act.wait_ge(dve_chunk, 12)
            for b in range(4):
                act.wait_ge(hp_done, b + 1)
                A(S(s_H)[:, 512 * b:512 * b + 512], ps[:, HP_BANK[b], :], ACT.Copy).then_inc(hp_evac, 1)
            for cc in range(NCH):
                act.wait_ge(sa_done, cc + 1)
                if cc >= 2:
                    act.wait_ge(yc_done, cc - 1)
                A(SAs[:, cc % 2, :], ps[:, 5, 0:256], ACT.Copy).then_inc(sa_evac, 1)
                act.wait_ge(yc_done, cc + 1)
                A(S4(s_y)[:, :, C * cc:C * cc + C], ps[:, 7 if cc % 2 else 0, 0:256].rearrange("p (f t) -> p f t", f=FT),
                  ACT.Copy).then_inc(yc_evac, 1)
                act.wait_ge(mix_done, 2 * KD + cc + 1)
                A(gates_rw[:, cc, :], ps[:, 2 + cc % 2, :], ACT.Sigmoid, bias=V("gb", KD + cc)).then_inc(gr_evac, 1)
            act.dma_start(x1[:, :, :], x.rearrange("o (t p) n -> p (o t) n", p=P)).then_inc(x_again, 16)
            for f in range(FT):
                act.wait_ge(gn_sqsum, f + 1)
                link(A(S4(s_y2)[:, f, :], ps[:, 4 + f, :], ACT.Ln, scale=1.0 / HD, bias=eps_gn))
                A(S4(s_y2)[:, f, :], S4(s_y2)[:, f, :], ACT.Exp, scale=-0.5).then_inc(gn_rstd, 1)
            for m in range(4):
                for hf in range(2):
                    act.wait_ge(lrow_done, 2 * m + hf + 1)
                    A(rows[:, m, 512 * hf:512 * hf + 512], ps[:, 6 + hf, :], ACT.Copy).then_inc(lrow_ready, 1)
            for t in range(NT):
                act.wait_ge(y_done, t + 1)
                if t >= 2:
                    act.wait_ge(x1_ready, t - 1)
                bk = 2 * (t % 2)
                link(A(ytok[:, t % 2, :], psf[:, 512 * bk:512 * bk + D], ACT.Copy))
                link(A(psf[:, 512 * bk:512 * bk + D], ytok[:, t % 2, :], ACT.Square, accum_out=V("ss", 4 + t)))
                link(A(V("ss", 4 + t), V("ss", 4 + t), ACT.Ln, scale=1.0 / D, bias=eps_rms))
                A(V("rs", 4 + t), V("ss", 4 + t), ACT.Exp, scale=-0.5).then_inc(rstd1, 1)
                act.wait_ge(x1_ready, t + 1)
                link(A(ytok[:, t % 2, :], x1[:, t, :], ACT.Square, accum_out=V("ss", 8 + t)))
                link(A(V("ss", 8 + t), V("ss", 8 + t), ACT.Ln, scale=1.0 / D, bias=eps_rms))
                A(V("rs", 8 + t), V("ss", 8 + t), ACT.Exp, scale=-0.5).then_inc(rstd2, 1)
                act.wait_ge(h2_ready, t + 1)
                act.dma_start(h2_dram[P * t:P * t + P, :], h2tok[:, t % 2, :]).then_inc(h2_stored[t % 2], 16)
                act.wait_ge(h2T_done, t + 1)
                A(hT[:, :, P * t:P * t + P], psf[:, 2048:2048 + D].rearrange("p (k t) -> p k t", k=KD),
                  ACT.Copy).then_inc(h2T_evac, 1)
            act.wait_ge(gsum_in, 1)
            A(rt[:, 16:32], rt[:, 0:16], ACT.Exp)
            A(rt[:, 36:40], rt[:, 32:36], ACT.Exp).then_inc(gsum_ready, 1)
            act.wait_ge(route_ready, 1)
            nc.scalar.preload_act_table_set("silu_and_others")
            steps = act.value_load(nblk_i[0:1, 0:1], min_val=E // 2, max_val=MAXB // 2)
            for u in range(2):
                act.sem_inc(yo_stored[u], 32)
            with act.Fori(0, steps) as it:
                for u in range(2):
                    act.wait_ge(up_done[u], it + 1)
                    A(sil[:, u, :], ps[:, 2 + u, 0:256], ACT.Silu).then_inc(sil_ready[u], 1)
                    act.wait_ge(down_done[u], it + 1)
                    act.wait_ge(yo_stored[u], it * 32 + 32)
                    A(yo[:, u, :], ps[:, 4 + u, :], ACT.Copy).then_inc(yo_ready[u], 1)
                    act.wait_ge(yo_ready[u], it + 2)
                    for hf in range(2):
                        act.dma_start(ye_dram[bass.ds(it * (2 * CAP) + CAP * u, CAP), 512 * hf:512 * hf + 512],
                                      yo[64 * hf:64 * hf + 64, u, :]).then_inc(yo_stored[u], 16)
            for t in range(NT):
                act.wait_ge(fin_ss, t + 1)
                link(A(fin[t % 2][:, 3, :], fin[t % 2][:, 2, :], ACT.Square, accum_out=V("ss", 12 + t)))
                link(A(V("ss", 12 + t), V("ss", 12 + t), ACT.Ln, scale=1.0 / D, bias=eps_rms))
                A(V("rs", 12 + t), V("ss", 12 + t), ACT.Exp, scale=-0.5).then_inc(fin_rstd, 1)

        @block.vector
        def _(dve):
            links = [0]

            def link(ins):
                links[0] += 1
                ins.then_inc(dve_link, 1)
                dve.wait_ge(dve_link, links[0])

            TT, TS, STT, CP = (nc.vector.tensor_tensor, nc.vector.tensor_scalar, nc.vector.scalar_tensor_tensor,
                               nc.vector.tensor_copy)
            nc.vector.memset(prow[:, :], 0.0).then_inc(prow_zero, 1)
            dve.wait_ge(rows_turned, 1)
            link(CP(par[:, 0:NROW], ps[:, 6, 0:NROW]))
            dve.wait_ge(act_link, 1)
            link(TT(V("silc"), V("silc"), V("c"), ALU.mult))
            link(TS(V("omka"), V("ka"), -1.0, 1.0, ALU.mult, ALU.add))
            nc.vector.memset(raw[:, :, 0:1], 0.0)

            def modulation(acc, src_of, arrive, free, ready):
                arrive()
                for k in range(KD):
                    w = src_of[:, k, :]
                    if k == 0:
                        ins = TS(acc, w, V("silc", 0), None, ALU.mult)
                    else:
                        ins = STT(acc, w, V("silc", k), acc, ALU.mult, ALU.add)
                    if k < KD - 1:
                        link(ins)
                ins.then_inc(dve_link, 1)
                links[0] += 1
                dve.wait_ge(dve_link, links[0])
                nc.vector.engine_nop().then_inc(free, 1)
                if ready is not None:
                    nc.vector.engine_nop().then_inc(ready, 1)

            modulation(acc_e[:, 0, 0:512], chunk("MOD0", KD), lambda: arrived(dve, "MOD0"), dve_chunk, None)
            modulation(acc_e[:, 0, 512:1024], chunk("MOD1", KD), lambda: arrived(dve, "MOD1"), dve_chunk, acc_ready)
            dve.wait_ge(rstd0, 1)
            for t in range(NT):
                TS(xn[:, t, :], xin[:, t, :], V("rs", 8 + t), None, ALU.mult).then_inc(xn_ready, 1)
            modulation(acc_e[:, 1, 0:512], chunk("MOD2", KD), lambda: arrived(dve, "MOD2"), dve_chunk, None)
            modulation(acc_e[:, 1, 512:1024], chunk("MOD3", KD), lambda: arrived(dve, "MOD3"), dve_chunk, acc_ready)
            dve.wait_ge(modcol_done, 1)
            TT(V("SH1"), ps[:, 7, 0:8], V("bmod", 0, 8), ALU.add)
            link(TT(V("A1"), ps[:, 7, 8:16], V("bmod", 8, 8), ALU.add))
            STT(V("A1"), V("A1"), 1.0, V("g0"), ALU.add, ALU.mult).then_inc(modcol_ready, 1)

            order = [(12, lora[:, 0, :], P), (13, lora[:, 1, :], P), (14, lora[0:32, 2, :], 32)]
            order += [(4 + f, S4(s_k)[:, f, :], P) for f in range(FT)]
            order += [(f, S4(s_r)[:, f, :], P) for f in range(FT)]
            order += [(8 + f, S4(s_v)[:, f, :], P) for f in range(FT)]
            for n, (m, dst, r_) in enumerate(order):
                dve.wait_ge(pa_evac, n + 1)
                if n == 3:
                    dve.wait_ge(xT_done, KD)
                    dve.wait_ge(zero_stored, 64)
                b = raw[0:r_, n % 2, :]
                link(TT(dst, b[:, 0:T], b[:, 1:T + 1], ALU.subtract))
                STT(dst, dst, V("mu", m)[0:r_, :], b[:, 1:T + 1], ALU.mult, ALU.add).then_inc(shifted, 1)
            dve.wait_ge(shifted, 15)
            for f in range(FT):
                ins = TS(S4(s_kk)[:, f, :], S4(s_k)[:, f, :], V("kk", f), None, ALU.mult)
            link(ins)
            TT(S(s_kk2), S(s_kk), S(s_kk), ALU.mult).then_inc(kk2_ready, 1)
            for f in range(FT):
                dve.wait_ge(pa_evac, 15 + f + 1)
                for cc in range(NCH):
                    sl = slice(C * cc, C * cc + C)
                    ins = nc.vector.tensor_tensor_scan(S4(s_cum)[:, f, sl], K("ones")[:, 0:C], S4(s_sig)[:, f, sl], 0.0,
                                                       ALU.mult, ALU.add)
            link(ins)
            TT(S(s_sig), S(s_cum), S(s_sig), ALU.subtract).then_inc(cum_ready, 1)
            for f in range(FT):
                dve.wait_ge(pd_done, f + 1)
                TS(S4(s_kk2)[:, f, :], ps[:, 6 + f % 2, :], 1e-24, None, ALU.max).then_inc(kk_max, 1)
            dve.wait_ge(rn_ready, 1)
            dve.wait_ge(exps_ready, 1)
            dve.wait_ge(pa_evac, 15 + 2 * FT)
            link(TT(S(s_kk), S(s_kk), S(s_kk2), ALU.mult))
            link(TT(S(s_kk2), S(s_kk), S(s_a), ALU.mult))
            dve.wait_ge(pa_done, 15 + 3 * FT)
            ARv = S(s_AR, 2).rearrange("p (g a t) -> p g a t", a=2, t=C)
            P3 = lambda i: S(i).rearrange("p (g t) -> p g t", t=C)
            link(STT(ARv[:, :, 0, :], P3(s_kk), -1.0, P3(s_sig), ALU.mult, ALU.mult))
            link(TT(S(s_B), S(s_kk2), S(s_Pi), ALU.mult))
            for f in range(FT):
                ins = TS(S4(s_a)[:, f, :], S4(s_a)[:, f, :], V("ka", f), V("omka", f), ALU.mult, ALU.add)
            link(ins)
            link(TT(S(s_k), S(s_k), S(s_a), ALU.mult))
            for f in range(FT):
                ins = STT(S4(s_a)[:, f, :], S4(s_r)[:, f, :], V("rk", f), S4(s_k)[:, f, :], ALU.mult, ALU.mult)
            ins.then_inc(bonus_in, 1)
            TT(ARv[:, :, 1, :], P3(s_r), P3(s_P), ALU.mult)
            link(CP(PC[:, :], P3(s_P)[:, :, C - 1]))
            link(TT(S(s_Kd), S(s_k), S(s_Pi), ALU.mult))
            pcb = PC[:, :].rearrange("p (g o) -> p g o", o=1).broadcast_to((P, FT * NCH, C))
            TT(P3(s_Bh), P3(s_B), pcb, ALU.mult)
            TT(P3(s_Kh), P3(s_Kd), pcb, ALU.mult).then_inc(tok_src, 1)
            dve.wait_ge(bonus_in, 1)
            for f in range(FT):
                dve.wait_ge(pd_done, FT + f + 1)
                TT(S4(s_bonus)[:, f, :], ps[:, 6 + f % 2, :], S4(s_v)[:, f, :], ALU.mult).then_inc(bonus_ready, 1)
            for n in range(1, 3 * NCH, 2):
                dve.wait_ge(tr_done, n + 1)
                cc, dst = n % NCH, tok[(s_Vt, s_Bt, s_Kt)[n // NCH]]
                src = ps[0:64, n % 6, :].rearrange("p (f d) -> p f d", f=FT)
                CP(dst[0:64, cc, :, :], src[:, :, 0:64])
                CP(dst[64:128, cc, :, :], src[:, :, 64:128]).then_inc(tr_dve, 1)

            dve.wait_ge(tr_done, 3 * NCH)
            for h in range(NH):
                z = psf[:, 1536 * (h % 2):1536 * (h % 2) + ZW]
                dve.wait_ge(log_ready, h + 1)
                STT(sp_buf[h % 2], z, 0.0, e_buf[h % 2], ALU.max, ALU.add).then_inc(sp_ready, 1)
                modulation(acc_l[h], chunk(f"MOD{4 + h}", KD), lambda: arrived(dve, f"MOD{4 + h}"), dve_chunk, lacc_ready)
            modc = V("modc", 0, 32)
            own = eb[:, 0:2048].rearrange("p (j q n) -> p j q n", j=4, q=4)
            dve.wait_ge(av_all, NH)
            for j in range(NH):
                dve.wait_ge(lcol_done, j + 1)
                TT(own[:, j % 4], ps[:, LATE_BANK[j], :].rearrange("p (q n) -> p q n", q=4),
                   K("ident").rearrange("p (o n) -> p o n", o=1).broadcast_to((P, 4, P)), ALU.mult).then_inc(lcol_evac, 1)
                dve.wait_ge(lcol_evac, j + 1)
                ins = nc.vector.tensor_reduce(modc[:, 4 * j:4 * j + 4].rearrange("p (q o) -> p q o", o=1), own[:, j % 4], AX, ALU.add)
            link(ins)
            link(TT(modc, modc, V("bl", 0, 32), ALU.add))
            for m, (plus, gi) in enumerate(((0.0, 0), (0.0, None), (1.0, 1), (0.0, 2))):
                if gi is not None:
                    ins = STT(V("modc", 8 * m, 8), V("modc", 8 * m, 8), plus, V("gl", 8 * gi, 8), ALU.add, ALU.mult)
            link(ins)

            dve.wait_ge(av_all, NH)
            eyeb = K("eye").rearrange("p (o t) -> p o t", o=1).broadcast_to((P, FT * NCH, C))
            CP(P3(s_X), eyeb)
            link(CP(P3(s_XT), eyeb))

            def mk(name, k=0):
                return K(name)[:, 64 * k:64 * k + 64].rearrange("p (o t) -> p o t", o=1).broadcast_to((P, NCH, C))

            for f in range(FT):
                BA = psf[:, 0:1024].rearrange("p (c a t) -> p c a t", c=NCH, a=2)
                KA = psf[:, 3072:4096].rearrange("p (c a t) -> p c a t", c=NCH, a=2)
                MM = ps[:, 4 + f % 2, :].rearrange("p (c t) -> p c t", c=NCH)
                dve.wait_ge(gram_done, 3 * f + 1)
                TT(chk[s_MT][:, f], BA[:, :, 0, :], mk("strictU"), ALU.mult)
                nc.vector.copy_predicated(chk[s_XT][:, f], mk("lvlU").bitcast(I32), BA[:, :, 0, :])
                dve.wait_ge(gram_done, 3 * f + 2)
                TT(chk[s_Mrb][:, f], BA[:, :, 1, :], mk("inclU"), ALU.mult).then_inc(gram_evac, 1)
                nc.vector.copy_predicated(chk[s_X][:, f], mk("lvlL").bitcast(I32), MM).then_inc(gram_evac, 1)
                dve.wait_ge(gram_done, 3 * f + 3)
                TT(chk[s_Mak][:, f], KA[:, :, 0, :], mk("strictU"), ALU.mult)
                TT(chk[s_Mrk][:, f], KA[:, :, 1, :], mk("inclU"), ALU.mult).then_inc(gram_evac, 1)
            for k in range(1, 6):
                for f in range(FT):
                    n = FT * (k - 1) + f
                    dve.wait_ge(invx_done, n + 1)
                    X_new = ps[:, 4 + f % 2, :].rearrange("p (c t) -> p c t", c=NCH)
                    if k < 5:
                        nc.vector.copy_predicated(chk[s_X][:, f], mk("lvlL", k).bitcast(I32), X_new).then_inc(invx_evac, 1)
                    else:
                        nc.vector.copy_predicated(chk[s_XT][:, f], mk("lvlU", k).bitcast(I32), X_new).then_inc(invx_evac, 1)
            PCv = PC[:, :].rearrange("p (f c) -> p f c", c=NCH)
            f4 = lambda a: a.rearrange("p (f v) -> p f v", f=FT)
            for cc in range(NCH):
                if cc == 0:
                    dve.wait_ge(hp_evac, 4)
                    CP(Zs[:, :], tok[s_H][:, 0, :, :].rearrange("p f v -> p (f v)")).then_inc(zc_evac, 1)
                else:
                    dve.wait_ge(zc_done, cc)
                    dve.wait_ge(sa_done, cc)
                    TT(Zs[:, :], ps[:, 4, 0:256], tok[s_H][:, cc, :, :].rearrange("p f v -> p (f v)"), ALU.add).then_inc(zc_evac, 1)
                if cc < NCH - 1:
                    if cc == 0:
                        dve.wait_ge(st_done, 1)
                        CP(ST[:, 1, :], ps[:, 6, 0:256]).then_inc(st_evac, 1)
                    else:
                        dve.wait_ge(st_evac, cc)
                        pc1 = PCv[:, :, cc:cc + 1].broadcast_to((P, FT, HD))
                        link(TT(f4(SD[:, :]), f4(ST[:, cc % 2, :]), pc1, ALU.mult))
                        dve.wait_ge(st_done, cc + 1)
                        dve.wait_ge(yc_done, cc)
                        TT(ST[:, (cc + 1) % 2, :], SD[:, :], ps[:, 6, 0:256], ALU.add).then_inc(st_evac, 1)
            for f in range(FT):
                dve.wait_ge(gn_sum, f + 1)
                STT(S4(s_y)[:, f, :], ps[:, f, :], -1.0 / HD, S4(s_y)[:, f, :], ALU.mult, ALU.add).then_inc(yrw_mean, 1)
                dve.wait_ge(yrw_mean, f + 1)
                TT(S4(s_y2)[:, f, :], S4(s_y)[:, f, :], S4(s_y)[:, f, :], ALU.mult).then_inc(gn_sq, 1)
            for f in range(FT):
                dve.wait_ge(gn_rstd, f + 1)
                y = S4(s_y)[:, f, :]
                link(TT(y, y, S4(s_y2)[:, f, :], ALU.mult))
                link(TS(y, y, V("lnw", f), V("lnb", f), ALU.mult, ALU.add))
                link(TT(y, y, S4(s_bonus)[:, f, :], ALU.add))
                ins = TT(y, y, S4(s_g)[:, f, :], ALU.mult)
            ins.then_inc(yrw_ready, 1)
            dve.wait_ge(yrw_ready, 1)
            def diagonals(m):
                for hf in range(2):
                    n = 2 * m + hf
                    if n >= 2:
                        dve.wait_ge(lrow_done, n - 1)
                    cols = V("modc", 8 * m + 4 * hf, 4).rearrange("p (q o) -> p q o", o=1).broadcast_to((P, 4, P))
                    TT(DG[n % 2], K("ident").rearrange("p (o n) -> p o n", o=1).broadcast_to((P, 4, P)), cols,
                       ALU.mult).then_inc(diag_ready, 1)

            dve.wait_ge(sb_gated, KD)
            dve.wait_ge(gr_evac, KD)
            for n in range(KD):
                dve.wait_ge(mix_done, 3 * KD + n + 1)
                link(TT(gated[:, n % 2, :], gates_rw[:, n, :], ps[:, n % 4, :], ALU.mult))
                TT(merged[:, n, :], merged[:, n, :], gated[:, n % 2, :], ALU.add).then_inc(merged_ready, 1)
                if n % 2 == 0:
                    diagonals(n // 2)
            dve.wait_ge(lrow_ready, 8)
            dve.wait_ge(x_again, 16)
            for t in range(NT):
                dve.wait_ge(rstd1, t + 1)
                y = ytok[:, t % 2, :]
                link(STT(y, y, V("rs", 4 + t), rows[:, 0, :], ALU.mult, ALU.mult))
                TT(x1[:, t, :], x1[:, t, :], y, ALU.add).then_inc(x1_ready, 1)
                dve.wait_ge(rstd2, t + 1)
                if t >= 2:
                    dve.wait_ge(h2_stored[t % 2], 16)
                    dve.wait_ge(h2T_done, t - 1)
                hh = h2tok[:, t % 2, :]
                link(STT(hh, x1[:, t, :], V("rs", 8 + t), rows[:, 2, :], ALU.mult, ALU.mult))
                TT(hh, hh, rows[:, 1, :], ALU.add).then_inc(h2_ready, 1)
            R = rview
            gl, el = R(0, 16, 4), R(16, 128, 4)
            dve.wait_ge(logit_done, 1)
            lg = psf[:, 0:4 * 64].rearrange("p (t n) -> p t n", t=NT)
            CP(gl, lg[:, :, 0:NG])
            link(CP(el, lg[:, :, NG:NG + E]))
            gmax = rt[:, 40:44].rearrange("p (t o) -> p t o", o=1)
            bc = lambda a, n: a.broadcast_to((P, NT, n))
            io = K("iota64").rearrange("p (o n) -> p o n", o=1)
            o1 = lambda a: a.rearrange("p (t o) -> p t o", o=1)
            link(nc.vector.tensor_reduce(gmax, gl, AX, ALU.max))
            link(TT(rt[:, 0:16].rearrange("p (t n) -> p t n", t=NT), gl, bc(gmax, NG), ALU.subtract))

            def first_max(vals, n, mx, oh, tmp, idx):
                link(nc.vector.tensor_reduce(mx, vals, AX, ALU.max))
                link(TT(tmp, vals, bc(mx, n), ALU.is_lt))
                link(STT(tmp, tmp, 64.0, io[:, :, 0:n].broadcast_to((P, NT, n)), ALU.mult, ALU.add))
                link(nc.vector.tensor_reduce(idx, tmp, AX, ALU.min))
                link(TT(oh, io[:, :, 0:n].broadcast_to((P, NT, n)), bc(idx, n), ALU.is_equal))

            ohg, tmg = R(144, 16, 4), R(160, 16, 4)
            i_g, m1, m2, i1, i2 = (o1(rt[:, a:a + 4]) for a in (44, 48, 52, 56, 60))
            first_max(gl, NG, gmax, ohg, tmg, i_g)
            ml, tme, oh1, oh2, oh = (R(a, 128, 4) for a in (176, 304, 432, 560, 688))
            g8 = lambda a: a.rearrange("p t (g e) -> p (t g) e", e=EG)
            og = R(144, 16, 16)
            link(TT(g8(ml), g8(el), og.broadcast_to((P, 16, EG)), ALU.mult))
            link(TS(R(144, 16, 4), ohg, 1.0, BIG, ALU.subtract, ALU.mult))
            link(TT(g8(ml), g8(ml), og.broadcast_to((P, 16, EG)), ALU.add))
            first_max(ml, E, m1, oh1, tme, i1)
            link(STT(tme, oh1, -2 * BIG, ml, ALU.mult, ALU.add))
            link(CP(ml, tme))
            first_max(ml, E, m2, oh2, tme, i2)
            link(TT(o1(rt[:, 32:36]), m2, m1, ALU.subtract))
            TT(oh, oh1, oh2, ALU.add).then_inc(gsum_in, 1)
            dve.wait_ge(gsum_in, 1)
            nc.vector.engine_nop().then_inc(oh_ready, 1)
            dve.wait_ge(gsum_ready, 1)
            gs = o1(rt[:, 64:68])
            link(nc.vector.tensor_reduce(gs, rt[:, 16:32].rearrange("p (t n) -> p t n", t=NT), AX, ALU.add))
            link(STT(rt[:, 68:72], rt[:, 36:40], 1.0, rt[:, 64:68], ALU.add, ALU.mult))
            link(nc.vector.reciprocal(routf[:, 0:4], rt[:, 68:72]))
            link(TT(routf[:, 4:8], routf[:, 0:4], rt[:, 36:40], ALU.mult))
            dve.wait_ge(rank_done, 1)
            rk_all = R(816, 128, 4)
            link(CP(rk_all, ps[:, 1, 0:128].rearrange("p (t e) -> p t e", t=NT)))
            cnt, nov, ends, base = rt[:, 72:104], rt[:, 104:136], rt[:, 136:168], rt[:, 168:200]
            link(CP(cnt, ps[:, 2, 0:E]))
            cmp7 = R(944, 7 * E, 7)
            link(TT(cmp7, cnt.rearrange("p (o e) -> p o e", o=1).broadcast_to((P, 7, E)),
                    K("m64")[:, 1:8].rearrange("p (m o) -> p m o", o=1).broadcast_to((P, 7, E)), ALU.is_gt))
            link(nc.vector.tensor_reduce(nov.rearrange("p (e o) -> p e o", o=1), cmp7.rearrange("p m e -> p e m"), AX, ALU.add))
            link(nc.vector.tensor_tensor_scan(ends, K("ones")[:, 0:E], nov, float(E), ALU.mult, ALU.add))
            link(TT(base, ends, nov, ALU.subtract))
            for ch, (ohc, ic) in enumerate(((oh1, i1), (oh2, i2))):
                rk_, bs_, q_, blk_, t1, rr = (rt[:, 200 + 24 * ch + 4 * a:204 + 24 * ch + 4 * a] for a in range(6))
                link(TT(tme, rk_all, ohc, ALU.mult))
                link(nc.vector.tensor_reduce(o1(rk_), tme, AX, ALU.add))
                link(TT(tme, ohc, base.rearrange("p (o e) -> p o e", o=1).broadcast_to((P, NT, E)), ALU.mult))
                link(nc.vector.tensor_reduce(o1(bs_), tme, AX, ALU.add))
                c7 = R(944, 28, 4)
                link(TT(c7, o1(rk_).broadcast_to((P, NT, 7)),
                        K("m64")[:, 1:8].rearrange("p (o m) -> p o m", o=1).broadcast_to((P, NT, 7)), ALU.is_ge))
                link(nc.vector.tensor_reduce(o1(q_), c7, AX, ALU.add))
                link(STT(blk_, bs_, -1.0, q_, ALU.add, ALU.add))
                link(TT(blk_, blk_, ic.rearrange("p t o -> p (t o)"), ALU.subtract))
                link(TS(t1, q_, 0.0, None, ALU.is_gt))
                link(TT(blk_, blk_, t1, ALU.mult))
                link(TT(blk_, blk_, ic.rearrange("p t o -> p (t o)"), ALU.add))
                link(STT(rr, q_, -float(CAP), rk_, ALU.mult, ALU.add))
                link(STT(routf[:, 8:16].rearrange("p (t c) -> p c t", c=2)[:, ch, :], blk_, float(CAP), rr, ALU.mult, ALU.add))
                ohr = R(1168 + 256 * ch, 256, 4)
                link(TT(ohr, io[:, :, 0:CAP].broadcast_to((P, NT, CAP)), o1(rr).broadcast_to((P, NT, CAP)), ALU.is_equal))
                ohb = selb[:, ch]
                link(TT(ohb, io[:, :, 0:MAXB].broadcast_to((P, NT, MAXB)), o1(blk_).broadcast_to((P, NT, MAXB)), ALU.is_equal))
                link(TT(ohb, ohb, o1(K("tok")).broadcast_to((P, NT, MAXB)), ALU.mult))
            link(CP(slots_i[:, :], routf[:, 8:16]))
            nc.vector.engine_nop().then_inc(sel_ready, 1)
            ov = ovb
            b16 = K("blk16")[0:1, :].rearrange("p (m o) -> p m o", o=1).broadcast_to((1, 16, E))
            link(TT(ov[0:1], ends[0:1].rearrange("p (o e) -> p o e", o=1).broadcast_to((1, 16, E)), b16, ALU.is_le))
            link(nc.vector.tensor_reduce(rt[0:1, 260:276].rearrange("p (m o) -> p m o", o=1), ov[0:1], AX, ALU.add))
            link(TS(rt[0:1, 260:276], rt[0:1, 260:276], float(E - 1), None, ALU.min))
            link(CP(nblk_i[0:1, 2:18], rt[0:1, 260:276]))
            lt8 = rt[0:1, 276:284]
            link(TT(lt8, K("blk16")[0:1, 0:16:2], ends[0:1, E - 1:E].broadcast_to((1, 8)), ALU.is_lt))
            link(nc.vector.tensor_reduce(rt[0:1, 284:285], lt8, AX, ALU.add))
            link(CP(nblk_i[0:1, 1:2], rt[0:1, 284:285]))
            link(TS(nblk_i[0:1, 0:1], rt[0:1, 284:285], float(E // 2), None, ALU.add))
            dve.wait_ge(idx_done, 1)
            link(CP(idx_i[:, :], ps[0:CAP, 3, 0:MAXB]))
            nc.vector.engine_nop().then_inc(route_ready, 1)
            dve.wait_ge(route_ready, 1)
            steps = dve.value_load(nblk_i[0:1, 0:1], min_val=E // 2, max_val=MAXB // 2)
            with dve.Fori(0, steps) as it:
                for u in range(2):
                    dve.wait_ge(hg_done[u], it + 2)
                    CP(hgT[:, u, :, :].rearrange("p k s -> p (k s)"), ps[:, 0, :]).then_inc(hg_ready[u], 1)
                    dve.wait_ge(sil_ready[u], it + 1)
                    TT(hid[:, u, :], sil[:, u, :], ps[:, 2 + u, 256:512], ALU.mult).then_inc(hid_ready[u], 1)
                    dve.wait_ge(ht_done[u], it + 1)
                    CP(hidT[:, u, :], ps[:, 1, 0:256]).then_inc(ht_ready[u], 1)
            for t in range(NT):
                dve.wait_ge(pick_in[t % 2], 32 * (t // 2 + 1))
                if t >= 2:
                    dve.wait_ge(out_stored[t % 2], 16)
                b = fin[t % 2]
                link(TS(b[:, 2, :], b[:, 0, :], routf[:, t:t + 1], None, ALU.mult))
                STT(b[:, 2, :], b[:, 1, :], routf[:, 4 + t:5 + t], b[:, 2, :], ALU.mult, ALU.add).then_inc(fin_ss, 1)
                dve.wait_ge(fin_rstd, t + 1)
                link(STT(b[:, 2, :], b[:, 2, :], V("rs", 12 + t), rows[:, 3, :], ALU.mult, ALU.mult))
                nc.vector.tensor_tensor(b[:, 2, :], b[:, 2, :], x1[:, t, :], ALU.add).then_inc(fin_ready, 1)
                if t < NT - 1:
                    nc.vector.engine_nop().then_inc(pick_used, 1)

        @block.tensor
        def _(pe):
            mm, tr = nc.tensor.matmul, nc.tensor.transpose
            ident = K("ident")
            pe.wait_ge(consts_in, 16)
            pe.wait_ge(rows_in, 16 * 12)
            tr(ps[:, 6, 0:NROW], prow[:, :], ident[0:NROW, 0:NROW]).then_inc(rows_turned, 1)
            for m in range(2):
                pe.wait_ge(acc_ready, m + 1)
                a = acc_e[:, m, :].rearrange("p (q k) -> p k q", k=KD)
                for k in range(KD):
                    last = mm(ps[:, 7, 8 * m + k:8 * m + k + 1], a[:, k, :], K("ones")[:, 0:1], start=True, stop=True)
            last.then_inc(modcol_done, 1)
            pe.wait_ge(xn_ready, NT)
            for k in range(KD):
                if k >= 4:
                    pe.wait_ge(xT_evac, k - 3)
                for t in range(NT):
                    src = xn[:, t, :].rearrange("p (q k) -> p k q", k=KD)[:, k, :]
                    last = tr(ps[:, k % 4, P * t:P * t + P], src, ident)
                last.then_inc(xT_done, 1)
            pe.wait_ge(xT_evac, KD)

            g = 0

            def group():
                nonlocal g
                if g >= 6:
                    pe.wait_ge(pa_evac, g - 5)
                g += 1
                return (g - 1) % 6

            def project(name, tiles):
                w = chunk(name, KD)
                arrived(pe, name)
                for i, (a, m_) in enumerate(tiles):
                    b = group()
                    for k in range(KD):
                        last = mm(ps[0:m_, b, :], w[:, k, a:a + m_], hT[:, k, :], start=(k == 0), stop=(k == KD - 1))
                    last.then_inc(pa_done, 1)

            full = [(P * f, P) for f in range(FT)]
            project("LORA", [(0, P), (128, P), (256, 32)])
            project("CK", full)
            project("CR", full)
            project("CV", full)
            pe.wait_ge(lora_in, 16 * 6)
            pe.wait_ge(lora_act, 1)
            pe.wait_ge(shifted, 3)
            for f in range(FT):
                mm(ps[:, group(), :], wlo[0:64, 0, P * f:P * f + P], lora[0:64, 0, :], start=True, stop=True).then_inc(pa_done, 1)
            for f in range(FT):
                mm(ps[:, group(), :], wlo[64:128, 0, P * f:P * f + P], lora[64:128, 0, :], start=True, stop=True).then_inc(pa_done, 1)
            for f in range(FT):
                b = group()
                mm(ps[:, b, :], wlo[:, 1, P * f:P * f + P], lora[:, 1, :], start=True, stop=False)
                mm(ps[:, b, :], wlo[0:32, 2, P * f:P * f + P], lora[0:32, 2, :], start=False, stop=True).then_inc(pa_done, 1)
            project("AQ", full)
            pe.wait_ge(kk2_ready, 1)
            for f in range(FT):
                if f >= 2:
                    pe.wait_ge(kk_max, f - 1)
                mm(ps[:, 6 + f % 2, :], K("blk"), S4(s_kk2)[:, f, :], start=True, stop=True).then_inc(pd_done, 1)
            project("AK", full)
            pe.wait_ge(bonus_in, 1)
            for f in range(FT):
                if f >= 2:
                    pe.wait_ge(bonus_ready, f - 1)
                mm(ps[:, 6 + f % 2, :], K("blk"), S4(s_bonus)[:, f, :], start=True, stop=True).then_inc(pd_done, 1)
            arrived(pe, "AV")
            w = chunk("AV", KD)
            for t in range(NT):
                b = group()
                for k in range(KD):
                    last = mm(ps[:, b, :], hT[:, k, P * t:P * t + P], w[:, k, :], start=(k == 0), stop=(k == KD - 1))
                last.then_inc(pa_done, 1)
            pe.wait_ge(pa_evac, g)
            pe.wait_ge(tok_src, 1)
            pe.wait_ge(bonus_ready, FT)
            for n in range(3 * NCH):
                if n >= 6:
                    s = tr_act if n % 2 == 0 else tr_dve
                    pe.wait_ge(s, (n - 6) // 2 + 1)
                src = (s_v, s_Bh, s_Kh)[n // NCH]
                cc = n % NCH
                for f in range(FT):
                    last = tr(ps[0:64, n % 6, P * f:P * f + P], S4(src)[:, f, C * cc:C * cc + C], ident)
                last.then_inc(tr_done, 1)
            pe.wait_ge(tr_act, 12)
            pe.wait_ge(tr_dve, 12)

            def scores(h):
                f, a = h // 2, HD * (h % 2)
                if h >= 2:
                    pe.wait_ge(att_ready, h - 1)
                for j in (0, 1, 3, 2):
                    o = 1536 * (h % 2) + OFF[j]
                    last = mm(psf[:, o:o + WID[j]], S4(s_ka)[a:a + HD, f, P * j:P * j + P],
                              S4(s_q)[a:a + HD, f, P * j:T], start=(j != 3), stop=True, skip_group_check=True)
                last.then_inc(z_done, 1)

            def sums(h):
                pe.wait_ge(sp_masked, h + 1)
                sp = sp_buf[h % 2]
                for j in range(NT):
                    for jj in range(j, NT):
                        o = 1536 * (h % 2) + OFF[j] + P * (jj - j)
                        last = mm(psf[:, o:o + WID[jj]], K("ntri") if jj == j else K("nones"),
                                  sp[:, OFF[jj]:OFF[jj] + WID[jj]], start=False, stop=True, skip_group_check=True)
                last.then_inc(cum_done, 1)

            def values(h):
                f, a = h // 2, HD * (h % 2)
                if h % 2 == 0 and f >= 1:
                    pe.wait_ge(ysb_ready, f)
                pe.wait_ge(att_masked, h + 1)
                for j in range(NT):
                    last = mm(ps[a:a + HD, 6, P * j:T], S4(s_va)[:, j, HD * h:HD * h + HD],
                              e_buf[h % 2][:, OFF[j]:OFF[j] + WID[j]], start=(j == 0), stop=(j == NT - 1),
                              skip_group_check=True)
                last.then_inc(av_all, 1)

            def gate(branch, n, ks, bank):
                if ks[0] == 0:
                    arrived(pe, f"{branch}{n // 2}")
                    if branch == "GS" and n:
                        pe.wait_ge(gs_evac, n)
                    if branch == "GR" and n >= 2:
                        pe.wait_ge(gr_evac, n - 1)
                w = chunk(f"{branch}{n // 2}", KD)
                for k in ks:
                    last = mm(ps[:, bank, :], w[:, k, P * (n % 2):P * (n % 2) + P], hT[:, k, :], start=(k == 0), stop=(k == KD - 1))
                if ks[-1] == KD - 1:
                    last.then_inc(mix_done, 1)

            def attention_output(n, ks):
                if ks[0] == 0:
                    arrived(pe, "OSB")
                    if n >= 2:
                        pe.wait_ge(osb_evac, n - 1)
                for k in ks:
                    last = mm(ps[:, 2 + n % 2, :], chunk("OSB", 4)[:, k, P * n:P * n + P], S4(s_q)[:, k, :], start=(k == 0),
                              stop=(k == FT - 1))
                if ks[-1] == FT - 1:
                    last.then_inc(mix_done, 1)

            scores(0)
            for h in range(NH):
                if h + 1 < NH:
                    scores(h + 1)
                first = FILL_ATT if h else 0
                if first:
                    gate("GS", h, range(first), 7)
                sums(h)
                gate("GS", h, range(first, KD), 7)
                values(h)
            pe.wait_ge(lacc_ready, NH)
            def late_sum(j):
                if j >= 4:
                    earlier = max(i for i in range(j) if LATE_BANK[i] == LATE_BANK[j])
                    pe.wait_ge(lcol_evac, earlier + 1)
                mm(ps[:, LATE_BANK[j], :], K("ones"), acc_l[j], start=True, stop=True).then_inc(lcol_done, 1)

            for j in range(6):
                late_sum(j)
            pe.wait_ge(ysb_ready, FT)

            for f in range(FT):
                def products(src, o):
                    for cc in range(NCH):
                        for a in (0, HD):
                            last = mm(psf[a:a + HD, o + P * cc:o + P * cc + P], chk[src][a:a + HD, f, cc, :],
                                      AR[a:a + HD, f, cc, :, :].rearrange("p a t -> p (a t)"), start=True, stop=True,
                                      skip_group_check=True)
                    last.then_inc(gram_done, 1)

                if f >= 1:
                    if f == 1:
                        pe.wait_ge(lcol_evac, NH)
                    attention_output(f - 1, range(FT))
                    pe.wait_ge(gram_evac, 3 * f - 1)
                products(s_B, 0)
                if f == 0:
                    late_sum(6)
                    late_sum(7)
                for cc in range(NCH):
                    for a in (0, HD):
                        last = mm(ps[a:a + HD, 4 + f % 2, C * cc:C * cc + C], AR[a:a + HD, f, cc, 0, :],
                                  chk[s_B][a:a + HD, f, cc, :], start=True, stop=True, skip_group_check=True)
                last.then_inc(gram_done, 1)
                if f >= 1:
                    pe.wait_ge(gram_evac, 3 * f)
                products(s_Kd, 3072)
            pe.wait_ge(gram_evac, 3 * FT)

            def tiles64(bank, lhs, rhs, f, sig):
                for cc in range(NCH):
                    for a in (0, HD):
                        last = mm(ps[a:a + HD, bank, C * cc:C * cc + C], chk[lhs][a:a + HD, f, cc, :],
                                  chk[rhs][a:a + HD, f, cc, :], start=True, stop=True, skip_group_check=True)
                last.then_inc(sig, 1)

            def w_product(k, f):
                n = FT * (k - 1) + f
                if k > 1:
                    pe.wait_ge(invx_evac, n - FT + 1)
                if n >= 2:
                    pe.wait_ge(invw_evac, n - 1)
                tiles64(f % 2, s_MT, s_X, f, invw_done)
                attention_output(k + 2, (f,))

            def x_product(k, f):
                n = FT * (k - 1) + f
                pe.wait_ge(invw_evac, n + 1)
                if k > 1:
                    pe.wait_ge(invt_evac, n - FT + 1)
                if n >= 2:
                    pe.wait_ge(invx_evac, n - 1)
                if k < 5:
                    tiles64(4 + f % 2, s_XT, s_W, f, invx_done)
                else:
                    tiles64(4 + f % 2, s_W, s_XT, f, invx_done)

            def x_transpose(k, f):
                n = FT * (k - 1) + f
                pe.wait_ge(invx_evac, n + 1)
                if n >= 1:
                    pe.wait_ge(invt_evac, n)
                for cc in range(NCH):
                    last = tr(psf[0:64, 6 * 512 + P * cc:6 * 512 + P * cc + P], chk[s_X][:, f, cc, :], ident)
                last.then_inc(invt_done, 1)

            for k in range(1, 6):
                w_product(k, 0)
                if k > 1:
                    x_transpose(k - 1, 3)
                w_product(k, 1)
                x_product(k, 0)
                w_product(k, 2)
                x_product(k, 1)
                if k < 5:
                    x_transpose(k, 0)
                w_product(k, 3)
                x_product(k, 2)
                if k < 5:
                    x_transpose(k, 1)
                x_product(k, 3)
                if k < 5:
                    x_transpose(k, 2)
            pe.wait_ge(invx_evac, 5 * FT)
            pe.wait_ge(osb_evac, KD)
            for b in range(4):
                for cc in (2 * b, 2 * b + 1):
                    for f in range(FT):
                        for a in (0, HD):
                            o = 256 * (cc % 2) + HD * f
                            last = mm(ps[a:a + HD, HP_BANK[b], o:o + HD], chk[s_Mak][a:a + HD, f, cc, :],
                                      tok[s_Vt][a:a + HD, cc, f, :], start=True, stop=True, skip_group_check=True)
                last.then_inc(hp_done, 1)
            fa = [(f, a) for f in range(FT) for a in (0, HD)]
            for cc in range(NCH):
                cur = ST[:, cc % 2, :]
                gate("GR", cc, (0, 1), 2 + cc % 2)
                if cc:
                    pe.wait_ge(st_evac, cc)
                    for f, a in fa:
                        last = mm(ps[a:a + HD, 4, HD * f:HD * f + HD], AR[a:a + HD, f, cc, 0, :],
                                  cur[a:a + HD, HD * f:HD * f + HD], start=True, stop=True, skip_group_check=True)
                    last.then_inc(zc_done, 1)
                gate("GR", cc, (2, 3, 4), 2 + cc % 2)
                pe.wait_ge(zc_evac, cc + 1)
                for f, a in fa:
                    last = mm(ps[a:a + HD, 5, HD * f:HD * f + HD], chk[s_XT][a:a + HD, f, cc, :],
                              Zs[a:a + HD, HD * f:HD * f + HD], start=True, stop=True, skip_group_check=True)
                last.then_inc(sa_done, 1)
                gate("GR", cc, (5, 6, 7), 2 + cc % 2)
                pe.wait_ge(sa_evac, cc + 1)
                sa = SAs[:, cc % 2, :]
                if cc < NCH - 1:
                    for f, a in fa:
                        mm(ps[a:a + HD, 6, HD * f:HD * f + HD], tok[s_Bt][a:a + HD, cc, f, :],
                           sa[a:a + HD, HD * f:HD * f + HD], start=True, stop=False, skip_group_check=True)
                        last = mm(ps[a:a + HD, 6, HD * f:HD * f + HD], tok[s_Kt][a:a + HD, cc, f, :],
                                  tok[s_Vt][a:a + HD, cc, f, :], start=False, stop=True, skip_group_check=True)
                    last.then_inc(st_done, 1)
                yb = 7 if cc % 2 else 0
                if cc >= 2:
                    pe.wait_ge(yc_evac, cc - 1)
                if cc == 0:
                    pe.wait_ge(hp_evac, 4)
                for f, a in fa:
                    o = ps[a:a + HD, yb, HD * f:HD * f + HD]
                    if cc:
                        mm(o, cur[a:a + HD, HD * f:HD * f + HD], AR[a:a + HD, f, cc, 1, :], start=True, stop=False, skip_group_check=True)
                    mm(o, sa[a:a + HD, HD * f:HD * f + HD], chk[s_Mrb][a:a + HD, f, cc, :], start=(cc == 0), stop=False, skip_group_check=True)
                    last = mm(o, tok[s_Vt][a:a + HD, cc, f, :], chk[s_Mrk][a:a + HD, f, cc, :], start=False, stop=True, skip_group_check=True)
                last.then_inc(yc_done, 1)
            pe.wait_ge(yc_evac, NCH)
            pe.wait_ge(gr_evac, KD)
            for f in range(FT):
                mm(ps[:, f, :], K("blk"), S4(s_y)[:, f, :], start=True, stop=True).then_inc(gn_sum, 1)
            pe.wait_ge(st_evac, NCH - 1)
            pe.wait_ge(zc_evac, NCH)
            for f in range(FT):
                pe.wait_ge(gn_sq, f + 1)
                mm(ps[:, 4 + f, :], K("blk"), S4(s_y2)[:, f, :], start=True, stop=True).then_inc(gn_sqsum, 1)

            def late_row(m):
                for hf in range(2):
                    pe.wait_ge(diag_ready, 2 * m + hf + 1)
                    if m:
                        pe.wait_ge(lrow_ready, 2 * m + hf - 1)
                    mm(ps[:, 6 + hf, :], K("ones"), DG[hf].rearrange("p q n -> p (q n)"), start=True, stop=True).then_inc(lrow_done, 1)

            pe.wait_ge(yrw_mean, FT)
            pe.wait_ge(yrw_ready, 1)
            pe.wait_ge(orw_in, 32)
            for f in range(KD):
                if f >= 4:
                    pe.wait_ge(merged_ready, f - 3)
                for k in range(FT):
                    last = mm(ps[:, f % 4, :], orw[k // 2][:, k % 2, P * f:P * f + P], S4(s_y)[:, k, :], start=(k == 0), stop=(k == FT - 1))
                last.then_inc(mix_done, 1)
                if f % 2:
                    late_row(f // 2)

            def transposes_h2(t):
                pe.wait_ge(h2_ready, t + 1)
                if t:
                    pe.wait_ge(h2T_evac, t)
                for k in range(KD):
                    src = h2tok[:, t % 2, :].rearrange("p (q k) -> p k q", k=KD)[:, k, :]
                    last = tr(psf[:, 2048 + P * k:2048 + P * k + P], src, ident)
                last.then_inc(h2T_done, 1)

            pe.wait_ge(merged_ready, KD)
            arrived(pe, "WO0")
            arrived(pe, "WO1")
            for t in range(NT):
                bk = 2 * (t % 2)
                if t >= 2:
                    pe.wait_ge(rstd1, t - 1)
                for hf in range(2):
                    w = chunk(f"WO{hf}", KD)
                    for k in range(KD):
                        last = mm(ps[:, bk + hf, :], merged[:, k, P * t:P * t + P], w[:, k, :], start=(k == 0), stop=(k == KD - 1))
                last.then_inc(y_done, 1)
                if t >= 1:
                    transposes_h2(t - 1)
            transposes_h2(NT - 1)
            pe.wait_ge(h2T_evac, NT)
            pe.wait_ge(rstd1, NT)
            for t in range(NT):
                for k in range(KD):
                    last = mm(ps[:, 0, 64 * t:64 * t + NG + E], hT[:, k, P * t:P * t + P], wr[:, k, :], start=(k == 0),
                              stop=(k == KD - 1), skip_group_check=True)
            last.then_inc(logit_done, 1)
            pe.wait_ge(oh_ready, 1)
            oh = rview(688, 128, 4)
            for t in range(NT):
                for q in range(t):
                    mm(ps[:, 1, E * t:E * t + E], K("ones"), oh[:, q, :], start=(q == 0), stop=False, skip_group_check=True)
                mm(ps[:, 1, E * t:E * t + E], K("before"), oh[:, t, :], start=(t == 0), stop=True, skip_group_check=True)
            for q in range(NT):
                last = mm(ps[:, 2, 0:E], K("ones"), oh[:, q, :], start=(q == 0), stop=(q == NT - 1))
            last.then_inc(rank_done, 1)
            pe.wait_ge(sel_ready, 1)
            for ch in range(2):
                ohr = rview(1168 + 256 * ch, 256, 4)
                for t in range(NT):
                    last = mm(ps[0:CAP, 3, 0:MAXB], ohr[:, t, :], selb[:, ch, t, :], start=(ch == 0 and t == 0),
                              stop=(ch == 1 and t == NT - 1))
            last.then_inc(idx_done, 1)
            pe.wait_ge(route_ready, 1)
            steps = pe.value_load(nblk_i[0:1, 0:1], min_val=E // 2, max_val=MAXB // 2)
            for u in range(2):
                pe.sem_inc(hg_done[u], 1)
                pe.sem_inc(yo_ready[u], 1)
            with pe.Fori(0, steps) as it:
                for u in range(2):
                    pe.wait_ge(hrow_in[u], it * 16 + 16)
                    pe.sem_inc(pe_pass, 1)
                    hv = hrow[0:CAP, u, :].rearrange("p (q k) -> p k q", k=KD)
                    for k in range(KD):
                        last = tr(ps[:, 0, CAP * k:CAP * k + CAP], hv[:, k, :], ident[0:CAP, 0:CAP])
                    last.then_inc(hg_done[u], 1)
                    pe.wait_ge(hg_ready[u], it + 1)
                    pe.wait_ge(w_in_sem[u][0], it * 16 + 16)
                    pe.wait_ge(w_in_sem[u][1], it * 16 + 16)
                    for k in range(KD):
                        for hf in range(2):
                            w2 = eset[u][:, 0:2, :].rearrange("p m (k n) -> p m k n", k=KD)
                            last = mm(ps[64 * hf:64 * hf + 64, 2 + u, :].rearrange("p (m n) -> p m n", m=2), hgT[:, u, k, :],
                                      w2[:, :, k, 256 * hf:256 * hf + 256], start=(k == 0), stop=(k == KD - 1))
                    last.then_inc(up_done[u], 1)
                    pe.wait_ge(hid_ready[u], it + 1)
                    for j in range(2):
                        last = tr(ps[:, 1, P * j:P * j + P], hid[:, u, P * j:P * j + P], ident)
                    last.then_inc(ht_done[u], 1)
                    pe.wait_ge(ht_ready[u], it + 1)
                    pe.wait_ge(w_in_sem[u][2], it * 16 + 16)
                    pe.wait_ge(yo_ready[u], it + 1)
                    wd = eset[u][:, 2, :].rearrange("p (k n) -> p k n", k=4)
                    hv2 = hidT[:, u, :].rearrange("p (j h s) -> p j h s", j=2, h=2)
                    for k in range(4):
                        for hf in range(2):
                            last = mm(ps[64 * hf:64 * hf + 64, 4 + u, :], hv2[:, k % 2, k // 2, :],
                                      wd[:, k, 512 * hf:512 * hf + 512], start=(k == 0), stop=(k == 3))
                    last.then_inc(down_done[u], 1)


_INS = ['x', 'c', 'w_mod', 'b_mod', 'norm_gains', 'w_in', 'gate_bias', 'shift_mu', 'w0', 'w_decay_up', 'a0',
        'w_iclr_up', 'w_gate_up', 'k_k', 'k_a', 'r_k', 'lnx_w', 'lnx_b', 'w_o_sb', 'w_o_rw', 'w_out',
        'w_group', 'w_router', 'w_up1', 'w_up3', 'w_down']


def kernel(**inputs):
    import concourse.bacc as bacc
    from concourse.bass_utils import run_bass_kernel_spmd

    nc = bacc.Bacc("TRN2", target_bir_lowering=False, num_devices=1)
    arrays, args = {}, []
    for name in _INS:
        a = np.ascontiguousarray(inputs[name])
        arrays[f"in_{name}"] = a
        args.append(nc.dram_tensor(f"in_{name}", a.shape, mybir.dt.from_np(a.dtype), kind="ExternalInput").ap())
    arrays["in_consts"] = constants()
    args.append(nc.dram_tensor("in_consts", (P, NCONST), F32, kind="ExternalInput").ap())
    args.append(nc.dram_tensor("out_0", (1, T, D), F32, kind="ExternalOutput").ap())
    build(nc, *args)
    r = run_bass_kernel_spmd(nc, [arrays], core_ids=[0])
    return r.results[0]["out_0"]
```

```python
from contextlib import ExitStack

import numpy as np

import concourse.bass as bass
from concourse import mybir

F32 = mybir.dt.float32
F32R = mybir.dt.float32r
I32 = mybir.dt.int32
ALU = mybir.AluOpType
ACT = mybir.ActivationFunctionType
AX = mybir.AxisListType.X

P = 128
T = 512
D = 1024
KD = D // P
NT = T // P
W = 512
FT = W // P
HD = 64
NH = 8
C = 64
NCH = T // C
E = 32
EG = 8
NG = 4
CAP = 64
MAXB = 48
DECAY = float(np.exp(-0.5))
BIG = 1e30

COL_Q, COL_K, COL_V = 0, W, 2 * W
COL_RW = 3 * W
COL_LORA = COL_RW + 3 * W
N_LORA = 288
COL_GATE = COL_LORA + N_LORA

OFF = [0, 512, 1024, 896]
WID = [T - P * j for j in range(NT)]
ZW = 1280

_widths = [("ident", 128), ("ntri", 128), ("nones", 128), ("ones", 128), ("blk", 128), ("before", 128),
           ("strictU", 64), ("inclU", 64), ("eye", 64), ("lvlL", 6 * 64), ("lvlU", 6 * 64),
           ("iota64", 64), ("m64", 8), ("blk16", 16), ("tok", 4), ("eps", 4)]
CONST = {}
_at = 0
for _n, _w in _widths:
    CONST[_n] = (_at, _w)
    _at += _w
NCONST = _at

_rows = [("mu", 15), ("w0", 4), ("a0", 4), ("kk", 4), ("ka", 4), ("rk", 4), ("lnw", 4), ("lnb", 4), ("gb", 16),
         ("bl", 32), ("gl", 24)]
NROW = sum(w for _, w in _rows)
_pw = _rows + [("c", 8), ("bmod", 16), ("g0", 8), ("silc", 8), ("omka", 4), ("A1", 8), ("SH1", 8), ("ss", 16), ("rs", 16),
               ("modc", 32)]
PAR = {}
_at = 0
for _n, _w in _pw:
    PAR[_n] = (_at, _w)
    _at += _w
NPAR = _at


def constants():
    m = np.zeros((P, NCONST), np.float32)

    def put(name, v):
        a, w = CONST[name]
        m[:, a:a + w] = np.asarray(v, np.float32).reshape(P, w)

    p = np.arange(P)[:, None]
    q = np.arange(P)[None, :]
    put("ident", p == q)
    put("ntri", -(p >= q).astype(np.float32))
    put("nones", -np.ones((P, P)))
    put("ones", np.ones((P, P)))
    put("blk", (p // 64) == (q // 64))
    put("before", p < q)
    r = p % 64
    c = np.arange(64)[None, :]
    put("strictU", r < c)
    put("inclU", r <= c)
    put("eye", r == c)

    def level(k, t, s):
        return ((t >> (k + 1)) == (s >> (k + 1))) & (((t >> k) & 1) == 1) & (((s >> k) & 1) == 0)

    put("lvlL", np.concatenate([level(k, r, c) for k in range(6)], 1))
    put("lvlU", np.concatenate([level(k, c, r) for k in range(6)], 1))
    put("iota64", np.broadcast_to(c, (P, 64)))
    put("m64", np.broadcast_to(CAP * np.arange(8)[None, :], (P, 8)))
    put("blk16", np.broadcast_to(E + np.arange(16)[None, :], (P, 16)))
    put("tok", p + P * np.arange(4)[None, :])
    put("eps", np.broadcast_to(np.array([[1e-6, 64e-5, 1.0, 0.0]]), (P, 4)))
    return m


def build(nc, x, c, w_mod, b_mod, gains, w_in, gate_bias, shift_mu, w0, w_decay_up, a0, w_iclr_up, w_gate_up,
          k_k, k_a, r_k, lnx_w, lnx_b, w_o_sb, w_o_rw, w_out, w_group, w_router, w_up1, w_up3, w_down,
          consts, out):
    ctx = ExitStack()
    with ctx:
        def sb(name, shape, dt=F32):
            return ctx.enter_context(nc.sbuf_tensor(name, shape, dt))

        def sem(name):
            return ctx.enter_context(nc.semaphore(name))

        h2_dram = nc.dram_tensor("h2_rows", [T, D], F32, kind="Internal").ap()
        ye_dram = nc.dram_tensor("expert_rows", [MAXB * CAP, D], F32, kind="Internal").ap()

        cst = sb("cst", [P, NCONST])
        par = sb("par", [P, NPAR])
        wr = sb("wr", [P, KD, NG + E])
        hT = sb("hT", [P, KD, T])
        with (nc.sbuf_tensor("w_parts", [P, 2, 2, KD, P], F32R) as w_parts,
              nc.sbuf_tensor("between0", [P, 2 * 4096 + 3 * 2048], F32), nc.sbuf_tensor("h_upper", [P, KD, T], F32R) as h_hi,
              nc.sbuf_tensor("between1", [P, 2048], F32), nc.sbuf_tensor("h_lower", [P, KD, T], F32R) as h_lo):
            pass
        ring = sb("ring", [P, 3, 4096])
        with nc.sbuf_tensor("below", [P, 10 * 2048 + 2 * ZW], F32), nc.sbuf_tensor("sp_parts", [P, 2, ZW], F32R) as sp_parts:
            pass
        arena = sb("arena", [P, 15, 2048])
        tri_r = sb("tri_r", [P, 2, P], F32R)
        prow = sb("prow", [NROW, P])
        raw = sb("raw", [P, 2, T + 1])
        PC = sb("PC", [P, FT * NCH])
        ST = sb("ST", [P, 2, FT * HD])
        SDZ = sb("SDZ", [P, 2, FT * HD])
        SD, Zs = SDZ[:, 0, :], SDZ[:, 1, :]
        SAs = sb("SAs", [P, 2, FT * HD])
        rt = sb("rt", [P, 2048 // 4])
        routf = sb("routf", [P, 16])
        slots_i = sb("slots_i", [P, 8], I32)
        idx_i = sb("idx_i", [CAP, MAXB], I32)
        idx_now = sb("idx_now", [CAP, 2], I32)
        nblk_i = sb("nblk_i", [1, 20], I32)
        ps = ctx.enter_context(nc.psum_tensor("ps", [P, 8, 512], F32))
        psf = ps[:, :, :].rearrange("p b n -> p (b n)")

        def K(name):
            a, w = CONST[name]
            return cst[:, a:a + w]

        def V(name, i=None, n=1):
            a, w = PAR[name]
            return par[:, a:a + w] if i is None else par[:, a + i:a + i + n]

        def S(i, n=1):
            return arena[:, i:i + n, :].rearrange("p a b -> p (a b)")

        def S4(i):
            return arena[:, i, :].rearrange("p (f t) -> p f t", f=FT)

        eps_rms, eps_gn, one = K("eps")[:, 0:1], K("eps")[:, 1:2], K("eps")[:, 2:3]

        s_r, s_k, s_v = 0, 1, 10
        s_sig, s_cum, s_a, s_P, s_Pi = 3, 4, 5, 6, 7
        s_AR, s_lora, s_g = 8, 8, 13
        s_kk, s_kk2, s_Bh, s_Kh = 11, 12, 11, 12
        s_Vt, s_Bt, s_Kt = 0, 1, 4
        s_q, s_ka, s_va, s_scr = 2, 14, 6, 10
        s_B, s_Kd, s_bonus = 3, 7, 5
        s_MT, s_X, s_XT, s_Mak, s_Mrb, s_Mrk, s_W = 10, 11, 12, 14, 3, 7, 6
        s_H, s_y, s_y2 = 6, 10, 12
        s_orw = (11, 14)
        s_rows, s_x1 = 0, 3

        wlo = S(s_ka)[:, 0:3 * W].rearrange("p (a n) -> p a n", a=3)
        AR = S(s_AR, 2).rearrange("p (f c a t) -> p f c a t", f=FT, c=NCH, a=2)
        lora = S(s_lora, 1).rearrange("p (a t) -> p a t", a=4)
        tok = {i: arena[:, i, :].rearrange("p (c f d) -> p c f d", c=NCH, f=FT) for i in (s_Vt, s_Bt, s_Kt, s_H)}
        chk = {i: arena[:, i, :].rearrange("p (f c t) -> p f c t", f=FT, c=NCH)
               for i in (s_MT, s_X, s_XT, s_Mak, s_Mrb, s_Mrk, s_W, s_B, s_Kd)}
        eb = S(s_scr, 3)
        e_buf = [eb[:, 0:ZW], eb[:, ZW:2 * ZW]]
        sp_hi, sp_lo = sp_parts[:, 0, :], sp_parts[:, 1, :]
        merged = ring[:, 0, :].rearrange("p (k t) -> p k t", k=KD)
        rows = S(s_rows, 2).rearrange("p (m n) -> p m n", m=4)
        x1 = S(s_x1, 2).rearrange("p (t n) -> p t n", t=NT)
        xin, xn = x1, S(s_rows, 2).rearrange("p (t n) -> p t n", t=NT)
        acc_e = S(5, 1).rearrange("p (b n) -> p b n", b=2)
        acc_l = [raw[:, 0, 0:512], raw[:, 1, 0:512]] + [a[:, :, :].rearrange("p b n -> p (b n)") for a in (ST, SAs, SDZ)]
        acc_l += [rt[:, :], S(12, 1)[:, 1024:1536], S(12, 1)[:, 1536:2048]]
        DG = [a.rearrange("p (q n) -> p q n", q=4) for a in (raw[:, 0, 0:512], raw[:, 1, 0:512], rt[:, :])]
        ytok = S(2, 1).rearrange("p (b n) -> p b n", b=2)
        h2tok = S(5, 1).rearrange("p (b n) -> p b n", b=2)
        osb = raw[:, :, 1:T + 1]
        gates_rw = ring[:, 2, :].rearrange("p (k t) -> p k t", k=KD)
        gated = S(5, 1)[:, 0:1024].rearrange("p (b n) -> p b n", b=2)
        eset_up = [ring[:, 0:2, :], S(8, 4).rearrange("p (m n) -> p m n", m=2)]
        eset_down = [ring[:, 2, :], S(6, 2)]
        hrow = S(14, 1).rearrange("p (b n) -> p b n", b=2)
        hgT = S(12, 1)[:, 0:1024].rearrange("p (b k s) -> p b k s", b=2, k=KD)
        yo = S(12, 1)[:, 1024:2048].rearrange("p (b n) -> p b n", b=2)
        sil = S(13, 1)[:, 0:512].rearrange("p (b n) -> p b n", b=2)
        hid = S(13, 1)[:, 512:1024].rearrange("p (b n) -> p b n", b=2)
        hidT = S(13, 1)[:, 1024:1536].rearrange("p (b n) -> p b n", b=2)
        rsc = S(12, 1)
        selb = S(13, 1)[:, 0:2 * NT * MAXB].rearrange("p (c t b) -> p c t b", c=2, t=NT)
        ovb = S(13, 1)[:, 512:1024].rearrange("p (m e) -> p m e", e=E)

        def rview(a, n, t):
            return rsc[:, a:a + n].rearrange("p (t n) -> p t n", t=t)

        fin = [S(5 + 2 * t, 2).rearrange("p (a n) -> p a n", a=4) for t in range(NT)]

        prow_zero, rows_in, rows_turned = sem("prow_zero"), sem("rows_in"), sem("rows_turned")
        consts_in, params_in, lora_in, x_in = sem("consts_in"), sem("params_in"), sem("lora_in"), sem("x_in")
        ring_in = [sem(f"ring_in{i}") for i in range(6)]
        dve_chunk = sem("dve_chunk")
        act_link, dve_link, pool_link = sem("act_link"), sem("dve_link"), sem("pool_link")
        acc_ready, modcol_done, modcol_ready = sem("acc_ready"), sem("modcol_done"), sem("modcol_ready")
        rstd0, xn_ready, xT_done, xT_even, xT_odd = sem("rstd0"), sem("xn_ready"), sem("xT_done"), sem("xT_even"), sem("xT_odd")
        modc_ready = sem("modc_ready")
        par_ready, w_rounded, w_split, h_rounded = (sem(n) for n in ("par_ready", "w_rounded", "w_split", "h_rounded"))
        h_split = [sem("h_split_even"), sem("h_split_odd")]
        proj_tiles = [("LORA", 0, P), ("LORA", P, P), ("LORA", 2 * P, 32)]
        proj_tiles += [(name, P * f, P) for name in ("CK", "CR", "CV") for f in range(FT)]
        pa_done, pa_evac, shifted = sem("pa_done"), sem("pa_evac"), sem("shifted")
        lora_act = sem("lora_act")
        cum_ready, exps_ready = sem("cum_ready"), sem("exps_ready")
        kk2_ready, pd_done, kk_max, rn_ready, bonus_in, bonus_ready = (sem(n) for n in (
            "kk2_ready", "pd_done", "kk_max", "rn_ready", "bonus_in", "bonus_ready"))
        tok_src, tr_done, tr_act, tr_dve = sem("tok_src"), sem("tr_done"), sem("tr_act"), sem("tr_dve")
        tri_ready, sp_rounded, sp_split = sem("tri_ready"), sem("sp_rounded"), sem("sp_split")
        z_done, log_ready, sp_ready, sp_masked, cum_done, att_ready, att_masked, av_all, ysb_ready = (
            sem(n) for n in ("z_done", "log_ready", "sp_ready", "sp_masked", "cum_done", "att_ready",
                             "att_masked", "av_all", "ysb_ready"))
        gram_done, gram_evac, invw_done, invw_evac, invx_done, invx_evac, invt_done, invt_evac = (sem(n) for n in (
            "gram_done", "gram_evac", "invw_done", "invw_evac", "invx_done", "invx_evac", "invt_done", "invt_evac"))
        hp_done, hp_evac, zc_done, zc_evac, sa_done, sa_evac, st_done, st_evac, yc_done, yc_evac = (sem(n) for n in (
            "hp_done", "hp_evac", "zc_done", "zc_evac", "sa_done", "sa_evac", "st_done", "st_evac", "yc_done", "yc_evac"))
        gn_sum, gn_sq, gn_sqsum, gn_rstd, yrw_ready, yrw_mean = (sem(n) for n in (
            "gn_sum", "gn_sq", "gn_sqsum", "gn_rstd", "yrw_ready", "yrw_mean"))
        orw_in, gs_evac, gs_ready, sb_gated = sem("orw_in"), sem("gs_evac"), sem("gs_ready"), sem("sb_gated")
        mix_done, osb_evac, gr_evac, merged_ready = sem("mix_done"), sem("osb_evac"), sem("gr_evac"), sem("merged_ready")
        lacc_ready, lcol_done, lcol_evac, diag_ready, lrow_done, lrow_ready = (sem(n) for n in (
            "lacc_ready", "lcol_done", "lcol_evac", "diag_ready", "lrow_done", "lrow_ready"))
        register_pass = sem("register_pass")
        zero_tile, zero_stored = sem("zero_tile"), sem("zero_stored")
        x_again = sem("x_again")
        y_done, rstd1, x1_ready, rstd2, h2_ready, h2T_done, h2T_evac = (sem(n) for n in (
            "y_done", "rstd1", "x1_ready", "rstd2", "h2_ready", "h2T_done", "h2T_evac"))
        h2_stored = [sem("h2_stored0"), sem("h2_stored1")]
        logit_done, gsum_ready, oh_ready, rank_done, sel_ready, idx_done, route_ready = (sem(n) for n in (
            "logit_done", "gsum_ready", "oh_ready", "rank_done", "sel_ready", "idx_done", "route_ready"))
        w_in_sem = [[sem(f"expert_w{m}_in{u}") for m in range(3)] for u in range(2)]
        hrow_in = [sem("hrow_in0"), sem("hrow_in1")]
        hg_done = [sem("hg_done0"), sem("hg_done1")]
        hg_ready = [sem("hg_ready0"), sem("hg_ready1")]
        up_done = [sem("up_done0"), sem("up_done1")]
        sil_ready = [sem("sil_ready0"), sem("sil_ready1")]
        hid_ready = [sem("hid_ready0"), sem("hid_ready1")]
        ht_done = [sem("ht_done0"), sem("ht_done1")]
        ht_ready = [sem("ht_ready0"), sem("ht_ready1")]
        down_done = [sem("down_done0"), sem("down_done1")]
        yo_ready = [sem("yo_ready0"), sem("yo_ready1")]
        yo_stored = [sem("yo_stored0"), sem("yo_stored1")]
        pick_in = [sem(f"pick_in{t}") for t in range(NT)]
        fin_first, fin_ss, fin_rstd, fin_ready = (sem(n) for n in (
            "fin_first", "fin_ss", "fin_rstd", "fin_ready"))
        out_stored = [sem("out_stored0"), sem("out_stored1")]

        N_SMALL = 4
        FILL_ATT = 5
        LATE_BANK = (2, 3, 4, 5, 2, 3, 2, 3)
        GRAM_FILL = (1, 2)
        HP_BANK = (0, 1, 6, 7)
        wv = w_in.rearrange("o (p k) n -> p (o k) n", k=KD)
        mv = w_mod.rearrange("o (p k) n -> p (o k) n", k=KD)

        def win(a, n):
            return wv[:, :, a:a + n], KD * n

        mod = [(mv[:, :, 512 * j:512 * j + 512], 4096) for j in range(12)]
        wo = w_out.rearrange("o (k p) n -> p (o k) n", p=P)
        gate_q = [win(COL_GATE + 256 * j, 256) for j in range(8)]
        chunk_table = [(f"MOD{j}", *mod[j], j % 3) for j in range(4)]
        chunk_table += [("LORA", *win(COL_LORA, N_LORA), 1), ("CK", *win(COL_RW + W, W), 2), ("CR", *win(COL_RW, W), 1),
                        ("CV", *win(COL_RW + 2 * W, W), 2), ("AQ", *win(COL_Q, W), 1), ("AK", *win(COL_K, W), 0),
                        ("AV", *win(COL_V, W), 1),
                        ("MOD4", *mod[4], 2), ("GS0", *gate_q[0], 3), ("GS1", *gate_q[1], 4), ("MOD5", *mod[5], 2),
                        ("MOD6", *mod[6], 2), ("GS2", *gate_q[2], 3), ("MOD7", *mod[7], 2), ("MOD8", *mod[8], 2),
                        ("GS3", *gate_q[3], 4), ("MOD9", *mod[9], 2), ("MOD10", *mod[10], 2), ("MOD11", *mod[11], 2),
                        ("OSB", w_o_sb.rearrange("o (k p) n -> p (o k) n", p=P), 4096, 1),
                        ("GR0", *gate_q[4], 3), ("GR1", *gate_q[5], 4), ("GR2", *gate_q[6], 3), ("GR3", *gate_q[7], 4),
                        ("WO0", wo[:, :, 0:512], 4096, 1), ("WO1", wo[:, :, 512:1024], 4096, 5)]
        chunk_names = [c_[0] for c_ in chunk_table]
        slot_of = [c_[3] for c_ in chunk_table]
        before = {}
        for n, sl in enumerate(slot_of):
            shared = {1: (1, 3, 4), 3: (1, 3), 4: (1, 4)}.get(sl, (sl,))
            before[n] = max([i for i in range(n) if slot_of[i] in shared], default=None)
        orw = [S(i, 1).rearrange("p (k n) -> p k n", k=2) for i in s_orw]

        def used_by(n):
            name = chunk_names[n]
            if name.startswith("MOD"):
                return dve_chunk, int(name[3:]) + 1
            return {"LORA": (w_split, 3), "CK": (w_split, 7), "CR": (w_split, 11), "CV": (w_split, 15), "AQ": (pa_done, 31),
                    "AK": (pa_done, 35), "AV": (pa_done, 39), "GS0": (mix_done, 2), "GS1": (mix_done, 4),
                    "GS2": (mix_done, 6), "GS3": (mix_done, 8), "OSB": (mix_done, 16), "GR0": (mix_done, 18),
                    "GR1": (mix_done, 20), "GR2": (mix_done, 22), "GR3": (mix_done, 24)}[name]

        def arrived(eng, name):
            n = chunk_names.index(name)
            eng.wait_ge(ring_in[slot_of[n]], 16 * slot_of[:n + 1].count(slot_of[n]))

        def ring_place(n):
            if slot_of[n] == 5:
                return S(6, 2)
            at = {3: 4096, 4: 4096 + 2048}.get(slot_of[n], 4096 * slot_of[n])
            return ring[:, :, :].rearrange("p s n -> p (s n)")[:, at:at + chunk_table[n][2]]

        def chunk(name, k):
            return ring_place(chunk_names.index(name)).rearrange("p (k n) -> p k n", k=k)

        up1 = w_up1.rearrange("o e (p k) n -> p (o e) (k n)", k=KD)
        up3 = w_up3.rearrange("o e (p k) n -> p (o e) (k n)", k=KD)
        dn = w_down.rearrange("o e (k p) n -> p (o e) k n", p=P)
        esrc = [up1, up3, dn]

        def load_expert(eng, u, m, e):
            if m < 2:
                dst = eset_up[u][:, m, :]
                src = esrc[m][:, bass.ds(e, 1), :].rearrange("p a n -> p (a n)")
            else:
                src = dn[:, bass.ds(e, 1), :, :].rearrange("p a k n -> p (a k) n")
                dst = eset_down[u].rearrange("p (k n) -> p k n", k=4)
            eng.dma_start(dst, src).then_inc(w_in_sem[u][m], 16)

        def load_orw(eng):
            eng.wait_ge(hp_done, 4)
            wsrc = w_o_rw.rearrange("o (k p) n -> p (o k) n", p=P)
            for i in range(2):
                eng.dma_start(orw[i], wsrc[:, 2 * i:2 * i + 2, :]).then_inc(orw_in, 16)

        block = ctx.enter_context(nc.Block())

        @block.sync
        def _(sp):
            sp.wait_ge(params_in, 16 * N_SMALL)
            for n, (name, src, width, sl) in enumerate(chunk_table):
                if before[n] is not None:
                    s, v = used_by(before[n])
                    sp.wait_ge(s, v)
                if name == "AK":
                    sp.wait_ge(pa_done, 15)
                if name == "GR2":
                    load_orw(sp)
                if name == "WO1":
                    sp.wait_ge(yc_done, NCH)
                    sp.wait_ge(zc_evac, NCH)
                sp.dma_start(ring_place(n).rearrange("p (k n) -> p k n", k=src.shape[1]), src).then_inc(ring_in[sl], 16)
            sp.wait_ge(merged_ready, KD)
            load_expert(sp, 0, 2, 0)
            sp.wait_ge(mix_done, 4 * KD)
            load_expert(sp, 1, 0, 1)
            load_expert(sp, 1, 1, 1)
            sp.wait_ge(y_done, NT)
            load_expert(sp, 0, 0, 0)
            load_expert(sp, 0, 1, 0)
            load_expert(sp, 1, 2, 1)
            with sp.Fori(1, E // 2) as it:
                for u in range(2):
                    sp.wait_ge(up_done[u], it)
                    load_expert(sp, u, 0, 2 * it + u)
                    load_expert(sp, u, 1, 2 * it + u)
                    sp.wait_ge(down_done[u], it)
                    load_expert(sp, u, 2, 2 * it + u)
            sp.wait_ge(route_ready, 1)
            n_over = sp.value_load(nblk_i[0:1, 1:2], min_val=0, max_val=8)
            with sp.If(n_over > 0):
                with sp.Fori(0, n_over) as it:
                    for u in range(2):
                        e = sp.value_load(nblk_i[0:1, bass.ds(2 * it + 2 + u, 1)], min_val=0, max_val=E - 1)
                        sp.wait_ge(up_done[u], it + E // 2)
                        load_expert(sp, u, 0, e)
                        load_expert(sp, u, 1, e)
                        sp.wait_ge(down_done[u], it + E // 2)
                        load_expert(sp, u, 2, e)
            with sp.Else():
                sp.nop()
            sp.nop()
            for t in range(NT):
                sp.wait_ge(fin_ready, t + 1)
                sp.dma_start(out[0, P * t:P * t + P, :], fin[t][:, 2, :]).then_inc(out_stored[t % 2], 16)
            sp.wait_ge(out_stored[0], 32)
            sp.wait_ge(out_stored[1], 32)

        @block.gpsimd
        def _(pool):
            def weight_lower(n):
                name, a, w = proj_tiles[n]
                pool.wait_ge(w_rounded, n + 1)
                nc.gpsimd.tensor_tensor(w_parts[:, n % 2, 1, :, 0:w], chunk(name, KD)[:, :, a:a + w],
                                        w_parts[:, n % 2, 0, :, 0:w].bitcast(F32), ALU.subtract).then_inc(w_split, 1)

            pool.wait_ge(rstd0, 1)
            for t in range(NT):
                nc.gpsimd.tensor_scalar(xn[:, t, :], xin[:, t, :], V("rs", 8 + t), None, ALU.mult).then_inc(xn_ready, 1)

            pool.wait_ge(xn_ready, NT)
            weight_lower(0)
            weight_lower(1)
            for k in range(0, KD, 2):
                pool.wait_ge(h_rounded, k + 1)
                nc.gpsimd.tensor_tensor(h_lo[:, k, :], hT[:, k, :], h_hi[:, k, :].bitcast(F32), ALU.subtract).then_inc(h_split[0], 1)
            for n in range(2, len(proj_tiles)):
                weight_lower(n)

            def diag(buf, ready):
                for j in range(NT):
                    v = buf[:, OFF[j]:OFF[j] + P]
                    last = nc.gpsimd.affine_select(out=v, in_=v, compare_op=ALU.is_gt, fill=0.0, base=0,
                                                   pattern=[[1, P]], channel_multiplier=-1)
                last.then_inc(ready, 1)

            for h in range(NH + 1):
                if h < NH:
                    pool.wait_ge(sp_ready, h + 1)
                    diag(e_buf[h % 2], sp_masked)
                if h >= 1:
                    pool.wait_ge(att_ready, h)
                    diag(e_buf[(h - 1) % 2], att_masked)
                if h < NH:
                    pool.wait_ge(sp_rounded, h + 1)
                    nc.gpsimd.tensor_tensor(sp_lo, e_buf[h % 2], sp_hi.bitcast(F32), ALU.subtract).then_inc(sp_split, 1)
            pool.wait_ge(gs_ready, 1)
            for n in range(KD):
                pool.wait_ge(osb_evac, n + 1)
                nc.gpsimd.tensor_tensor(merged[:, n, :], merged[:, n, :], osb[:, n % 2, :], ALU.mult).then_inc(sb_gated, 1)
            pool.wait_ge(modc_ready, 1)
            pool.wait_ge(sb_gated, KD)
            for n in range(8):
                if n >= 3:
                    pool.wait_ge(lrow_done, n - 2)
                cols = V("modc", 4 * n, 4).rearrange("p (q o) -> p q o", o=1).broadcast_to((P, 4, P))
                nc.gpsimd.tensor_tensor(DG[n % 3], K("ident").rearrange("p (o n) -> p o n", o=1).broadcast_to((P, 4, P)), cols,
                                        ALU.mult).then_inc(diag_ready, 1)
            pool.wait_ge(x1_ready, NT)
            pool.wait_ge(rstd2, NT)
            nc.gpsimd.memset(S(2), 0.0).then_inc(zero_tile, 1)
            pool.wait_ge(zero_tile, 1)
            over = ye_dram[E * CAP:MAXB * CAP, :].rearrange("(p r) n -> p (r n)", p=P)
            for q in range(4):
                pool.dma_start(over[:, 2048 * q:2048 * q + 2048], S(2)).then_inc(zero_stored, 16)
            pool.wait_ge(route_ready, 1)
            pool.wait_ge(zero_stored, 64)
            pool.wait_ge(h2_stored[0], 32)
            pool.wait_ge(h2_stored[1], 32)
            steps = pool.value_load(nblk_i[0:1, 0:1], min_val=E // 2, max_val=MAXB // 2)
            with pool.Fori(0, steps) as it:
                for u in range(2):
                    pool.wait_ge(hg_done[u], it + 1)
                    nc.gpsimd.tensor_copy(idx_now[:, u:u + 1], idx_i[:, bass.ds(2 * it + u, 1)]).then_inc(pool_link, 1)
                    pool.wait_ge(pool_link, 2 * it + u + 1)
                    pool.sem_inc(register_pass, 1)
                    nc.gpsimd.indirect_dma_start(
                        out=hrow[0:CAP, u, :], out_offset=None, in_=h2_dram,
                        in_offset=bass.IndirectOffsetOnAxis(ap=idx_now[:, u:u + 1], axis=0)).then_inc(hrow_in[u], 16)
            for u in range(2):
                pool.wait_ge(yo_stored[u], steps * 32 + 32)
                pool.sem_inc(register_pass, 1)
            for t in range(NT):
                for ch in range(2):
                    nc.gpsimd.indirect_dma_start(
                        out=fin[t][:, ch, :], out_offset=None, in_=ye_dram,
                        in_offset=bass.IndirectOffsetOnAxis(ap=slots_i[:, 2 * t + ch:2 * t + ch + 1], axis=0)
                    ).then_inc(pick_in[t], 16)

        @block.scalar
        def _(act):
            links = [0]

            def link(ins):
                links[0] += 1
                ins.then_inc(act_link, 1)
                act.wait_ge(act_link, links[0])

            A = nc.scalar.activation
            act.dma_start(V("c"), c.rearrange("o (p k) -> p (o k)", k=KD)).then_inc(params_in, 16)
            for m in range(2):
                act.dma_start(V("bmod", 8 * m, 8), b_mod[0:1, D * m:D * m + D].rearrange("o (p k) -> p (o k)", k=KD)).then_inc(params_in, 16)
            act.dma_start(V("g0"), gains[0, 0:1, :].rearrange("o (p k) -> p (o k)", k=KD)).then_inc(params_in, 16)
            act.dma_start(cst[:, :], consts).then_inc(consts_in, 16)
            act.dma_start(xin[:, :, :], x.rearrange("o (t p) n -> p (o t) n", p=P)).then_inc(x_in, 16)
            act.wait_ge(params_in, 16 * N_SMALL)
            link(A(V("silc"), V("c"), ACT.Sigmoid))
            act.wait_ge(prow_zero, 1)
            act.dma_start(prow[0:14, :], shift_mu[0:1, 0:1792].rearrange("o (f p) -> (o f) p", p=P)).then_inc(rows_in, 16)
            act.dma_start(prow[14:15, 0:32], shift_mu[0:1, 1792:1824]).then_inc(rows_in, 16)
            for name, src in (("w0", w0), ("a0", a0), ("kk", k_k), ("ka", k_a), ("lnw", lnx_w), ("lnb", lnx_b),
                              ("gb", gate_bias)):
                a, w = PAR[name]
                act.dma_start(prow[a:a + w, :], src.rearrange("o (f p) -> (o f) p", p=P)).then_inc(rows_in, 16)
            a, w = PAR["bl"]
            act.dma_start(prow[a:a + w, :], b_mod[0:1, 2 * D:].rearrange("o (f p) -> (o f) p", p=P)).then_inc(rows_in, 16)
            a, w = PAR["gl"]
            act.dma_start(prow[a:a + w, :], gains[0, 1:4, :].rearrange("g (f p) -> (g f) p", p=P)).then_inc(rows_in, 16)
            a, w = PAR["rk"]
            act.dma_start(prow[a:a + w, :], r_k.rearrange("o (f a) d -> (o f) (a d)", a=2)).then_inc(rows_in, 16)
            act.dma_start(wlo[0:64, 0, :], w_decay_up[0]).then_inc(lora_in, 16)
            act.dma_start(wlo[64:128, 0, :], w_iclr_up[0]).then_inc(lora_in, 16)
            act.dma_start(wlo[:, 1, :], w_gate_up[0, 0:128, :]).then_inc(lora_in, 16)
            act.dma_start(wlo[0:32, 2, :], w_gate_up[0, 128:160, :]).then_inc(lora_in, 16)
            act.dma_start(wr[:, :, 0:NG], w_group.rearrange("o (p k) n -> p (o k) n", k=KD)).then_inc(lora_in, 16)
            act.dma_start(wr[:, :, NG:], w_router.rearrange("o (p k) n -> p (o k) n", k=KD)).then_inc(lora_in, 16)
            act.wait_ge(consts_in, 16)
            nc.scalar.preload_act_table_set("natural_log_exp_and_others")
            act.wait_ge(x_in, 16)
            for t in range(NT):
                link(A(xn[:, t, :], xin[:, t, :], ACT.Square, accum_out=V("ss", t)))
            link(A(V("ss", 0, 4), V("ss", 0, 4), ACT.Ln, scale=1.0 / D, bias=eps_rms))
            A(V("rs", 8, 4), V("ss", 0, 4), ACT.Exp, scale=-0.5).then_inc(rstd0, 1)
            act.wait_ge(dve_chunk, 4)
            def weight_upper(n):
                name, a, w = proj_tiles[n]
                arrived(act, name)
                if n >= 2:
                    act.wait_ge(pa_done, n - 1)
                A(w_parts[:, n % 2, 0, :, 0:w], chunk(name, KD)[:, :, a:a + w], ACT.Copy).then_inc(w_rounded, 1)

            weight_upper(0)
            weight_upper(1)
            act.wait_ge(modcol_ready, 1)
            for k in range(KD):
                if k % 2 == 0:
                    act.wait_ge(xT_done, k + 1)
                    A(hT[:, k, :], ps[:, k % 7, :], ACT.Identity, scale=V("A1", k), bias=V("SH1", k)).then_inc(xT_even, 1)
                    act.wait_ge(xT_even, k // 2 + 1)
                else:
                    act.wait_ge(xT_odd, k // 2 + 1)
                A(h_hi[:, k, :], hT[:, k, :], ACT.Copy).then_inc(h_rounded, 1)

            g = 0

            def evac(dst, func, **kw):
                nonlocal g
                act.wait_ge(pa_done, g + 1)
                bank = ps[:, g % 6, 0:T]
                ins = A(dst, bank[0:dst.shape[0], :], func, **kw)
                ins.then_inc(pa_evac, 1)
                g += 1
                return ins

            for n in range(15):
                if n >= 2:
                    act.wait_ge(shifted, n - 1)
                evac(raw[0:32 if n == 2 else P, n % 2, 1:T + 1], ACT.Copy)
                if n + 2 < 15:
                    weight_upper(n + 2)
                if n == 4:
                    act.wait_ge(shifted, 3)
                    A(lora[0:64, 0, :], lora[0:64, 0, :], ACT.Tanh)
                    A(lora[:, 1, :], lora[:, 1, :], ACT.Sigmoid)
                    A(lora[0:32, 2, :], lora[0:32, 2, :], ACT.Sigmoid).then_inc(lora_act, 1)
            for f in range(FT):
                evac(S4(s_sig)[:, f, :], ACT.Sigmoid, bias=V("w0", f))
            for f in range(FT):
                evac(S4(s_a)[:, f, :], ACT.Sigmoid, bias=V("a0", f))
            for f in range(FT):
                evac(S4(s_g)[:, f, :], ACT.Copy)
            act.wait_ge(cum_ready, 1)
            A(S(s_P), S(s_cum), ACT.Exp, scale=-DECAY)
            A(S(s_Pi), S(s_cum), ACT.Exp, scale=DECAY)
            A(S(s_sig), S(s_sig), ACT.Exp, scale=-DECAY).then_inc(exps_ready, 1)
            act.wait_ge(kk_max, FT)
            link(A(S(s_kk2), S(s_kk2), ACT.Ln))
            A(S(s_kk2), S(s_kk2), ACT.Exp, scale=-0.5).then_inc(rn_ready, 1)
            for f in range(FT):
                evac(S4(s_q)[:, f, :], ACT.Copy, scale=HD ** -0.5)
            for f in range(FT):
                evac(S4(s_ka)[:, f, :], ACT.Copy)
            act.wait_ge(tok_src, 1)
            for t in range(NT):
                evac(S4(s_va)[:, t, :], ACT.Copy)
            for n in range(0, 3 * NCH, 2):
                act.wait_ge(tr_done, n + 1)
                cc, dst = n % NCH, tok[(s_Vt, s_Bt, s_Kt)[n // NCH]]
                src = ps[0:64, n % 6, :].rearrange("p (f d) -> p f d", f=FT)
                A(dst[0:64, cc, :, :], src[:, :, 0:64], ACT.Copy)
                A(dst[64:128, cc, :, :], src[:, :, 64:128], ACT.Copy).then_inc(tr_act, 1)

            A(tri_r[:, 0, :], K("ntri"), ACT.Copy)
            A(tri_r[:, 1, :], K("nones"), ACT.Copy).then_inc(tri_ready, 1)
            nc.scalar.preload_act_table_set("natural_log_exp_and_others")
            for h in range(NH + 1):
                if h < NH:
                    act.wait_ge(z_done, h + 1)
                    if h >= 2:
                        act.wait_ge(av_all, h - 1)
                    link(A(e_buf[h % 2], psf[:, 1536 * (h % 2):1536 * (h % 2) + ZW], ACT.Abs))
                    link(A(e_buf[h % 2], e_buf[h % 2], ACT.Exp, scale=-1.0))
                    A(e_buf[h % 2], e_buf[h % 2], ACT.Ln, bias=one).then_inc(log_ready, 1)
                if h >= 1:
                    g_ = h - 1
                    act.wait_ge(cum_done, g_ + 1)
                    A(e_buf[g_ % 2], psf[:, 1536 * (g_ % 2):1536 * (g_ % 2) + ZW], ACT.Exp).then_inc(att_ready, 1)
                    act.wait_ge(mix_done, g_ + 1)
                    A(merged[:, g_, :], ps[:, 7, :], ACT.Identity, bias=V("gb", g_)).then_inc(gs_evac, 1)
                if h < NH:
                    act.wait_ge(sp_masked, h + 1)
                    A(sp_hi, e_buf[h % 2], ACT.Copy).then_inc(sp_rounded, 1)
                if h >= 1:
                    if g_ % 2 == 1:
                        f = g_ // 2
                        act.wait_ge(av_all, 2 * f + 2)
                        A(S4(s_q)[:, f, :], ps[:, 6, :], ACT.Copy).then_inc(ysb_ready, 1)

            act.wait_ge(gs_evac, KD)
            A(merged[:, :, :], merged[:, :, :], ACT.Sigmoid).then_inc(gs_ready, 1)

            def w_out_of_psum(k, f):
                act.wait_ge(invw_done, FT * (k - 1) + f + 1)
                A(S4(s_W)[:, f, :], ps[:, f % 2, :], ACT.Copy).then_inc(invw_evac, 1)

            def xt_out_of_psum(k, f):
                act.wait_ge(invt_done, FT * (k - 1) + f + 1)
                src = psf[0:64, 6 * 512:8 * 512].rearrange("p (c a t) -> p c a t", c=NCH, a=2)
                A(chk[s_XT][0:64, f], src[:, :, 0, :], ACT.Copy)
                A(chk[s_XT][64:128, f], src[:, :, 1, :], ACT.Copy).then_inc(invt_evac, 1)

            def output_evac(n):
                act.wait_ge(mix_done, KD + n + 1)
                if n >= 2:
                    act.wait_ge(sb_gated, n - 1)
                A(osb[:, n % 2, :], ps[:, 2 + n % 2, :], ACT.Copy).then_inc(osb_evac, 1)

            for n in range(3):
                output_evac(n)
            for k in range(1, 6):
                w_out_of_psum(k, 0)
                if k > 1:
                    xt_out_of_psum(k - 1, 3)
                w_out_of_psum(k, 1)
                w_out_of_psum(k, 2)
                if k < 5:
                    xt_out_of_psum(k, 0)
                w_out_of_psum(k, 3)
                if k < 5:
                    xt_out_of_psum(k, 1)
                    xt_out_of_psum(k, 2)
                output_evac(k + 2)
            act.wait_ge(dve_chunk, 12)
            for b in range(4):
                act.wait_ge(hp_done, b + 1)
                A(S(s_H)[:, 512 * b:512 * b + 512], ps[:, HP_BANK[b], :], ACT.Copy).then_inc(hp_evac, 1)
            for cc in range(NCH):
                act.wait_ge(sa_done, cc + 1)
                if cc >= 2:
                    act.wait_ge(yc_done, cc - 1)
                A(SAs[:, cc % 2, :], ps[:, 5, 0:256], ACT.Copy).then_inc(sa_evac, 1)
                act.wait_ge(yc_done, cc + 1)
                A(S4(s_y)[:, :, C * cc:C * cc + C], ps[:, 7 if cc % 2 else 0, 0:256].rearrange("p (f t) -> p f t", f=FT),
                  ACT.Copy).then_inc(yc_evac, 1)
                act.wait_ge(mix_done, 2 * KD + cc + 1)
                A(gates_rw[:, cc, :], ps[:, 2 + cc % 2, :], ACT.Sigmoid, bias=V("gb", KD + cc)).then_inc(gr_evac, 1)
            act.dma_start(x1[:, :, :], x.rearrange("o (t p) n -> p (o t) n", p=P)).then_inc(x_again, 16)
            nc.scalar.preload_act_table_set("natural_log_exp_and_others")
            for f in range(FT):
                act.wait_ge(yrw_mean, f + 1)
                A(S4(s_y2)[:, f, :], S4(s_y)[:, f, :], ACT.Square).then_inc(gn_sq, 1)
            def late_row_evac(n):
                act.wait_ge(lrow_done, n + 1)
                A(rows[:, n // 2, 512 * (n % 2):512 * (n % 2) + 512], ps[:, n % 4, :], ACT.Copy).then_inc(lrow_ready, 1)

            for f in range(FT):
                act.wait_ge(gn_sqsum, f + 1)
                link(A(S4(s_y2)[:, f, :], ps[:, 4 + f, :], ACT.Ln, scale=1.0 / HD, bias=eps_gn))
                A(S4(s_y2)[:, f, :], S4(s_y2)[:, f, :], ACT.Exp, scale=-0.5).then_inc(gn_rstd, 1)
                if f >= 1:
                    late_row_evac(f - 1)
            for n in range(3, 8):
                late_row_evac(n)
            for t in range(NT):
                act.wait_ge(y_done, t + 1)
                bk = 2 * (t % 2)
                link(A(ytok[:, 0, :], psf[:, 512 * bk:512 * bk + D], ACT.Square, accum_out=V("ss", 4 + t)))
                link(A(V("ss", 4 + t), V("ss", 4 + t), ACT.Ln, scale=1.0 / D, bias=eps_rms))
                A(V("rs", 4 + t), V("ss", 4 + t), ACT.Exp, scale=-0.5).then_inc(rstd1, 1)
                act.wait_ge(x1_ready, t + 1)
                link(A(ytok[:, 0, :], x1[:, t, :], ACT.Square, accum_out=V("ss", 8 + t)))
                link(A(V("ss", 8 + t), V("ss", 8 + t), ACT.Ln, scale=1.0 / D, bias=eps_rms))
                A(V("rs", 8 + t), V("ss", 8 + t), ACT.Exp, scale=-0.5).then_inc(rstd2, 1)
                act.wait_ge(h2_ready, t + 1)
                act.dma_start(h2_dram[P * t:P * t + P, :], h2tok[:, t % 2, :]).then_inc(h2_stored[t % 2], 16)
                act.wait_ge(h2T_done, t + 1)
                A(hT[:, :, P * t:P * t + P], psf[:, 2048:2048 + D].rearrange("p (k t) -> p k t", k=KD),
                  ACT.Copy).then_inc(h2T_evac, 1)
            act.wait_ge(oh_ready, 1)
            A(rt[:, 16:32], rt[:, 0:16], ACT.Exp)
            A(rt[:, 36:40], rt[:, 32:36], ACT.Exp).then_inc(gsum_ready, 1)
            act.wait_ge(route_ready, 1)
            nc.scalar.preload_act_table_set("silu_and_others")
            steps = act.value_load(nblk_i[0:1, 0:1], min_val=E // 2, max_val=MAXB // 2)
            for u in range(2):
                act.sem_inc(yo_stored[u], 32)
            with act.Fori(0, steps) as it:
                for u in range(2):
                    act.wait_ge(up_done[u], it + 1)
                    A(sil[:, u, :], ps[:, 2 + u, 0:256], ACT.Silu).then_inc(sil_ready[u], 1)
                    act.wait_ge(down_done[u], it + 1)
                    act.wait_ge(yo_stored[u], it * 32 + 32)
                    A(yo[:, u, :], ps[:, 4 + u, :], ACT.Copy).then_inc(yo_ready[u], 1)
                    act.wait_ge(yo_ready[u], it + 2)
                    for hf in range(2):
                        act.dma_start(ye_dram[bass.ds(it * (2 * CAP) + CAP * u, CAP), 512 * hf:512 * hf + 512],
                                      yo[64 * hf:64 * hf + 64, u, :]).then_inc(yo_stored[u], 16)
            nc.scalar.preload_act_table_set("natural_log_exp_and_others")
            def weigh_first(t):
                act.wait_ge(pick_in[t], 32)
                A(fin[t][:, 2, :], fin[t][:, 0, :], ACT.Copy, scale=routf[:, t:t + 1]).then_inc(fin_first, 1)

            weigh_first(0)
            for t in range(NT):
                if t < NT - 1:
                    weigh_first(t + 1)
                act.wait_ge(fin_ss, t + 1)
                link(A(fin[t][:, 3, :], fin[t][:, 2, :], ACT.Square, accum_out=V("ss", 12 + t)))
                link(A(V("ss", 12 + t), V("ss", 12 + t), ACT.Ln, scale=1.0 / D, bias=eps_rms))
                A(V("rs", 12 + t), V("ss", 12 + t), ACT.Exp, scale=-0.5).then_inc(fin_rstd, 1)

        @block.vector
        def _(dve):
            links = [0]

            def link(ins):
                links[0] += 1
                ins.then_inc(dve_link, 1)
                dve.wait_ge(dve_link, links[0])

            TT, TS, STT, CP = (nc.vector.tensor_tensor, nc.vector.tensor_scalar, nc.vector.scalar_tensor_tensor,
                               nc.vector.tensor_copy)
            nc.vector.memset(prow[:, :], 0.0).then_inc(prow_zero, 1)
            dve.wait_ge(act_link, 1)
            link(TT(V("silc"), V("silc"), V("c"), ALU.mult))
            nc.vector.memset(raw[:, :, 0:1], 0.0)

            def modulation(acc, src_of, arrive, free, ready):
                arrive()
                for k in range(KD):
                    w = src_of[:, k, :]
                    if k == 0:
                        ins = TS(acc, w, V("silc", 0), None, ALU.mult)
                    else:
                        ins = STT(acc, w, V("silc", k), acc, ALU.mult, ALU.add)
                    if k < KD - 1:
                        link(ins)
                ins.then_inc(dve_link, 1)
                links[0] += 1
                dve.wait_ge(dve_link, links[0])
                nc.vector.engine_nop().then_inc(free, 1)
                if ready is not None:
                    nc.vector.engine_nop().then_inc(ready, 1)

            modulation(acc_e[:, 0, 0:512], chunk("MOD0", KD), lambda: arrived(dve, "MOD0"), dve_chunk, None)
            modulation(acc_e[:, 0, 512:1024], chunk("MOD1", KD), lambda: arrived(dve, "MOD1"), dve_chunk, acc_ready)
            dve.wait_ge(rows_turned, 1)
            CP(par[:, 0:NROW], ps[:, 6, 0:NROW]).then_inc(par_ready, 1)
            modulation(acc_e[:, 1, 0:512], chunk("MOD2", KD), lambda: arrived(dve, "MOD2"), dve_chunk, None)
            modulation(acc_e[:, 1, 512:1024], chunk("MOD3", KD), lambda: arrived(dve, "MOD3"), dve_chunk, acc_ready)
            dve.wait_ge(modcol_done, 1)
            TT(V("SH1"), ps[:, 7, 0:8], V("bmod", 0, 8), ALU.add)
            link(TT(V("A1"), ps[:, 7, 8:16], V("bmod", 8, 8), ALU.add))
            STT(V("A1"), V("A1"), 1.0, V("g0"), ALU.add, ALU.mult).then_inc(modcol_ready, 1)

            for k in range(1, KD, 2):
                dve.wait_ge(xT_done, k + 1)
                if k == 1:
                    dve.wait_ge(modcol_ready, 1)
                TS(hT[:, k, :], ps[:, k % 7, :], V("A1", k), V("SH1", k), ALU.mult, ALU.add).then_inc(xT_odd, 1)
            for k in range(1, KD, 2):
                dve.wait_ge(h_rounded, k + 1)
                TT(h_lo[:, k, :], hT[:, k, :], h_hi[:, k, :].bitcast(F32), ALU.subtract).then_inc(h_split[1], 1)
            dve.wait_ge(par_ready, 1)
            link(TS(V("omka"), V("ka"), -1.0, 1.0, ALU.mult, ALU.add))

            order = [(12, lora[:, 0, :], P), (13, lora[:, 1, :], P), (14, lora[0:32, 2, :], 32)]
            order += [(4 + f, S4(s_k)[:, f, :], P) for f in range(FT)]
            order += [(f, S4(s_r)[:, f, :], P) for f in range(FT)]
            order += [(8 + f, S4(s_v)[:, f, :], P) for f in range(FT)]
            for n, (m, dst, r_) in enumerate(order):
                dve.wait_ge(pa_evac, n + 1)
                if n == 3:
                    dve.wait_ge(xT_done, KD)
                b = raw[0:r_, n % 2, :]
                link(TT(dst, b[:, 0:T], b[:, 1:T + 1], ALU.subtract))
                STT(dst, dst, V("mu", m)[0:r_, :], b[:, 1:T + 1], ALU.mult, ALU.add).then_inc(shifted, 1)
            dve.wait_ge(shifted, 15)
            for f in range(FT):
                ins = TS(S4(s_kk)[:, f, :], S4(s_k)[:, f, :], V("kk", f), None, ALU.mult)
            link(ins)
            TT(S(s_kk2), S(s_kk), S(s_kk), ALU.mult).then_inc(kk2_ready, 1)
            for f in range(FT):
                dve.wait_ge(pa_evac, 15 + f + 1)
                for cc in range(NCH):
                    sl = slice(C * cc, C * cc + C)
                    ins = nc.vector.tensor_tensor_scan(S4(s_cum)[:, f, sl], K("ones")[:, 0:C], S4(s_sig)[:, f, sl], 0.0,
                                                       ALU.mult, ALU.add)
            link(ins)
            TT(S(s_sig), S(s_cum), S(s_sig), ALU.subtract).then_inc(cum_ready, 1)
            for f in range(FT):
                dve.wait_ge(pd_done, f + 1)
                TS(S4(s_kk2)[:, f, :], ps[:, 6 + f % 2, :], 1e-24, None, ALU.max).then_inc(kk_max, 1)
            dve.wait_ge(rn_ready, 1)
            dve.wait_ge(exps_ready, 1)
            dve.wait_ge(pa_evac, 15 + 2 * FT)
            link(TT(S(s_kk), S(s_kk), S(s_kk2), ALU.mult))
            link(TT(S(s_kk2), S(s_kk), S(s_a), ALU.mult))
            dve.wait_ge(pa_done, 15 + 3 * FT)
            ARv = S(s_AR, 2).rearrange("p (g a t) -> p g a t", a=2, t=C)
            P3 = lambda i: S(i).rearrange("p (g t) -> p g t", t=C)
            link(STT(ARv[:, :, 0, :], P3(s_kk), -1.0, P3(s_sig), ALU.mult, ALU.mult))
            link(TT(S(s_B), S(s_kk2), S(s_Pi), ALU.mult))
            for f in range(FT):
                ins = TS(S4(s_a)[:, f, :], S4(s_a)[:, f, :], V("ka", f), V("omka", f), ALU.mult, ALU.add)
            link(ins)
            link(TT(S(s_k), S(s_k), S(s_a), ALU.mult))
            for f in range(FT):
                ins = STT(S4(s_a)[:, f, :], S4(s_r)[:, f, :], V("rk", f), S4(s_k)[:, f, :], ALU.mult, ALU.mult)
            ins.then_inc(bonus_in, 1)
            TT(ARv[:, :, 1, :], P3(s_r), P3(s_P), ALU.mult)
            link(CP(PC[:, :], P3(s_P)[:, :, C - 1]))
            link(TT(S(s_Kd), S(s_k), S(s_Pi), ALU.mult))
            pcb = PC[:, :].rearrange("p (g o) -> p g o", o=1).broadcast_to((P, FT * NCH, C))
            TT(P3(s_Bh), P3(s_B), pcb, ALU.mult)
            TT(P3(s_Kh), P3(s_Kd), pcb, ALU.mult).then_inc(tok_src, 1)
            dve.wait_ge(bonus_in, 1)
            for f in range(FT):
                dve.wait_ge(pd_done, FT + f + 1)
                TT(S4(s_bonus)[:, f, :], ps[:, 6 + f % 2, :], S4(s_v)[:, f, :], ALU.mult).then_inc(bonus_ready, 1)
            for n in range(1, 3 * NCH, 2):
                dve.wait_ge(tr_done, n + 1)
                cc, dst = n % NCH, tok[(s_Vt, s_Bt, s_Kt)[n // NCH]]
                src = ps[0:64, n % 6, :].rearrange("p (f d) -> p f d", f=FT)
                CP(dst[0:64, cc, :, :], src[:, :, 0:64])
                CP(dst[64:128, cc, :, :], src[:, :, 64:128]).then_inc(tr_dve, 1)

            dve.wait_ge(tr_done, 3 * NCH)
            for h in range(NH):
                z = psf[:, 1536 * (h % 2):1536 * (h % 2) + ZW]
                dve.wait_ge(log_ready, h + 1)
                STT(e_buf[h % 2], z, 0.0, e_buf[h % 2], ALU.max, ALU.add).then_inc(sp_ready, 1)
                modulation(acc_l[h], chunk(f"MOD{4 + h}", KD), lambda: arrived(dve, f"MOD{4 + h}"), dve_chunk, lacc_ready)
            modc = V("modc", 0, 32)
            own = eb[:, 0:2048].rearrange("p (j q n) -> p j q n", j=4, q=4)
            dve.wait_ge(av_all, NH)
            for j in range(NH):
                dve.wait_ge(lcol_done, j + 1)
                TT(own[:, j % 4], ps[:, LATE_BANK[j], :].rearrange("p (q n) -> p q n", q=4),
                   K("ident").rearrange("p (o n) -> p o n", o=1).broadcast_to((P, 4, P)), ALU.mult).then_inc(lcol_evac, 1)
                dve.wait_ge(lcol_evac, j + 1)
                ins = nc.vector.tensor_reduce(modc[:, 4 * j:4 * j + 4].rearrange("p (q o) -> p q o", o=1), own[:, j % 4], AX, ALU.add)
            link(ins)
            link(TT(modc, modc, V("bl", 0, 32), ALU.add))
            for m, (plus, gi) in enumerate(((0.0, 0), (0.0, None), (1.0, 1), (0.0, 2))):
                if gi is not None:
                    ins = STT(V("modc", 8 * m, 8), V("modc", 8 * m, 8), plus, V("gl", 8 * gi, 8), ALU.add, ALU.mult)
            ins.then_inc(modc_ready, 1)

            dve.wait_ge(av_all, NH)
            eyeb = K("eye").rearrange("p (o t) -> p o t", o=1).broadcast_to((P, FT * NCH, C))
            CP(P3(s_X), eyeb)
            link(CP(P3(s_XT), eyeb))

            def mk(name, k=0):
                return K(name)[:, 64 * k:64 * k + 64].rearrange("p (o t) -> p o t", o=1).broadcast_to((P, NCH, C))

            for f in range(FT):
                BA = psf[:, 0:1024].rearrange("p (c a t) -> p c a t", c=NCH, a=2)
                KA = psf[:, 3072:4096].rearrange("p (c a t) -> p c a t", c=NCH, a=2)
                MM = ps[:, 4 + f % 2, :].rearrange("p (c t) -> p c t", c=NCH)
                dve.wait_ge(gram_done, 3 * f + 1)
                TT(chk[s_MT][:, f], BA[:, :, 0, :], mk("strictU"), ALU.mult)
                nc.vector.copy_predicated(chk[s_XT][:, f], mk("lvlU").bitcast(I32), BA[:, :, 0, :])
                dve.wait_ge(gram_done, 3 * f + 2)
                TT(chk[s_Mrb][:, f], BA[:, :, 1, :], mk("inclU"), ALU.mult).then_inc(gram_evac, 1)
                nc.vector.copy_predicated(chk[s_X][:, f], mk("lvlL").bitcast(I32), MM).then_inc(gram_evac, 1)
                dve.wait_ge(gram_done, 3 * f + 3)
                TT(chk[s_Mak][:, f], KA[:, :, 0, :], mk("strictU"), ALU.mult)
                TT(chk[s_Mrk][:, f], KA[:, :, 1, :], mk("inclU"), ALU.mult).then_inc(gram_evac, 1)
            for k in range(1, 6):
                for f in range(FT):
                    n = FT * (k - 1) + f
                    dve.wait_ge(invx_done, n + 1)
                    X_new = ps[:, 4 + f % 2, :].rearrange("p (c t) -> p c t", c=NCH)
                    if k < 5:
                        nc.vector.copy_predicated(chk[s_X][:, f], mk("lvlL", k).bitcast(I32), X_new).then_inc(invx_evac, 1)
                    else:
                        nc.vector.copy_predicated(chk[s_XT][:, f], mk("lvlU", k).bitcast(I32), X_new).then_inc(invx_evac, 1)
            PCv = PC[:, :].rearrange("p (f c) -> p f c", c=NCH)
            f4 = lambda a: a.rearrange("p (f v) -> p f v", f=FT)
            for cc in range(NCH):
                if cc == 0:
                    dve.wait_ge(hp_evac, 4)
                    CP(Zs[:, :], tok[s_H][:, 0, :, :].rearrange("p f v -> p (f v)")).then_inc(zc_evac, 1)
                else:
                    dve.wait_ge(zc_done, cc)
                    dve.wait_ge(sa_done, cc)
                    TT(Zs[:, :], ps[:, 4, 0:256], tok[s_H][:, cc, :, :].rearrange("p f v -> p (f v)"), ALU.add).then_inc(zc_evac, 1)
                if cc < NCH - 1:
                    if cc == 0:
                        dve.wait_ge(st_done, 1)
                        CP(ST[:, 1, :], ps[:, 6, 0:256]).then_inc(st_evac, 1)
                    else:
                        dve.wait_ge(st_evac, cc)
                        pc1 = PCv[:, :, cc:cc + 1].broadcast_to((P, FT, HD))
                        link(TT(f4(SD[:, :]), f4(ST[:, cc % 2, :]), pc1, ALU.mult))
                        dve.wait_ge(st_done, cc + 1)
                        dve.wait_ge(yc_done, cc)
                        TT(ST[:, (cc + 1) % 2, :], SD[:, :], ps[:, 6, 0:256], ALU.add).then_inc(st_evac, 1)
            for f in range(FT):
                dve.wait_ge(gn_sum, f + 1)
                STT(S4(s_y)[:, f, :], ps[:, f, :], -1.0 / HD, S4(s_y)[:, f, :], ALU.mult, ALU.add).then_inc(yrw_mean, 1)
            for f in range(FT):
                dve.wait_ge(gn_rstd, f + 1)
                y = S4(s_y)[:, f, :]
                link(TT(y, y, S4(s_y2)[:, f, :], ALU.mult))
                link(STT(y, y, V("lnw", f), S4(s_bonus)[:, f, :], ALU.mult, ALU.add))
                ins = STT(y, y, V("lnb", f), S4(s_g)[:, f, :], ALU.add, ALU.mult)
            ins.then_inc(yrw_ready, 1)
            dve.wait_ge(yrw_ready, 1)
            dve.wait_ge(sb_gated, KD)
            dve.wait_ge(gr_evac, KD)
            for n in range(KD):
                dve.wait_ge(mix_done, 3 * KD + n + 1)
                link(TT(gated[:, n % 2, :], gates_rw[:, n, :], ps[:, n % 4, :], ALU.mult))
                TT(merged[:, n, :], merged[:, n, :], gated[:, n % 2, :], ALU.add).then_inc(merged_ready, 1)
            dve.wait_ge(lrow_ready, 8)
            dve.wait_ge(x_again, 16)
            for t in range(NT):
                dve.wait_ge(rstd1, t + 1)
                y = ytok[:, 1, :]
                bk = 2 * (t % 2)
                link(STT(y, psf[:, 512 * bk:512 * bk + D], V("rs", 4 + t), rows[:, 0, :], ALU.mult, ALU.mult))
                TT(x1[:, t, :], x1[:, t, :], y, ALU.add).then_inc(x1_ready, 1)
                dve.wait_ge(rstd2, t + 1)
                if t >= 2:
                    dve.wait_ge(h2_stored[t % 2], 16)
                    dve.wait_ge(h2T_done, t - 1)
                hh = h2tok[:, t % 2, :]
                link(STT(hh, x1[:, t, :], V("rs", 8 + t), rows[:, 2, :], ALU.mult, ALU.mult))
                TT(hh, hh, rows[:, 1, :], ALU.add).then_inc(h2_ready, 1)
            R = rview
            gl, el = R(0, 16, 4), R(16, 128, 4)
            dve.wait_ge(logit_done, NT)
            lg = ps[:, 6, 0:4 * 64].rearrange("p (t n) -> p t n", t=NT)
            CP(gl, lg[:, :, 0:NG])
            link(CP(el, lg[:, :, NG:NG + E]))
            gmax = rt[:, 40:44].rearrange("p (t o) -> p t o", o=1)
            bc = lambda a, n: a.broadcast_to((P, NT, n))
            io = K("iota64").rearrange("p (o n) -> p o n", o=1)
            o1 = lambda a: a.rearrange("p (t o) -> p t o", o=1)
            link(nc.vector.tensor_reduce(gmax, gl, AX, ALU.max))
            link(TT(rt[:, 0:16].rearrange("p (t n) -> p t n", t=NT), gl, bc(gmax, NG), ALU.subtract))

            def first_max(vals, n, mx, oh, tmp, idx):
                link(TT(tmp, vals, bc(mx, n), ALU.is_lt))
                link(STT(tmp, tmp, 64.0, io[:, :, 0:n].broadcast_to((P, NT, n)), ALU.mult, ALU.add))
                link(nc.vector.tensor_reduce(idx, tmp, AX, ALU.min))
                link(TT(oh, io[:, :, 0:n].broadcast_to((P, NT, n)), bc(idx, n), ALU.is_equal))

            ohg, tmg = R(144, 16, 4), R(160, 16, 4)
            i_g, m1, m2, i1, i2 = (o1(rt[:, a:a + 4]) for a in (44, 48, 52, 56, 60))
            first_max(gl, NG, gmax, ohg, tmg, i_g)
            ml, tme, oh1, oh2, oh = (R(a, 128, 4) for a in (176, 304, 432, 560, 688))
            g8 = lambda a: a.rearrange("p t (g e) -> p (t g) e", e=EG)
            og = R(144, 16, 16)
            link(TT(g8(ml), g8(el), og.broadcast_to((P, 16, EG)), ALU.mult))
            link(TS(R(144, 16, 4), ohg, 1.0, BIG, ALU.subtract, ALU.mult))
            link(TT(g8(ml), g8(ml), og.broadcast_to((P, 16, EG)), ALU.add))
            link(nc.vector.tensor_reduce(m1, ml, AX, ALU.max))
            first_max(ml, E, m1, oh1, tme, i1)
            link(STT(ml, oh1, -2 * BIG, ml, ALU.mult, ALU.add))
            link(nc.vector.tensor_reduce(m2, ml, AX, ALU.max))
            first_max(ml, E, m2, oh2, tme, i2)
            link(TT(o1(rt[:, 32:36]), m2, m1, ALU.subtract))
            TT(oh, oh1, oh2, ALU.add).then_inc(oh_ready, 1)
            dve.wait_ge(gsum_ready, 1)
            gs = o1(rt[:, 64:68])
            link(nc.vector.tensor_reduce(gs, rt[:, 16:32].rearrange("p (t n) -> p t n", t=NT), AX, ALU.add))
            link(STT(rt[:, 68:72], rt[:, 36:40], 1.0, rt[:, 64:68], ALU.add, ALU.mult))
            link(nc.vector.reciprocal(routf[:, 0:4], rt[:, 68:72]))
            link(TT(routf[:, 4:8], routf[:, 0:4], rt[:, 36:40], ALU.mult))
            dve.wait_ge(rank_done, 1)
            rk_all = R(816, 128, 4)
            link(CP(rk_all, ps[:, 1, 0:128].rearrange("p (t e) -> p t e", t=NT)))
            cnt, nov, ends, base = rt[:, 72:104], rt[:, 104:136], rt[:, 136:168], rt[:, 168:200]
            link(CP(cnt, ps[:, 1, NT * E:NT * E + E]))
            cmp7 = R(944, 7 * E, 7)
            link(TT(cmp7, cnt.rearrange("p (o e) -> p o e", o=1).broadcast_to((P, 7, E)),
                    K("m64")[:, 1:8].rearrange("p (m o) -> p m o", o=1).broadcast_to((P, 7, E)), ALU.is_gt))
            link(nc.vector.tensor_reduce(nov.rearrange("p (e o) -> p e o", o=1), cmp7.rearrange("p m e -> p e m"), AX, ALU.add))
            link(nc.vector.tensor_tensor_scan(ends, K("ones")[:, 0:E], nov, float(E), ALU.mult, ALU.add))
            link(TT(base, ends, nov, ALU.subtract))
            N2 = 2 * NT
            oh12, tm12, i12 = R(432, 256, N2), R(1680, 256, N2), rt[:, 56:64]
            rk_, bs_, q_, blk_, rr = (rt[:, 200 + N2 * a:200 + N2 * a + N2] for a in range(5))
            by_choice = lambda a: a.rearrange("p (c t) e -> p c (t e)", c=2)
            link(TT(by_choice(tm12), rk_all.rearrange("p t e -> p (t e)").rearrange("p (o n) -> p o n", o=1).broadcast_to((P, 2, NT * E)),
                    by_choice(oh12), ALU.mult))
            link(nc.vector.tensor_reduce(o1(rk_), tm12, AX, ALU.add))
            link(TT(tm12, oh12, base.rearrange("p (o e) -> p o e", o=1).broadcast_to((P, N2, E)), ALU.mult))
            link(nc.vector.tensor_reduce(o1(bs_), tm12, AX, ALU.add))
            c7 = R(944, 7 * N2, N2)
            link(TT(c7, o1(rk_).broadcast_to((P, N2, 7)),
                    K("m64")[:, 1:8].rearrange("p (o m) -> p o m", o=1).broadcast_to((P, N2, 7)), ALU.is_ge))
            link(nc.vector.tensor_reduce(o1(q_), c7, AX, ALU.add))
            link(STT(blk_, bs_, -1.0, q_, ALU.add, ALU.add))
            link(TT(blk_, blk_, i12, ALU.subtract))
            link(STT(blk_, q_, 0.0, blk_, ALU.is_gt, ALU.mult))
            TT(blk_, blk_, i12, ALU.add)
            link(STT(rr, q_, -float(CAP), rk_, ALU.mult, ALU.add))
            TT(R(1168, 512, N2), io[:, :, 0:CAP].broadcast_to((P, N2, CAP)), o1(rr).broadcast_to((P, N2, CAP)), ALU.is_equal)
            ohb = selb.rearrange("p c t b -> p (c t) b")
            link(TT(ohb, io[:, :, 0:MAXB].broadcast_to((P, N2, MAXB)), o1(blk_).broadcast_to((P, N2, MAXB)), ALU.is_equal))
            TT(selb, selb, K("tok").rearrange("p (c t o) -> p c t o", c=1, o=1).broadcast_to((P, 2, NT, MAXB)),
               ALU.mult).then_inc(sel_ready, 1)
            two = lambda a: a.rearrange("p (c t) -> p c t", c=2)
            link(STT(routf[:, 8:16].rearrange("p (t c) -> p c t", c=2), two(blk_), float(CAP), two(rr), ALU.mult, ALU.add))
            link(CP(slots_i[:, :], routf[:, 8:16]))
            ov = ovb
            b16 = K("blk16")[0:1, :].rearrange("p (m o) -> p m o", o=1).broadcast_to((1, 16, E))
            link(TT(ov[0:1], ends[0:1].rearrange("p (o e) -> p o e", o=1).broadcast_to((1, 16, E)), b16, ALU.is_le))
            link(nc.vector.tensor_reduce(rt[0:1, 260:276].rearrange("p (m o) -> p m o", o=1), ov[0:1], AX, ALU.add))
            link(TS(rt[0:1, 260:276], rt[0:1, 260:276], float(E - 1), None, ALU.min))
            link(CP(nblk_i[0:1, 2:18], rt[0:1, 260:276]))
            lt8 = rt[0:1, 276:284]
            link(TT(lt8, K("blk16")[0:1, 0:16:2], ends[0:1, E - 1:E].broadcast_to((1, 8)), ALU.is_lt))
            link(nc.vector.tensor_reduce(rt[0:1, 284:285], lt8, AX, ALU.add))
            link(CP(nblk_i[0:1, 1:2], rt[0:1, 284:285]))
            link(TS(nblk_i[0:1, 0:1], rt[0:1, 284:285], float(E // 2), None, ALU.add))
            dve.wait_ge(idx_done, 1)
            link(CP(idx_i[:, :], ps[0:CAP, 3, 0:MAXB]))
            nc.vector.engine_nop().then_inc(route_ready, 1)
            dve.wait_ge(route_ready, 1)
            steps = dve.value_load(nblk_i[0:1, 0:1], min_val=E // 2, max_val=MAXB // 2)
            with dve.Fori(0, steps) as it:
                for u in range(2):
                    dve.wait_ge(hg_done[u], it + 2)
                    CP(hgT[:, u, :, :].rearrange("p k s -> p (k s)"), ps[:, 0, :]).then_inc(hg_ready[u], 1)
                    dve.wait_ge(sil_ready[u], it + 1)
                    TT(hid[:, u, :], sil[:, u, :], ps[:, 2 + u, 256:512], ALU.mult).then_inc(hid_ready[u], 1)
                    dve.wait_ge(ht_done[u], it + 1)
                    CP(hidT[:, u, :], ps[:, 1, 0:256]).then_inc(ht_ready[u], 1)
            def combine(t):
                b = fin[t]
                dve.wait_ge(fin_first, t + 1)
                STT(b[:, 2, :], b[:, 1, :], routf[:, 4 + t:5 + t], b[:, 2, :], ALU.mult, ALU.add).then_inc(fin_ss, 1)

            combine(0)
            for t in range(NT):
                if t < NT - 1:
                    combine(t + 1)
                b = fin[t]
                dve.wait_ge(fin_rstd, t + 1)
                link(STT(b[:, 2, :], b[:, 2, :], V("rs", 12 + t), rows[:, 3, :], ALU.mult, ALU.mult))
                TT(b[:, 2, :], b[:, 2, :], x1[:, t, :], ALU.add).then_inc(fin_ready, 1)

        @block.tensor
        def _(pe):
            mm, tr = nc.tensor.matmul, nc.tensor.transpose
            ident = K("ident")
            pe.wait_ge(consts_in, 16)
            pe.wait_ge(rows_in, 16 * 12)
            tr(ps[:, 6, 0:NROW], prow[:, :], ident[0:NROW, 0:NROW]).then_inc(rows_turned, 1)
            def x_transpose_tile(k):
                for t in range(NT):
                    src = xn[:, t, :].rearrange("p (q k) -> p k q", k=KD)[:, k, :]
                    last = tr(ps[:, k % 7, P * t:P * t + P], src, ident)
                last.then_inc(xT_done, 1)

            def mod_columns(m):
                pe.wait_ge(acc_ready, m + 1)
                a = acc_e[:, m, :].rearrange("p (q k) -> p k q", k=KD)
                for k in range(KD):
                    last = mm(ps[:, 7, 8 * m + k:8 * m + k + 1], a[:, k, :], K("ones")[:, 0:1], start=True, stop=True)
                return last

            mod_columns(0)
            pe.wait_ge(xn_ready, NT)
            pe.wait_ge(par_ready, 1)
            for k in range(7):
                x_transpose_tile(k)
            mod_columns(1).then_inc(modcol_done, 1)
            pe.wait_ge(xT_even, 1)
            x_transpose_tile(7)
            pe.wait_ge(xT_even, KD // 2)
            pe.wait_ge(xT_odd, KD // 2)

            g = 0

            def group():
                nonlocal g
                if g >= 6:
                    pe.wait_ge(pa_evac, g - 5)
                g += 1
                return (g - 1) % 6

            def project(name, tiles):
                w = chunk(name, KD)
                arrived(pe, name)
                for i, (a, m_) in enumerate(tiles):
                    b = group()
                    for k in range(KD):
                        last = mm(ps[0:m_, b, :], w[:, k, a:a + m_], hT[:, k, :], start=(k == 0), stop=(k == KD - 1))
                    last.then_inc(pa_done, 1)

            full = [(P * f, P) for f in range(FT)]
            for n, (_, _, m_) in enumerate(proj_tiles):
                b = group()
                pe.wait_ge(w_split, n + 1)
                for k in range(KD):
                    if n == 0:
                        pe.wait_ge(h_rounded, k + 1)
                        pe.wait_ge(h_split[k % 2], k // 2 + 1)
                    hi, lo = w_parts[:, n % 2, 0, k, 0:m_], w_parts[:, n % 2, 1, k, 0:m_]
                    mm(ps[0:m_, b, :], hi, h_hi[:, k, :], start=(k == 0), stop=False)
                    mm(ps[0:m_, b, :], hi, h_lo[:, k, :], start=False, stop=False)
                    last = mm(ps[0:m_, b, :], lo, h_hi[:, k, :], start=False, stop=(k == KD - 1))
                last.then_inc(pa_done, 1)
            pe.wait_ge(lora_in, 16 * 6)
            pe.wait_ge(lora_act, 1)
            pe.wait_ge(shifted, 3)
            for f in range(FT):
                mm(ps[:, group(), :], wlo[0:64, 0, P * f:P * f + P], lora[0:64, 0, :], start=True, stop=True).then_inc(pa_done, 1)
            for f in range(FT):
                mm(ps[:, group(), :], wlo[64:128, 0, P * f:P * f + P], lora[64:128, 0, :], start=True, stop=True).then_inc(pa_done, 1)
            for f in range(FT):
                b = group()
                mm(ps[:, b, :], wlo[:, 1, P * f:P * f + P], lora[:, 1, :], start=True, stop=False)
                mm(ps[:, b, :], wlo[0:32, 2, P * f:P * f + P], lora[0:32, 2, :], start=False, stop=True).then_inc(pa_done, 1)
            pe.wait_ge(kk2_ready, 1)
            for f in range(FT):
                if f >= 2:
                    pe.wait_ge(kk_max, f - 1)
                mm(ps[:, 6 + f % 2, :], K("blk"), S4(s_kk2)[:, f, :], start=True, stop=True).then_inc(pd_done, 1)
            project("AQ", full)
            project("AK", full)
            pe.wait_ge(bonus_in, 1)
            for f in range(FT):
                if f >= 2:
                    pe.wait_ge(bonus_ready, f - 1)
                mm(ps[:, 6 + f % 2, :], K("blk"), S4(s_bonus)[:, f, :], start=True, stop=True).then_inc(pd_done, 1)
            arrived(pe, "AV")
            w = chunk("AV", KD)
            for t in range(NT):
                b = group()
                for k in range(KD):
                    last = mm(ps[:, b, :], hT[:, k, P * t:P * t + P], w[:, k, :], start=(k == 0), stop=(k == KD - 1))
                last.then_inc(pa_done, 1)
            pe.wait_ge(pa_evac, g)
            pe.wait_ge(tok_src, 1)
            pe.wait_ge(bonus_ready, FT)
            for n in range(3 * NCH):
                if n >= 6:
                    s = tr_act if n % 2 == 0 else tr_dve
                    pe.wait_ge(s, (n - 6) // 2 + 1)
                src = (s_v, s_Bh, s_Kh)[n // NCH]
                cc = n % NCH
                for f in range(FT):
                    last = tr(ps[0:64, n % 6, P * f:P * f + P], S4(src)[:, f, C * cc:C * cc + C], ident)
                last.then_inc(tr_done, 1)
            pe.wait_ge(tr_act, 12)
            pe.wait_ge(tr_dve, 12)

            def scores(h):
                f, a = h // 2, HD * (h % 2)
                if h >= 2:
                    pe.wait_ge(att_ready, h - 1)
                for j in (0, 1, 3, 2):
                    o = 1536 * (h % 2) + OFF[j]
                    last = mm(psf[:, o:o + WID[j]], S4(s_ka)[a:a + HD, f, P * j:P * j + P],
                              S4(s_q)[a:a + HD, f, P * j:T], start=(j != 3), stop=True, skip_group_check=True)
                last.then_inc(z_done, 1)

            def sums(h):
                pe.wait_ge(sp_split, h + 1)
                for j in range(NT):
                    for jj in range(j, NT):
                        o = 1536 * (h % 2) + OFF[j] + P * (jj - j)
                        for sp in (sp_hi, sp_lo):
                            last = mm(psf[:, o:o + WID[jj]], tri_r[:, 0 if jj == j else 1, :],
                                      sp[:, OFF[jj]:OFF[jj] + WID[jj]], start=False, stop=True, skip_group_check=True)
                last.then_inc(cum_done, 1)

            def values(h):
                f, a = h // 2, HD * (h % 2)
                if h % 2 == 0 and f >= 1:
                    pe.wait_ge(ysb_ready, f)
                pe.wait_ge(att_masked, h + 1)
                for j in range(NT):
                    last = mm(ps[a:a + HD, 6, P * j:T], S4(s_va)[:, j, HD * h:HD * h + HD],
                              e_buf[h % 2][:, OFF[j]:OFF[j] + WID[j]], start=(j == 0), stop=(j == NT - 1),
                              skip_group_check=True)
                last.then_inc(av_all, 1)

            def gate(branch, n, ks, bank):
                if ks[0] == 0:
                    arrived(pe, f"{branch}{n // 2}")
                    if branch == "GS" and n:
                        pe.wait_ge(gs_evac, n)
                    if branch == "GR" and n >= 2:
                        pe.wait_ge(gr_evac, n - 1)
                w = chunk(f"{branch}{n // 2}", KD)
                for k in ks:
                    last = mm(ps[:, bank, :], w[:, k, P * (n % 2):P * (n % 2) + P], hT[:, k, :], start=(k == 0), stop=(k == KD - 1))
                if ks[-1] == KD - 1:
                    last.then_inc(mix_done, 1)

            def attention_output(n, ks):
                if ks[0] == 0:
                    arrived(pe, "OSB")
                    if n >= 2:
                        pe.wait_ge(osb_evac, n - 1)
                for k in ks:
                    last = mm(ps[:, 2 + n % 2, :], chunk("OSB", 4)[:, k, P * n:P * n + P], S4(s_q)[:, k, :], start=(k == 0),
                              stop=(k == FT - 1))
                if ks[-1] == FT - 1:
                    last.then_inc(mix_done, 1)

            scores(0)
            pe.wait_ge(tri_ready, 1)
            for h in range(NH):
                if h + 1 < NH:
                    scores(h + 1)
                first = FILL_ATT
                gate("GS", h, range(first), 7)
                sums(h)
                gate("GS", h, range(first, KD), 7)
                values(h)
            pe.wait_ge(lacc_ready, NH)
            def late_sum(j):
                if j >= 4:
                    earlier = max(i for i in range(j) if LATE_BANK[i] == LATE_BANK[j])
                    pe.wait_ge(lcol_evac, earlier + 1)
                mm(ps[:, LATE_BANK[j], :], K("ones"), acc_l[j], start=True, stop=True).then_inc(lcol_done, 1)

            for j in range(6):
                late_sum(j)
            pe.wait_ge(ysb_ready, FT)

            for f in range(FT):
                def products(src, o):
                    for cc in range(NCH):
                        for a in (0, HD):
                            last = mm(psf[a:a + HD, o + P * cc:o + P * cc + P], chk[src][a:a + HD, f, cc, :],
                                      AR[a:a + HD, f, cc, :, :].rearrange("p a t -> p (a t)"), start=True, stop=True,
                                      skip_group_check=True)
                    last.then_inc(gram_done, 1)

                if f >= 1:
                    if f == 1:
                        pe.wait_ge(lcol_evac, NH)
                    if f in GRAM_FILL:
                        attention_output(GRAM_FILL.index(f), range(FT))
                    pe.wait_ge(gram_evac, 3 * f - 1)
                products(s_B, 0)
                if f == 0:
                    late_sum(6)
                    late_sum(7)
                for cc in range(NCH):
                    for a in (0, HD):
                        last = mm(ps[a:a + HD, 4 + f % 2, C * cc:C * cc + C], AR[a:a + HD, f, cc, 0, :],
                                  chk[s_B][a:a + HD, f, cc, :], start=True, stop=True, skip_group_check=True)
                last.then_inc(gram_done, 1)
                if f >= 1:
                    pe.wait_ge(gram_evac, 3 * f)
                products(s_Kd, 3072)
            pe.wait_ge(gram_evac, 3 * FT)

            for n in range(len(GRAM_FILL), 3):
                attention_output(n, range(FT))

            def tiles64(bank, lhs, rhs, f, sig):
                for cc in range(NCH):
                    for a in (0, HD):
                        last = mm(ps[a:a + HD, bank, C * cc:C * cc + C], chk[lhs][a:a + HD, f, cc, :],
                                  chk[rhs][a:a + HD, f, cc, :], start=True, stop=True, skip_group_check=True)
                last.then_inc(sig, 1)

            def w_product(k, f):
                n = FT * (k - 1) + f
                if k > 1:
                    pe.wait_ge(invx_evac, n - FT + 1)
                if n >= 2:
                    pe.wait_ge(invw_evac, n - 1)
                tiles64(f % 2, s_MT, s_X, f, invw_done)
                attention_output(k + 2, (f,))

            def x_product(k, f):
                n = FT * (k - 1) + f
                pe.wait_ge(invw_evac, n + 1)
                if k > 1:
                    pe.wait_ge(invt_evac, n - FT + 1)
                if n >= 2:
                    pe.wait_ge(invx_evac, n - 1)
                if k < 5:
                    tiles64(4 + f % 2, s_XT, s_W, f, invx_done)
                else:
                    tiles64(4 + f % 2, s_W, s_XT, f, invx_done)

            def x_transpose(k, f):
                n = FT * (k - 1) + f
                pe.wait_ge(invx_evac, n + 1)
                if n >= 1:
                    pe.wait_ge(invt_evac, n)
                for cc in range(NCH):
                    last = tr(psf[0:64, 6 * 512 + P * cc:6 * 512 + P * cc + P], chk[s_X][:, f, cc, :], ident)
                last.then_inc(invt_done, 1)

            for k in range(1, 6):
                w_product(k, 0)
                if k > 1:
                    x_transpose(k - 1, 3)
                w_product(k, 1)
                x_product(k, 0)
                w_product(k, 2)
                x_product(k, 1)
                if k < 5:
                    x_transpose(k, 0)
                w_product(k, 3)
                x_product(k, 2)
                if k < 5:
                    x_transpose(k, 1)
                x_product(k, 3)
                if k < 5:
                    x_transpose(k, 2)
            pe.wait_ge(invx_evac, 5 * FT)
            pe.wait_ge(osb_evac, KD)
            for b in range(4):
                for cc in (2 * b, 2 * b + 1):
                    for f in range(FT):
                        for a in (0, HD):
                            o = 256 * (cc % 2) + HD * f
                            last = mm(ps[a:a + HD, HP_BANK[b], o:o + HD], chk[s_Mak][a:a + HD, f, cc, :],
                                      tok[s_Vt][a:a + HD, cc, f, :], start=True, stop=True, skip_group_check=True)
                last.then_inc(hp_done, 1)
            fa = [(f, a) for f in range(FT) for a in (0, HD)]
            for cc in range(NCH):
                cur = ST[:, cc % 2, :]
                gate("GR", cc, (0, 1), 2 + cc % 2)
                if cc:
                    pe.wait_ge(st_evac, cc)
                    for f, a in fa:
                        last = mm(ps[a:a + HD, 4, HD * f:HD * f + HD], AR[a:a + HD, f, cc, 0, :],
                                  cur[a:a + HD, HD * f:HD * f + HD], start=True, stop=True, skip_group_check=True)
                    last.then_inc(zc_done, 1)
                gate("GR", cc, (2, 3, 4), 2 + cc % 2)
                pe.wait_ge(zc_evac, cc + 1)
                for f, a in fa:
                    last = mm(ps[a:a + HD, 5, HD * f:HD * f + HD], chk[s_XT][a:a + HD, f, cc, :],
                              Zs[a:a + HD, HD * f:HD * f + HD], start=True, stop=True, skip_group_check=True)
                last.then_inc(sa_done, 1)
                gate("GR", cc, (5, 6, 7), 2 + cc % 2)
                pe.wait_ge(sa_evac, cc + 1)
                sa = SAs[:, cc % 2, :]
                if cc < NCH - 1:
                    for f, a in fa:
                        mm(ps[a:a + HD, 6, HD * f:HD * f + HD], tok[s_Bt][a:a + HD, cc, f, :],
                           sa[a:a + HD, HD * f:HD * f + HD], start=True, stop=False, skip_group_check=True)
                        last = mm(ps[a:a + HD, 6, HD * f:HD * f + HD], tok[s_Kt][a:a + HD, cc, f, :],
                                  tok[s_Vt][a:a + HD, cc, f, :], start=False, stop=True, skip_group_check=True)
                    last.then_inc(st_done, 1)
                yb = 7 if cc % 2 else 0
                if cc >= 2:
                    pe.wait_ge(yc_evac, cc - 1)
                if cc == 0:
                    pe.wait_ge(hp_evac, 4)
                for f, a in fa:
                    o = ps[a:a + HD, yb, HD * f:HD * f + HD]
                    if cc:
                        mm(o, cur[a:a + HD, HD * f:HD * f + HD], AR[a:a + HD, f, cc, 1, :], start=True, stop=False, skip_group_check=True)
                    mm(o, sa[a:a + HD, HD * f:HD * f + HD], chk[s_Mrb][a:a + HD, f, cc, :], start=(cc == 0), stop=False, skip_group_check=True)
                    last = mm(o, tok[s_Vt][a:a + HD, cc, f, :], chk[s_Mrk][a:a + HD, f, cc, :], start=False, stop=True, skip_group_check=True)
                last.then_inc(yc_done, 1)
            pe.wait_ge(yc_evac, NCH)
            pe.wait_ge(gr_evac, KD)
            for f in range(FT):
                mm(ps[:, f, :], K("blk"), S4(s_y)[:, f, :], start=True, stop=True).then_inc(gn_sum, 1)
            pe.wait_ge(st_evac, NCH - 1)
            pe.wait_ge(zc_evac, NCH)
            for f in range(FT):
                pe.wait_ge(gn_sq, f + 1)
                mm(ps[:, 4 + f, :], K("blk"), S4(s_y2)[:, f, :], start=True, stop=True).then_inc(gn_sqsum, 1)

            pe.wait_ge(yrw_mean, FT)
            for n in range(8):
                pe.wait_ge(diag_ready, n + 1)
                if n >= 4:
                    pe.wait_ge(lrow_ready, n - 3)
                mm(ps[:, n % 4, :], K("ones"), DG[n % 3].rearrange("p q n -> p (q n)"), start=True, stop=True).then_inc(lrow_done, 1)

            pe.wait_ge(yrw_ready, 1)
            pe.wait_ge(orw_in, 32)
            for f in range(KD):
                if f >= 4:
                    pe.wait_ge(merged_ready, f - 3)
                else:
                    pe.wait_ge(lrow_ready, f + 5)
                for k in range(FT):
                    last = mm(ps[:, f % 4, :], orw[k // 2][:, k % 2, P * f:P * f + P], S4(s_y)[:, k, :], start=(k == 0), stop=(k == FT - 1))
                last.then_inc(mix_done, 1)

            def transposes_h2(t):
                pe.wait_ge(h2_ready, t + 1)
                if t:
                    pe.wait_ge(h2T_evac, t)
                for k in range(KD):
                    src = h2tok[:, t % 2, :].rearrange("p (q k) -> p k q", k=KD)[:, k, :]
                    last = tr(psf[:, 2048 + P * k:2048 + P * k + P], src, ident)
                last.then_inc(h2T_done, 1)

            def router_logits(t):
                pe.wait_ge(h2T_evac, t + 1)
                for k in range(KD):
                    last = mm(ps[:, 6, 64 * t:64 * t + NG + E], hT[:, k, P * t:P * t + P], wr[:, k, :], start=(k == 0),
                              stop=(k == KD - 1), skip_group_check=True)
                last.then_inc(logit_done, 1)

            pe.wait_ge(merged_ready, KD)
            arrived(pe, "WO0")
            arrived(pe, "WO1")
            for t in range(NT):
                bk = 2 * (t % 2)
                if t >= 2:
                    pe.wait_ge(x1_ready, t - 1)
                for hf in range(2):
                    w = chunk(f"WO{hf}", KD)
                    for k in range(KD):
                        if hf == 1 and k == 7 and t >= 1:
                            transposes_h2(t - 1)
                        last = mm(ps[:, bk + hf, :], merged[:, k, P * t:P * t + P], w[:, k, :], start=(k == 0), stop=(k == KD - 1))
                last.then_inc(y_done, 1)
                if 1 <= t < NT - 1:
                    router_logits(t - 1)
            router_logits(NT - 2)
            transposes_h2(NT - 1)
            router_logits(NT - 1)
            pe.wait_ge(oh_ready, 1)
            oh = rview(688, 128, 4)
            mm(ps[:, 1, 0:NT * E], K("before"), oh[:, :, :], start=True, stop=False, skip_group_check=True)
            for q in range(NT):
                last = mm(ps[:, 1, E * (q + 1):E * (NT + 1)].rearrange("p (t e) -> p t e", e=E), K("ones"),
                          oh[:, q:q + 1, :].broadcast_to((P, NT - q, E)), start=False, stop=(q == NT - 1), skip_group_check=True)
            last.then_inc(rank_done, 1)
            pe.wait_ge(sel_ready, 1)
            for ch in range(2):
                ohr = rview(1168 + 256 * ch, 256, 4)
                for t in range(NT):
                    last = mm(ps[0:CAP, 3, 0:MAXB], ohr[:, t, :], selb[:, ch, t, :], start=(ch == 0 and t == 0),
                              stop=(ch == 1 and t == NT - 1))
            last.then_inc(idx_done, 1)
            pe.wait_ge(route_ready, 1)
            steps = pe.value_load(nblk_i[0:1, 0:1], min_val=E // 2, max_val=MAXB // 2)
            for u in range(2):
                pe.sem_inc(hg_done[u], 1)
                pe.sem_inc(yo_ready[u], 1)
            with pe.Fori(0, steps) as it:
                for u in range(2):
                    pe.wait_ge(hrow_in[u], it * 16 + 16)
                    pe.sem_inc(register_pass, 1)
                    hv = hrow[0:CAP, u, :].rearrange("p (q k) -> p k q", k=KD)
                    for k in range(KD):
                        last = tr(ps[:, 0, CAP * k:CAP * k + CAP], hv[:, k, :], ident[0:CAP, 0:CAP])
                    last.then_inc(hg_done[u], 1)
                    pe.wait_ge(hg_ready[u], it + 1)
                    pe.wait_ge(w_in_sem[u][0], it * 16 + 16)
                    pe.wait_ge(w_in_sem[u][1], it * 16 + 16)
                    for k in range(KD):
                        for hf in range(2):
                            w2 = eset_up[u].rearrange("p m (k n) -> p m k n", k=KD)
                            last = mm(ps[64 * hf:64 * hf + 64, 2 + u, :].rearrange("p (m n) -> p m n", m=2), hgT[:, u, k, :],
                                      w2[:, :, k, 256 * hf:256 * hf + 256], start=(k == 0), stop=(k == KD - 1))
                    last.then_inc(up_done[u], 1)
                    pe.wait_ge(hid_ready[u], it + 1)
                    for j in range(2):
                        last = tr(ps[:, 1, P * j:P * j + P], hid[:, u, P * j:P * j + P], ident)
                    last.then_inc(ht_done[u], 1)
                    pe.wait_ge(ht_ready[u], it + 1)
                    pe.wait_ge(w_in_sem[u][2], it * 16 + 16)
                    pe.wait_ge(yo_ready[u], it + 1)
                    wd = eset_down[u].rearrange("p (k n) -> p k n", k=4)
                    hv2 = hidT[:, u, :].rearrange("p (j h s) -> p j h s", j=2, h=2)
                    for k in range(4):
                        for hf in range(2):
                            last = mm(ps[64 * hf:64 * hf + 64, 4 + u, :], hv2[:, k % 2, k // 2, :],
                                      wd[:, k, 512 * hf:512 * hf + 512], start=(k == 0), stop=(k == 3))
                    last.then_inc(down_done[u], 1)


_INS = ['x', 'c', 'w_mod', 'b_mod', 'norm_gains', 'w_in', 'gate_bias', 'shift_mu', 'w0', 'w_decay_up', 'a0',
        'w_iclr_up', 'w_gate_up', 'k_k', 'k_a', 'r_k', 'lnx_w', 'lnx_b', 'w_o_sb', 'w_o_rw', 'w_out',
        'w_group', 'w_router', 'w_up1', 'w_up3', 'w_down']


def kernel(**inputs):
    import concourse.bacc as bacc
    from concourse.bass_utils import run_bass_kernel_spmd

    nc = bacc.Bacc("TRN2", target_bir_lowering=False, num_devices=1)
    arrays, args = {}, []
    for name in _INS:
        a = np.ascontiguousarray(inputs[name])
        arrays[f"in_{name}"] = a
        args.append(nc.dram_tensor(f"in_{name}", a.shape, mybir.dt.from_np(a.dtype), kind="ExternalInput").ap())
    arrays["in_consts"] = constants()
    args.append(nc.dram_tensor("in_consts", (P, NCONST), F32, kind="ExternalInput").ap())
    args.append(nc.dram_tensor("out_0", (1, T, D), F32, kind="ExternalOutput").ap())
    build(nc, *args)
    r = run_bass_kernel_spmd(nc, [arrays], core_ids=[0])
    return r.results[0]["out_0"]
```
